# Optimizing a Trainium2 kernel written in Bass

```python
import jax, jax.numpy as jnp
from jax import lax
import numpy as np

D_MODEL = 1024
BATCH = 1
SEQ = 1024
DEPTH = 2
DEC_BATCH = 8
DEC_SEQ = 1
PAST_LEN = 256
PAGE_SIZE = 128

N_MIXERS = 2
N_A_LAYERS = (DEPTH + 1) // 2
N_B_LAYERS = DEPTH // 2

WINDOWS = (128, 512, 2048)
DILATIONS = (1, 4, 16)
N_GROUPS = 3
A_HEADS = 8
A_HEAD_DIM = 64
A_BLOCK = 128
R_HEADS = 4
R_QK_DIM = D_MODEL // R_HEADS
R_V_DIM = 2 * R_QK_DIM
R_CHUNK = 128
FFN_HIDDEN = ((8 * D_MODEL + 3 * 256 - 1) // (3 * 256)) * 256
ROPE_THETA = 10000.0
EPS = 1e-6

kernel_name = "dilated_window_retention_hybrid_step"

def rmsnorm(x, g):
    xf = x.astype(jnp.float32)
    y = xf * lax.rsqrt(jnp.mean(xf * xf, axis=-1, keepdims=True) + EPS)
    return (y * g.astype(jnp.float32)).astype(x.dtype)

def rope(x, pos):
    half = x.shape[-1] // 2
    inv = ROPE_THETA ** (-jnp.arange(half, dtype=jnp.float32) / half)
    ang = pos.astype(jnp.float32)[:, None] * inv[None, :]
    shp = (pos.shape[0],) + (1,) * (x.ndim - 3) + (half,)
    cos = jnp.cos(ang).reshape(shp)
    sin = jnp.sin(ang).reshape(shp)
    xf = x.astype(jnp.float32)
    x1, x2 = xf[..., :half], xf[..., half:]
    return jnp.concatenate([x1 * cos - x2 * sin, x2 * cos + x1 * sin], axis=-1).astype(x.dtype)

def swiglu(h, w_gate, w_up, w_down):
    return (jax.nn.silu(h @ w_gate) * (h @ w_up)) @ w_down

def a_project(h, pos, w_qkv, q_norm, k_norm):
    B, S, _ = h.shape
    p = (h @ w_qkv).reshape(B, S, N_GROUPS, 3, A_HEADS, A_HEAD_DIM)
    q = rmsnorm(p[:, :, :, 0], q_norm[:, None, :])
    k = rmsnorm(p[:, :, :, 1], k_norm[:, None, :])
    q = rope(q, pos) * (A_HEAD_DIM ** -0.5)
    k = rope(k, pos)
    return q, k, p[:, :, :, 2]

def dilated_band_attention(q, k, v, dil, n_rel):
    B, S, H, Dh = q.shape
    L = S // dil
    N = B * dil

    def to_sub(t):
        return t.reshape(B, L, dil, H, Dh).transpose(0, 2, 1, 3, 4).reshape(N, L, H, Dh)

    nb = -(-L // A_BLOCK)
    pad = nb * A_BLOCK - L
    qb = jnp.pad(to_sub(q), ((0, 0), (0, pad), (0, 0), (0, 0))).reshape(N, nb, A_BLOCK, H, Dh)

    def band(t):
        tb = jnp.pad(to_sub(t), ((0, 0), (A_BLOCK, pad), (0, 0), (0, 0))).reshape(N, nb + 1, A_BLOCK, H, Dh)
        return jnp.concatenate([tb[:, :-1], tb[:, 1:]], axis=2)

    kb, vb = band(k), band(v)
    s = jnp.einsum('nbqhd,nbkhd->nbhqk', qb, kb, preferred_element_type=jnp.float32)
    bi = jnp.arange(nb)[:, None, None]
    qi = jnp.arange(A_BLOCK)[None, :, None]
    kj = jnp.arange(2 * A_BLOCK)[None, None, :]
    dist = A_BLOCK + qi - kj
    kpos = bi * A_BLOCK + kj - A_BLOCK
    valid = (dist >= 0) & (dist <= n_rel) & (kpos >= 0)
    s = jnp.where(valid[:, None], s, -jnp.inf)
    m = jnp.max(s, axis=-1)
    p = jnp.exp(s - m[..., None])
    l = jnp.sum(p, axis=-1)
    acc = jnp.einsum('nbhqk,nbkhd->nbqhd', p, vb.astype(jnp.float32))

    def from_sub(t):
        t = t.reshape((N, nb * A_BLOCK) + t.shape[3:])[:, :L]
        tail = t.shape[2:]
        t = t.reshape((B, dil, L) + tail)
        return jnp.swapaxes(t, 1, 2).reshape((B, S) + tail)

    return from_sub(acc), from_sub(jnp.swapaxes(m, 2, 3)), from_sub(jnp.swapaxes(l, 2, 3))

def combine_groups(accs, ms, ls):
    m_all = jnp.stack(ms)
    w = jnp.exp(m_all - jnp.max(m_all, axis=0))
    num = jnp.einsum('gbshd,gbsh->bshd', jnp.stack(accs), w)
    den = jnp.sum(jnp.stack(ls) * w, axis=0)
    return num / den[..., None]

def mixer_a_prompt(h, w_qkv, q_norm, k_norm, w_o):
    B, S, _ = h.shape
    q, k, v = a_project(h, jnp.arange(S), w_qkv, q_norm, k_norm)
    accs, ms, ls, rows = [], [], [], []
    for g in range(N_GROUPS):
        acc, m, l = dilated_band_attention(q[:, :, g], k[:, :, g], v[:, :, g],
                                           DILATIONS[g], WINDOWS[g] // DILATIONS[g])
        accs.append(acc); ms.append(m); ls.append(l)
        keep = min(WINDOWS[g], S)
        rows.append(jnp.stack([k[:, :, g], v[:, :, g]], axis=2)[:, S - keep:])
    o = combine_groups(accs, ms, ls).astype(h.dtype).reshape(B, S, A_HEADS * A_HEAD_DIM)
    return o @ w_o, rows

def mixer_a_sample(h, bufs, w_qkv, q_norm, k_norm, w_o):
    B, T, _ = h.shape
    q, k, v = a_project(h, PAST_LEN + jnp.arange(T), w_qkv, q_norm, k_norm)
    accs, ms, ls, new_bufs = [], [], [], []
    for g in range(N_GROUPS):
        buf = bufs[g]
        Lg = buf.shape[1]
        cat = jnp.concatenate([buf, jnp.stack([k[:, :, g], v[:, :, g]], axis=2).astype(buf.dtype)], axis=1)
        n_rel = WINDOWS[g] // DILATIONS[g]
        ridx = Lg + jnp.arange(T)[:, None] - DILATIONS[g] * jnp.arange(n_rel + 1)[None, :]
        kv = jnp.take(cat, jnp.maximum(ridx, 0), axis=1)
        s = jnp.einsum('bthd,btjhd->bthj', q[:, :, g], kv[:, :, :, 0], preferred_element_type=jnp.float32)
        s = jnp.where((ridx >= 0)[None, :, None, :], s, -jnp.inf)
        m = jnp.max(s, axis=-1)
        p = jnp.exp(s - m[..., None])
        accs.append(jnp.einsum('bthj,btjhd->bthd', p, kv[:, :, :, 1].astype(jnp.float32)))
        ms.append(m); ls.append(jnp.sum(p, axis=-1))
        new_bufs.append(cat[:, T:])
    o = combine_groups(accs, ms, ls).astype(h.dtype).reshape(B, T, A_HEADS * A_HEAD_DIM)
    return o @ w_o, new_bufs

def retention_log_decay():
    return jnp.log1p(-jnp.exp2(-5.0 - jnp.arange(R_HEADS, dtype=jnp.float32)))

def retention_chunk(state, q, k, v, log_decay):
    C = q.shape[2]
    idx = jnp.arange(C, dtype=jnp.float32)
    rel = idx[:, None] - idx[None, :]
    dmask = jnp.where(rel >= 0, jnp.exp(jnp.maximum(rel, 0.0) * log_decay[:, None, None]), 0.0)
    q_decay = jnp.exp((idx + 1.0)[None, :] * log_decay[:, None])
    k_decay = jnp.exp((C - 1.0 - idx)[None, :] * log_decay[:, None])
    inter = jnp.einsum('bhcd,bhde->bhce', q, state) * q_decay[None, :, :, None]
    scores = jnp.einsum('bhid,bhjd->bhij', q, k) * dmask[None]
    o = inter + jnp.einsum('bhij,bhje->bhie', scores, v)
    new_state = state * jnp.exp(C * log_decay)[None, :, None, None] + \
        jnp.einsum('bhjd,bhje->bhde', k * k_decay[None, :, :, None], v)
    return o, new_state

def r_project(h, pos, w_in):
    B, S, _ = h.shape
    p = h @ w_in
    nqk, nv = R_HEADS * R_QK_DIM, R_HEADS * R_V_DIM
    q = p[..., :nqk].reshape(B, S, R_HEADS, R_QK_DIM)
    k = p[..., nqk:2 * nqk].reshape(B, S, R_HEADS, R_QK_DIM)
    v = p[..., 2 * nqk:2 * nqk + nv].reshape(B, S, R_HEADS, R_V_DIM)
    gate = p[..., 2 * nqk + nv:]
    q = rope(q, pos)
    k = rope(k, pos) * (R_QK_DIM ** -0.5)
    return q, k, v, gate

def r_output(o, gate, out_norm, w_o):
    B, S = o.shape[:2]
    y = rmsnorm(o, out_norm).reshape(B, S, R_HEADS * R_V_DIM)
    y = y * jax.nn.silu(gate.astype(jnp.float32))
    return y.astype(gate.dtype) @ w_o

def mixer_b_prompt(h, w_in, out_norm, w_o):
    B, S, _ = h.shape
    q, k, v, gate = r_project(h, jnp.arange(S), w_in)
    lg = retention_log_decay()
    nc = S // R_CHUNK

    def chunks(t):
        return t.astype(jnp.float32).reshape(B, nc, R_CHUNK, R_HEADS, t.shape[-1]).transpose(1, 0, 3, 2, 4)

    def step(state, qkv):
        o, st = retention_chunk(state, qkv[0], qkv[1], qkv[2], lg)
        return st, o

    s0 = jnp.zeros((B, R_HEADS, R_QK_DIM, R_V_DIM), jnp.float32)
    s_final, o = lax.scan(step, s0, (chunks(q), chunks(k), chunks(v)))
    o = o.transpose(1, 0, 3, 2, 4).reshape(B, S, R_HEADS, R_V_DIM)
    return r_output(o, gate, out_norm, w_o), s_final

def mixer_b_sample(h, state, w_in, out_norm, w_o):
    B, T, _ = h.shape
    q, k, v, gate = r_project(h, PAST_LEN + jnp.arange(T), w_in)

    def heads_first(t):
        return t.astype(jnp.float32).transpose(0, 2, 1, 3)

    o, new_state = retention_chunk(state.astype(jnp.float32), heads_first(q), heads_first(k),
                                   heads_first(v), retention_log_decay())
    return r_output(o.transpose(0, 2, 1, 3), gate, out_norm, w_o), new_state

def setup_inputs(seed: int = 0) -> dict:
    key = jax.random.key(seed)
    ks = jax.random.split(key, 24)
    f32 = jnp.float32

    def nrm(k, shape, scale):
        return scale * jax.random.normal(k, shape, f32)

    a_width = A_HEADS * A_HEAD_DIM
    r_in = R_HEADS * (2 * R_QK_DIM + 2 * R_V_DIM)
    return {
        "x_prompt": nrm(ks[0], (BATCH, SEQ, D_MODEL), 1.0),
        "x_sample": nrm(ks[1], (DEC_BATCH, DEC_SEQ, D_MODEL), 1.0),
        "cache_kv_g0": nrm(ks[2], (N_A_LAYERS, DEC_BATCH, min(WINDOWS[0], PAST_LEN), 2, A_HEADS, A_HEAD_DIM), 1.0),
        "cache_kv_g1": nrm(ks[3], (N_A_LAYERS, DEC_BATCH, min(WINDOWS[1], PAST_LEN), 2, A_HEADS, A_HEAD_DIM), 1.0),
        "cache_kv_g2": nrm(ks[4], (N_A_LAYERS, DEC_BATCH, min(WINDOWS[2], PAST_LEN), 2, A_HEADS, A_HEAD_DIM), 1.0),
        "state_retention": nrm(ks[5], (N_B_LAYERS, DEC_BATCH, R_HEADS, R_QK_DIM, R_V_DIM), 1.0),
        "mix_norm": 1.0 + nrm(ks[6], (DEPTH, D_MODEL), 0.1),
        "ffn_norm": 1.0 + nrm(ks[7], (DEPTH, D_MODEL), 0.1),
        "a_w_qkv": nrm(ks[8], (N_A_LAYERS, D_MODEL, N_GROUPS * 3 * a_width), D_MODEL ** -0.5),
        "a_q_norm": 1.0 + nrm(ks[9], (N_A_LAYERS, N_GROUPS, A_HEAD_DIM), 0.1),
        "a_k_norm": 1.0 + nrm(ks[10], (N_A_LAYERS, N_GROUPS, A_HEAD_DIM), 0.1),
        "a_w_o": nrm(ks[11], (N_A_LAYERS, a_width, D_MODEL), a_width ** -0.5),
        "r_w_in": nrm(ks[12], (N_B_LAYERS, D_MODEL, r_in), D_MODEL ** -0.5),
        "r_out_norm": 1.0 + nrm(ks[13], (N_B_LAYERS, R_HEADS, R_V_DIM), 0.1),
        "r_w_o": nrm(ks[14], (N_B_LAYERS, R_HEADS * R_V_DIM, D_MODEL), (R_HEADS * R_V_DIM) ** -0.5),
        "f_w_gate": nrm(ks[15], (DEPTH, D_MODEL, FFN_HIDDEN), D_MODEL ** -0.5),
        "f_w_up": nrm(ks[16], (DEPTH, D_MODEL, FFN_HIDDEN), D_MODEL ** -0.5),
        "f_w_down": nrm(ks[17], (DEPTH, FFN_HIDDEN, D_MODEL), FFN_HIDDEN ** -0.5),
    }

def reference(x_prompt, x_sample, cache_kv_g0, cache_kv_g1, cache_kv_g2, state_retention,
              mix_norm, ffn_norm, a_w_qkv, a_q_norm, a_k_norm, a_w_o,
              r_w_in, r_out_norm, r_w_o, f_w_gate, f_w_up, f_w_down):
    xp, xs = x_prompt, x_sample
    caches = (cache_kv_g0, cache_kv_g1, cache_kv_g2)
    kv_p = [[] for _ in range(N_GROUPS)]
    kv_s = [[] for _ in range(N_GROUPS)]
    ret_p, ret_s = [], []
    for i in range(DEPTH):
        hp = rmsnorm(xp, mix_norm[i])
        hs = rmsnorm(xs, mix_norm[i])
        j = i // N_MIXERS
        if i % N_MIXERS == 0:
            yp, rows = mixer_a_prompt(hp, a_w_qkv[j], a_q_norm[j], a_k_norm[j], a_w_o[j])
            ys, bufs = mixer_a_sample(hs, [c[j] for c in caches], a_w_qkv[j], a_q_norm[j], a_k_norm[j], a_w_o[j])
            for g in range(N_GROUPS):
                kv_p[g].append(rows[g])
                kv_s[g].append(bufs[g])
        else:
            yp, sp = mixer_b_prompt(hp, r_w_in[j], r_out_norm[j], r_w_o[j])
            ys, ss = mixer_b_sample(hs, state_retention[j], r_w_in[j], r_out_norm[j], r_w_o[j])
            ret_p.append(sp)
            ret_s.append(ss)
        xp = xp + yp
        xs = xs + ys
        xp = xp + swiglu(rmsnorm(xp, ffn_norm[i]), f_w_gate[i], f_w_up[i], f_w_down[i])
        xs = xs + swiglu(rmsnorm(xs, ffn_norm[i]), f_w_gate[i], f_w_up[i], f_w_down[i])
    return (xp, xs,
            jnp.stack(kv_p[0]), jnp.stack(kv_s[0]),
            jnp.stack(kv_p[1]), jnp.stack(kv_s[1]),
            jnp.stack(kv_p[2]), jnp.stack(kv_s[2]),
            jnp.stack(ret_p), jnp.stack(ret_s))


_drawn_inputs = setup_inputs


def setup_inputs(seed=0):
    import zlib

    import numpy as np

    out = dict(_drawn_inputs(seed))
    spreads = {}
    factors = {'a_q_norm': 2.956}
    for name, (base, spread) in spreads.items():
        noise = np.random.default_rng([zlib.crc32(name.encode()), seed]).standard_normal(out[name].shape)
        drawn = base * np.exp(spread * noise) if base else spread * noise
        out[name] = __import__('jax').numpy.asarray(drawn.astype(out[name].dtype))
    for name, factor in factors.items():
        out[name] = (out[name] * factor).astype(out[name].dtype)
    return out
```

```python
from contextlib import ExitStack

import concourse.bass as bass
from concourse import mybir

F32 = mybir.dt.float32
F32R = mybir.dt.float32r
ALU = mybir.AluOpType
ACT = mybir.ActivationFunctionType
AX = mybir.AxisListType

P = 128
D = 1024
KC = D // P
NS, NP = 8, 1024
T = NS + NP
TG = 3
TS = T // TG
MT = 1 + NP // P
UW = 2048
HC = UW // KC
G, H, DH = 3, 8, 64
AW = H * DH
RH, RQ, RV = 4, 256, 512
FF = 2816
FG = FF // HC
EPS = 1e-6
NB = 6
SLOTS = 3
RS = 4

QKV_J, WO_J, FFN_J, R1_J, RO_J = 6 * MT, 8 * TG, 12 + 8 * TG, 12 + 2 * MT + 12, 8 * TG
J_QKV = 0
J_WO = J_QKV + G * QKV_J
J_FFN0 = J_WO + WO_J
J_R1 = J_FFN0 + FG * FFN_J
J_RO = J_R1 + RH * R1_J
J_FFN1 = J_RO + RH * RO_J
U_QKV = 0
U_WO = U_QKV + 6 * G
U_FFN0 = U_WO + 3
U_R1 = U_FFN0 + 3 * FG
U_RO = U_R1 + 6 * RH
U_FFN1 = U_RO + 3 * RH
UNITS = U_FFN1 + 3 * FG
PAIRS = 4
AT_SEGMENTS = [(0, 0, 1), (0, 1, PAIRS), (1, 0, PAIRS), (2, 0, PAIRS)]
AT_UNITS = [(g, i, k) for g in range(G) for i in range(PAIRS) for k in range(2)]
AT_PREV = [g == 0 and (i, k) != (0, 0) or g == 1 and k == 1 for g, i, k in AT_UNITS]
AT_LOADS = [16 * (6 if g == 2 else 4 if prev else 3) for (g, _, _), prev in zip(AT_UNITS, AT_PREV)]
AT_STORES = [32 if g == 2 else 16 for g, _, _ in AT_UNITS]
OUT_TILES = [(0, 1, 2), (3, 4, 5), (6, 7)]


def free(j, i=0, per=0):
    return i * (per // NB) + (j // NB + 1)


def drain(j, i=0, per=0):
    return i * (per // NB) + (j // NB + 2)


def tile_columns(m):
    return 0 if m == 0 else NS + P * (m - 1)


def trunk(nc, x, w, c, kv_cache, state_in, y, kv_p, kv_s, ret_p, ret_s, scratch):
    qkv_dram, acc_dram, q_dram, k_dram, v_dram, g_dram = scratch
    ctx = ExitStack()

    def sb(name, shape, dt=F32, scope=None):
        return (scope or ctx).enter_context(nc.sbuf_tensor(name, shape, dt))

    def sem(name):
        return ctx.enter_context(nc.semaphore(name))

    xT = sb("xT", [P, KC, T])
    raw = sb("raw", [P, SLOTS, UW])
    wH = sb("wH", [P, SLOTS, UW], F32R)
    wL = sb("wL", [P, SLOTS, UW], F32R)
    gains = sb("gains", [P, 4, KC])
    small = sb("small", [P, 2])
    epsb = small[:, 0:1]
    eps64 = small[:, 1:2]
    ones = sb("ones", [P, P])
    ident = sb("ident", [P, P])

    A = ExitStack()
    hH = sb("hH", [P, KC, T], F32R, A)
    hL = sb("hL", [P, KC, T], F32R, A)
    sq = sb("sq", [P, 4, TS], scope=A)
    un = sb("un", [P, 4, TS], scope=A)
    rt = sb("rt", [P, TG, TS], scope=A)
    B = ExitStack()
    ropeC = sb("ropeC", [P, MT, DH], scope=B)
    ropeS = sb("ropeS", [P, MT, DH], scope=B)
    qkg = sb("qkg", [P, 2 * G, DH], scope=B)
    junk = sb("junk", [P, 2, HC], scope=B)
    ss = sb("ss", [P, 2, 4], scope=B)
    rq = sb("rq", [P, 2, 4], scope=B)
    ri = sb("ri", [P, 2, 4], scope=B)
    qn = sb("qn", [P, 4, DH], scope=B)
    qc = sb("qc", [P, 4, DH], scope=B)
    qs = sb("qs", [P, 4, DH], scope=B)
    ot = sb("ot", [P, NB, HC], scope=B)
    B.close()
    B = ExitStack()
    hidH = sb("hidH", [P, 2, T], F32R, B)
    hidL = sb("hidL", [P, 2, T], F32R, B)
    B.close()
    B = ExitStack()
    cosR = sb("cosR", [P, T], scope=B)
    sinR = sb("sinR", [P, T], scope=B)
    rw = sb("rw", [P, 4, 2 * TS], scope=B)
    B.close()
    gs = un
    us = rt
    A.close()

    A = ExitStack()
    oH = sb("oH", [P, 4, T], F32R, A)
    oL = sb("oL", [P, 4, T], F32R, A)
    B = ExitStack()
    maskP = sb("maskP", [P, 2 * P], scope=B)
    maskD = sb("maskD", [P, P], scope=B)
    qkv = sb("qkv", [P, 2, 3, AW], scope=B)
    vprev = sb("vprev", [P, 2, AW], scope=B)
    aq = sb("aq", [P, 4, P], scope=B)
    ak = sb("ak", [P, 4, 2 * P], scope=B)
    sc = sb("sc", [P, H, 2 * P], scope=B)
    pt = sb("pt", [P, H, 2, P], scope=B)
    al = sb("al", [P, 2, H, DH + 2], scope=B)
    cb = sb("cb", [P, 2, G, H, DH + 2], scope=B)
    cw = sb("cw", [P, 2, G, H], scope=B)
    cm = sb("cm", [P, 4, H], scope=B)
    cp = sb("cp", [P, 3, AW], scope=B)
    B.close()
    B = ExitStack()
    bK = sb("bK", [P, 2, 2, AW], scope=B)
    bQ = sb("bQ", [P, 2, 2, AW], scope=B)
    bV = sb("bV", [P, NS, 2, AW], scope=B)
    bS = sb("bS", [P, 2, NS * H], scope=B)
    bP = sb("bP", [NS * H, 2 * P], scope=B)
    bM = sb("bM", [P, NS, NS * H], scope=B)
    bT = sb("bT", [P, 2, NS, NS * H], scope=B)
    bD = sb("bD", [NS * H, AW], scope=B)
    bE = sb("bE", [NS * H, NS], scope=B)
    bA = sb("bA", [NS * H, AW], scope=B)
    bl = sb("bl", [NS * H, 4], scope=B)
    B.close()
    A.close()

    A = ExitStack()
    yH = sb("yH", [P, 4, T], F32R, A)
    yL = sb("yL", [P, 4, T], F32R, A)
    dmask = sb("dmask", [P, P], scope=A)
    qdec = sb("qdec", [P, P], scope=A)
    decay = sb("decay", [P, 4], scope=A)
    ron = sb("ron", [P, 4], scope=A)
    eye8 = sb("eye8", [P, NS, NS], scope=A)
    g1, gC, kdec = decay[:, 0:1], decay[:, 1:2], decay[:, 2:3]
    rqT = sb("rqT", [P, RS, 2, P], scope=A)
    rkT = sb("rkT", [P, RS, 2, P], scope=A)
    rv = sb("rv", [P, RS, RV], scope=A)
    rg = sb("rg", [P, RS, 4, P], scope=A)
    kd = sb("kd", [P, 2, 2, P], scope=A)
    qd = sb("qd", [P, 2, 2, P], scope=A)
    sT = sb("sT", [P, 2, P], scope=A)
    state = sb("state", [P, 2, RV], scope=A)
    rsq = sb("rsq", [P, 4, P], scope=A)
    rr = sb("rr", [P, 2, P], scope=A)
    ry = sb("ry", [P, 2, 4, P], scope=A)
    zS = sb("zS", [P, RS, 2, RV], scope=A)
    zV = sb("zV", [P, RS, RV], scope=A)
    zq = sb("zq", [P, 2, 2, NS], scope=A)
    zg = sb("zg", [P, 4, NS], scope=A)
    zm = sb("zm", [P, 2, NS, NS], scope=A)
    zo = sb("zo", [NS, RV], scope=A)
    zl = sb("zl", [NS, 4], scope=A)
    zy = sb("zy", [P, 2, 4, NS], scope=A)
    A.close()

    ps = ctx.enter_context(nc.psum_tensor("ps", [P, 8, 512], F32))

    raw_loaded = [sem(f"raw_loaded{s}") for s in range(SLOTS)]
    hi_ready = [sem(f"hi_ready{s}") for s in range(SLOTS)]
    lo_ready = [sem(f"lo_ready{s}") for s in range(SLOTS)]
    job_done = sem("job_done")
    drained = [sem(f"drained{b}") for b in range(NB)]
    x_loaded = sem("x_loaded")
    const_loaded = sem("const_loaded")
    table_loaded = sem("table_loaded")
    ones_set = sem("ones_set")
    sq_ready, sq_used, sum_done = sem("sq_ready"), sem("sq_used"), sem("sum_done")
    root_ready, recip_ready = sem("root_ready"), sem("recip_ready")
    normed, h_hi, h_lo = sem("normed"), sem("h_hi"), sem("h_lo")
    head_sq, root_q = sem("head_sq"), sem("root_q")
    rope_step, rope_done = sem("rope_step"), sem("rope_done")
    stored = [sem(f"stored{b}") for b in range(NB)]
    hid_hi, hid_ready = sem("hid_hi"), sem("hid_ready")
    rrope_step, rrope_done = sem("rrope_step"), sem("rrope_done")
    rstored = [sem(f"rstored{b}") for b in range(4)]
    at_loaded = [sem(f"at_loaded{b}") for b in range(2)]
    q_turned, k_turned, aq_ready, ak_ready, ak_prev = (sem(n) for n in ("q_turned", "k_turned", "aq_ready", "ak_ready", "ak_prev"))
    s_done, s_masked, m_ready, p_ready = sem("s_done"), sem("s_masked"), sem("m_ready"), sem("p_ready")
    p_turned, pt_ready, pt_ready2, pv_done, acc_ready = (sem(n) for n in ("p_turned", "pt_ready", "pt_ready2", "pv_done", "acc_ready"))
    acc_stored = [sem(f"acc_stored{b}") for b in range(2)]
    cb_loaded = [sem(f"cb_loaded{b}") for b in range(2)]
    c_step, cm_done, cw_exp, co_ready, co_turned, o_hi, o_lo = (sem(n) for n in ("c_step", "cm_done", "cw_exp", "co_ready", "co_turned", "o_hi", "o_lo"))
    b_loaded = [sem(f"b_loaded{b}") for b in range(2)]
    b_prod, b_red = sem("b_prod"), sem("b_red")
    bv_loaded, b_scored, b_turned, b_step, b_exp, b_pturned, b_masked, b_pv, b_diag, b_out, b_oh, b_ol = (
        sem(n) for n in ("bv_loaded", "b_scored", "b_turned", "b_step", "b_exp", "b_pturned", "b_masked", "b_pv",
                         "b_diag", "b_out", "b_oh", "b_ol"))
    r_loaded = [sem(f"r_loaded{b}") for b in range(RS)]
    k_up, kd_ready, rs_done, sT_ready, qd_ready, ro_done, up_done, st_ready = (
        sem(n) for n in ("k_up", "kd_ready", "rs_done", "sT_ready", "qd_ready", "ro_done", "up_done", "st_ready"))
    rsq_ready, rsum_done, rroot_ready, rstep, y_ready, y_hi, y_lo = (
        sem(n) for n in ("rsq_ready", "rsum_done", "rroot_ready", "rstep", "y_ready", "y_hi", "y_lo"))
    head_loaded, sp_gate, pe_gate = sem("head_loaded"), sem("sp_gate"), sem("pe_gate")
    z_loaded = [sem(f"z_loaded{b}") for b in range(RS)]
    zm_half = sem("zm_half")
    zqg_loaded, zm_ready, z_scaled, z_new, z_read = (sem(n) for n in ("zqg_loaded", "zm_ready", "z_scaled", "z_new", "z_read"))
    z_stored = [sem(f"z_stored{b}") for b in range(RS)]
    zl_step, zr_ready, zo_ready, zo_turned, zy_step, zy_hi, zy_lo = (
        sem(n) for n in ("zl_step", "zr_ready", "zo_ready", "zo_turned", "zy_step", "zy_hi", "zy_lo"))
    state_stored = sem("state_stored")
    copied = sem("copied")
    y_stored = sem("y_stored")


    def hi_ready_at(u, i=0, per=0):
        return i * (per // SLOTS) + (u // SLOTS + 1)

    def norm_x_wait(eng, n, t):
        if n == 0:
            eng.wait_ge(x_loaded, 16)
            return
        if n == 1 or n == 3:
            j = (J_WO + WO_J if n == 1 else J_RO + RH * RO_J) - 1
        else:
            j = J_FFN0 + FG * FFN_J - 1 - 8 * (TG - 1 - t)
        for jj in range(j - NB + 1, j + 1):
            eng.wait_ge(drained[jj % NB], drain(jj))

    def tok(t):
        return slice(t * TS, (t + 1) * TS)

    with nc.Block() as block:

        @block.gpsimd
        def _(pool):
            for s in range(SLOTS):
                pool.dma_start(raw[:, s, :], w[s]).then_inc(raw_loaded[s], 16)
            with pool.Fori(1, UNITS // SLOTS) as r:
                for s in range(SLOTS):
                    pool.wait_ge(lo_ready[s], r)
                    pool.dma_start(raw[:, s, :], w[bass.ds(r * SLOTS + s, 1)].rearrange("a p n -> (a p) n"))\
                        .then_inc(raw_loaded[s], 16)

        @block.sync
        def _(sp):
            sp.dma_start(xT[:, :, :], x).then_inc(x_loaded, 16)
            for dst, src in ((gains[:, :, :], c["gains"]), (small[:, :], c["small"]), (ident[:, :], c["ident"]),
                             (ropeC[:, :, :], c["ropeC"]), (ropeS[:, :, :], c["ropeS"]), (qkg[:, :, :], c["qkg"])):
                sp.dma_start(dst, src).then_inc(const_loaded, 16)
            for g in range(G):
                sp.dma_start(kv_s[g][:, 0:kv_s[g].shape[1] - 1, :], kv_cache[g][:, 1:, :]).then_inc(copied, 16)

            with sp.Fori(0, G) as g:
                for u in range(6):
                    for m in range(MT):
                        jj = u * MT + m
                        b = jj % NB
                        rows = NS if m == 0 else P
                        dst = qkv_dram[bass.ds(g, 1), u // 2, tile_columns(m):tile_columns(m) + rows,
                                       (u % 2) * HC:(u % 2 + 1) * HC].rearrange("a t n -> (a t) n")
                        if u < 4:
                            sp.wait_ge(rope_done, g * (4 * MT) + (jj + 1))
                        else:
                            sp.wait_ge(drained[b], drain(jj, g, QKV_J))
                        sp.sem_inc(sp_gate, 1)
                        sp.dma_start(dst, ot[0:rows, b, :]).then_inc(stored[b], 16)
            for b in range(NB):
                sp.wait_ge(stored[b], 16 * (G * QKV_J // NB + 1))
            for g in range(G):
                n = kv_p[g].shape[0]
                for s in range(2):
                    sp.dma_start(kv_p[g][:, s, :], qkv_dram[g, 1 + s, T - n:T, :]).then_inc(copied, 16)
                    sp.dma_start(kv_s[g][:, kv_s[g].shape[1] - 1, s * AW:(s + 1) * AW], qkv_dram[g, 1 + s, 0:NS, :]).then_inc(copied, 16)

            sp.wait_ge(job_done, J_WO)
            sp.wait_ge(rope_done, G * 4 * MT)
            sp.dma_start(maskP[:, :], c["maskP"]).then_inc(table_loaded, 16)
            sp.dma_start(maskD[:, :], c["maskD"]).then_inc(table_loaded, 16)

            def pieces(src, unit):
                g, i, k = unit
                if g == 0:
                    return [(slice(0, P), src[(2 * i + k) * P:(2 * i + k + 1) * P, :])]
                if g == 1:
                    return [(slice(0, P), src.rearrange("(l r) n -> r l n", r=4)[i, k * P:(k + 1) * P, :])]
                by_residue = src.rearrange("(l r) n -> r l n", r=16)
                return [(slice(q * 64, (q + 1) * 64), by_residue[4 * i + 2 * k + q, :, :]) for q in range(2)]

            def at_load(a):
                unit = AT_UNITS[a]
                g, _, k = unit
                if a >= 2:
                    sp.wait_ge(pv_done, a - 1)
                for s in range(3):
                    for part, src in pieces(qkv_dram[g, s, NS:T, :], unit):
                        sp.dma_start(qkv[part, k, s, :], src).then_inc(at_loaded[k], 16)
                if AT_PREV[a]:
                    for part, src in pieces(qkv_dram[g, 2, NS:T, :], AT_UNITS[a - 1]):
                        sp.dma_start(vprev[part, k, :], src).then_inc(at_loaded[k], 16)

            at_load(0)
            at_load(1)
            for a, unit in enumerate(AT_UNITS):
                if a + 2 < len(AT_UNITS):
                    at_load(a + 2)
                sp.wait_ge(acc_ready, a + 1)
                for part, dst in pieces(acc_dram[unit[0]], unit):
                    sp.dma_start(dst, al[part, unit[2], :, :].rearrange("p h n -> p (h n)")).then_inc(acc_stored[unit[2]], 16)
            for k in range(2):
                sp.wait_ge(acc_stored[k], 16 + sum(AT_STORES[k::2]))
            for m in range(NP // P):
                if m >= 2:
                    sp.wait_ge(co_ready, m - 1)
                sp.dma_start(cb[:, m % 2, :, :, :].rearrange("p g h n -> p g (h n)"),
                             acc_dram[:, m * P:(m + 1) * P, :].rearrange("g p n -> p g n")).then_inc(cb_loaded[m % 2], 16)

            sp.wait_ge(co_ready, NP // P)
            sp.wait_ge(co_turned, NP // P)
            sp.dma_start(bM[:, :, :], c["blockmask"]).then_inc(table_loaded, 16)
            sp.dma_start(bD[:, :], c["diagmask"]).then_inc(table_loaded, 16)
            sp.dma_start(bE[:, :], c["select"]).then_inc(table_loaded, 16)

            def cache_rows(b, s):
                cols = slice(s * AW, (s + 1) * AW)
                return ((slice(0, P), 0, kv_cache[0][b, :, cols]),
                        (slice(0, 64), 1, kv_cache[1][b, :, cols].rearrange("(l r) n -> l r n", r=4)[:, 0, :]),
                        (slice(64, 80), 1, kv_cache[2][b, :, cols].rearrange("(l r) n -> l r n", r=16)[:, 0, :]),
                        (slice(80, 83), 1, qkv_dram[:, 1 + s, b, :]))

            for b in range(NS):
                if b >= 2:
                    sp.wait_ge(b_scored, b - 1)
                for part, tl, src in cache_rows(b, 0):
                    sp.dma_start(bK[part, b % 2, tl, :], src).then_inc(b_loaded[b % 2], 16)
                for part, tl, g in ((slice(0, P), 0, 0), (slice(0, 64), 1, 1), (slice(64, 80), 1, 2)):
                    n = part.stop - part.start
                    sp.dma_start(bQ[part, b % 2, tl, :], qkv_dram[g, 0, b, :].partition_broadcast(n)).then_inc(b_loaded[b % 2], 16)
                sp.dma_start(bQ[80:83, b % 2, 1, :], qkv_dram[:, 0, b, :]).then_inc(b_loaded[b % 2], 16)
                for part, tl, src in cache_rows(b, 1):
                    sp.dma_start(bV[part, b, tl, :], src).then_inc(bv_loaded, 16)

            sp.wait_ge(job_done, J_R1)
            sp.dma_start(cosR[:, :], c["cosR"]).then_inc(table_loaded, 16)
            sp.dma_start(sinR[:, :], c["sinR"]).then_inc(table_loaded, 16)
            with sp.Fori(0, RH) as h:
                n = 0
                for dst in (q_dram, k_dram):
                    for t in range(TG):
                        sp.wait_ge(rrope_done, h * (2 * TG) + (n + 2))
                        sp.sem_inc(sp_gate, 1)
                        sp.dma_start(dst[bass.ds(h, 1), :, :, tok(t)].rearrange("a p f t -> (a p) f t"),
                                     rw[:, n % 4, :].rearrange("p (f t) -> p f t", f=2)).then_inc(rstored[n % 4], 16)
                        n += 1
                for u in range(2):
                    for m in range(MT):
                        rows = NS if m == 0 else P
                        jj = 12 + u * MT + m
                        sp.wait_ge(drained[jj % NB], drain(J_R1 + jj, h, R1_J))
                        sp.sem_inc(sp_gate, 1)
                        sp.dma_start(v_dram[bass.ds(h, 1), tile_columns(m):tile_columns(m) + rows,
                                            u * HC:(u + 1) * HC].rearrange("a t n -> (a t) n"),
                                     rw[0:rows, n % 4, 0:HC]).then_inc(rstored[n % 4], 16)
                        n += 1
                for u in range(2):
                    for t in range(TG):
                        for f in range(2):
                            jj = 12 + 2 * MT + u * 6 + t * 2 + f
                            sp.wait_ge(drained[jj % NB], drain(J_R1 + jj, h, R1_J))
                            sp.sem_inc(sp_gate, 1)
                            sp.dma_start(g_dram[bass.ds(h, 1), :, 2 * u + f, tok(t)].rearrange("a p t -> (a p) t"),
                                         rw[:, n % 4, 0:TS]).then_inc(rstored[n % 4], 16)
                            n += 1
            for b in range(4):
                sp.wait_ge(rstored[b], 16 * (RH * 36 // 4 + 1))

            sp.wait_ge(job_done, J_RO)
            sp.dma_start(eye8[:, :, :], c["eye8"]).then_inc(table_loaded, 16)
            with sp.Fori(0, RH) as h:
                head = bass.ds(h, 1)

                def chunk_load(ch):
                    k = ch % RS
                    cols = slice(NS + ch * P, NS + (ch + 1) * P)
                    sp.wait_ge(y_lo, h * 8 + (ch + 1))
                    sp.sem_inc(sp_gate, 1)
                    sp.dma_start(rqT[:, k, :, :], q_dram[head, :, :, cols].rearrange("a p f t -> (a p) f t")).then_inc(r_loaded[k], 16)
                    sp.dma_start(rkT[:, k, :, :], k_dram[head, :, :, cols].rearrange("a p f t -> (a p) f t")).then_inc(r_loaded[k], 16)
                    sp.dma_start(rv[:, k, :], v_dram[head, cols, :].rearrange("a t n -> (a t) n")).then_inc(r_loaded[k], 16)
                    sp.dma_start(rg[:, k, :, :], g_dram[head, :, :, cols].rearrange("a p f t -> (a p) f t")).then_inc(r_loaded[k], 16)

                def z_load(b):
                    k = b % RS
                    sp.wait_ge(z_stored[k], h * (16 * NS // RS) + 16 * (b // RS + 1))
                    sp.wait_ge(z_read, h * NS + (b + 1))
                    sp.sem_inc(sp_gate, 1)
                    sp.dma_start(zS[:, k, :, :], state_in[b, head, :, :].rearrange("a (f p) n -> (a p) f n", p=P))\
                        .then_inc(z_loaded[k], 16)
                    sp.dma_start(zV[:, k, :], v_dram[head, b:b + 1, :].rearrange("a t n -> (a t n)").partition_broadcast(P))\
                        .then_inc(z_loaded[k], 16)

                for n in range(RS):
                    chunk_load(n)
                    z_load(n)
                sp.wait_ge(zy_lo, h + 1)
                sp.sem_inc(sp_gate, 1)
                sp.dma_start(dmask[:, :], c["dmask"][head, :, :].rearrange("a p t -> (a p) t")).then_inc(head_loaded, 16)
                sp.dma_start(qdec[:, :], c["qdec"][head, :, :].rearrange("a p t -> (a p) t")).then_inc(head_loaded, 16)
                sp.dma_start(decay[:, :], c["decay"][head, :, :].rearrange("a p t -> (a p) t")).then_inc(head_loaded, 16)
                sp.dma_start(ron[:, :], c["ron"][head, :, :].rearrange("a p t -> (a p) t")).then_inc(head_loaded, 16)
                sp.dma_start(zq[:, 0, :, :], q_dram[head, :, :, 0:NS].rearrange("a p f t -> (a p) f t")).then_inc(zqg_loaded, 16)
                sp.dma_start(zq[:, 1, :, :], k_dram[head, :, :, 0:NS].rearrange("a p f t -> (a p) f t")).then_inc(zqg_loaded, 16)
                sp.dma_start(zg[:, :, :], g_dram[head, :, :, 0:NS].rearrange("a p f t -> (a p) f t")).then_inc(zqg_loaded, 16)
                for b in range(NS):
                    sp.wait_ge(z_new, h * (2 * NS) + (2 * b + 2))
                    sp.sem_inc(sp_gate, 1)
                    sp.dma_start(ret_s[b, head, :, :].rearrange("a (f p) n -> (a p) f n", p=P), zS[:, b % RS, :, :])\
                        .then_inc(z_stored[b % RS], 16)
                    if b + RS < NS:
                        chunk_load(b + RS)
                        z_load(b + RS)
                sp.wait_ge(st_ready, h * 16 + 16)
                sp.sem_inc(sp_gate, 1)
                sp.dma_start(ret_p[head, :, :].rearrange("a (f p) n -> (a p) f n", p=P), state[:, :, :]).then_inc(state_stored, 16)

            last = J_FFN1 + FG * FFN_J
            for jj in range(last - NB, last):
                sp.wait_ge(drained[jj % NB], drain(jj))
            sp.dma_start(y, xT[:, :, :]).then_inc(y_stored, 16)
            sp.wait_ge(y_stored, 16)
            sp.wait_ge(copied, 16 * (G + 4 * G))
            sp.wait_ge(state_stored, 16 * (RH + 1))
            for k in range(RS):
                sp.wait_ge(z_stored[k], 16 * (RH * NS // RS + 1))

        @block.scalar
        def _(act):
            def cut_hi(u, jobs, i=0, per_u=0, per_j=0):
                s = u % SLOTS
                act.wait_ge(raw_loaded[s], i * (16 * (per_u // SLOTS)) + 16 * (u // SLOTS + 1))
                if jobs:
                    act.wait_ge(job_done, i * per_j + jobs)
                act.activation(wH[:, s, :], raw[:, s, :], ACT.Copy).then_inc(hi_ready[s], 1)

            def norm(n):
                def squares(t):
                    norm_x_wait(act, n, t)
                    for k in range(KC):
                        a = (n * TG + t) * KC + k
                        if a >= 4:
                            act.wait_ge(sq_used, a - 3)
                        act.activation(sq[:, a % 4, :], xT[:, k, tok(t)], ACT.Square).then_inc(sq_ready, 1)

                def root(t):
                    b = 6 + (n * TG + t) % 2
                    act.wait_ge(sum_done, n * TG + t + 1)
                    act.activation(rt[:, t, :], ps[:, b, 0:TS], ACT.Sqrt, bias=epsb, scale=1.0 / D).then_inc(root_ready, 1)

                squares(0)
                squares(1)
                root(0)
                squares(2)
                root(1)
                root(2)
                for t in range(TG):
                    for k in range(KC):
                        a = (n * TG + t) * KC + k
                        act.wait_ge(normed, a + 1)
                        act.activation(hH[:, k, tok(t)], un[:, a % 4, :], ACT.Copy).then_inc(h_hi, 1)

            act.wait_ge(const_loaded, 96)
            cut_hi(0, 0)
            cut_hi(1, 0)
            norm(0)

            with act.Fori(0, G) as g:
                for u in range(6):
                    if u == 0:
                        act.wait_ge(drained[NB - 1], free(NB - 1, g, QKV_J))
                    cut_hi(U_QKV + u + 2, u * MT, g, 6, QKV_J)
                    for m in range(MT):
                        jj = u * MT + m
                        b = jj % NB
                        act.wait_ge(job_done, g * QKV_J + (jj + 1))
                        if u < 4:
                            k = jj % 2
                            bank = ps[:, b, 0:HC].rearrange("p (h d) -> p h d", h=4)
                            for h in range(4):
                                act.activation(junk[:, k, h * DH:(h + 1) * DH], bank[:, h, :], ACT.Square,
                                               accum_out=ss[:, k, h:h + 1]).then_inc(head_sq, 1)
                            act.wait_ge(head_sq, g * (16 * MT) + 4 * (jj + 1))
                            if jj >= 2:
                                act.wait_ge(rope_done, g * (4 * MT) + (jj - 1))
                            if u < 2:
                                act.activation(rq[:, k, :], ss[:, k, :], ACT.Sqrt, bias=eps64, scale=1.0).then_inc(root_q, 1)
                            else:
                                act.activation(rq[:, k, :], ss[:, k, :], ACT.Sqrt, bias=epsb, scale=1.0 / DH).then_inc(root_q, 1)
                        else:
                            act.wait_ge(stored[b], g * (16 * (QKV_J // NB)) + 16 * (jj // NB + 1))
                            act.activation(ot[:, b, :], ps[:, b, 0:HC], ACT.Copy).then_inc(drained[b], 1)

            def at_unit(k, a, i, prev):
                def n(x):
                    return i * (2 * x)
                if a:
                    act.wait_ge(s_done, n(2) + 2 * a)
                if prev:
                    act.activation(ak[:, :, 0:P], ak[:, :, P:2 * P], ACT.Copy).then_inc(ak_prev, 1)
                act.wait_ge(q_turned, n(1) + (a + 1))
                act.activation(aq[:, :, :], ps[:, 0, :].rearrange("p (c t) -> p c t", c=4), ACT.Copy).then_inc(aq_ready, 1)
                act.wait_ge(m_ready, n(1) + (a + 1))
                for xh in range(H):
                    w_ = sc[:, xh, 0:2 * P] if prev else sc[:, xh, P:2 * P]
                    act.activation(w_, w_, ACT.Exp, bias=al[:, k, xh, DH:DH + 1],
                                   accum_out=al[:, k, xh, DH + 1:DH + 2]).then_inc(p_ready, 1)
                for q in (1, 3):
                    act.wait_ge(p_turned, n(4) + (4 * a + q + 1))
                    if prev:
                        act.activation(pt[:, 2 * q:2 * q + 2, :, :], ps[:, 2 + q, :].rearrange("p (x h t) -> p x h t", x=2, h=2),
                                       ACT.Copy).then_inc(pt_ready2, 1)
                    else:
                        act.activation(pt[:, 2 * q:2 * q + 2, 1, :], ps[:, 2 + q, :].rearrange("p (x h t) -> p x h t", x=2, h=2)[:, :, 1, :],
                                       ACT.Copy).then_inc(pt_ready2, 1)

            act.wait_ge(table_loaded, 32)
            base = 0
            for g, lo, hi in AT_SEGMENTS:
                kinds = AT_PREV[base:base + 2]
                if hi - lo == 1:
                    for k in range(2):
                        at_unit(k, base + k, 0, kinds[k])
                else:
                    with act.Fori(0, hi - lo) as i:
                        for k in range(2):
                            at_unit(k, base + k, i, kinds[k])
                base += 2 * (hi - lo)
            for m in range(NP // P):
                act.wait_ge(c_step, 7 * m + 3)
                act.activation(cw[:, m % 2, :, :], cw[:, m % 2, :, :], ACT.Exp).then_inc(cw_exp, 1)
                act.wait_ge(co_turned, m + 1)
                act.activation(oH[:, :, NS + m * P:NS + (m + 1) * P], ps[:, m % 2, :].rearrange("p (c t) -> p c t", c=4),
                               ACT.Copy).then_inc(o_hi, 1)
            act.wait_ge(b_step, 2)
            act.activation(bP[:, 0:211], bP[:, 0:211], ACT.Exp, bias=bl[:, 0:1], accum_out=bl[:, 1:2]).then_inc(b_exp, 1)
            act.wait_ge(b_out, 1)
            act.activation(oH[:, :, 0:NS], ps[:, 3, 0:4 * NS].rearrange("p (c t) -> p c t", c=4), ACT.Copy).then_inc(b_oh, 1)

            for u in range(3):
                cut_hi(U_WO + u + 2, J_WO + (0, 9, 18)[u])
            norm(1)

            def ffn_turn(i, j0, u0, last=False):
                cut_hi(u0 + 2, j0, i, 3, FFN_J)
                for p in range(6):
                    jg, ju = j0 + 2 * p, j0 + 2 * p + 1
                    act.wait_ge(job_done, i * FFN_J + (jg + 1))
                    act.wait_ge(drained[ju % NB], free(ju, i, FFN_J))
                    act.activation(gs[:, p % 3, :], ps[:, jg % NB, 0:TS], ACT.Silu).then_inc(drained[jg % NB], 1)
                if not last:
                    cut_hi(u0 + 3, j0 + 12, i, 3, FFN_J)
                    cut_hi(u0 + 4, j0 + 12, i, 3, FFN_J)

            with act.Fori(0, FG) as i:
                ffn_turn(i, J_FFN0, U_FFN0)
            norm(2)

            act.wait_ge(const_loaded, 96)
            with act.Fori(0, RH) as h:
                def unit_cut(u):
                    cut_hi(U_R1 + u + 2, J_R1 + (0, 6, 12, 12 + MT, 12 + 2 * MT, 18 + 2 * MT)[u], h, 6, R1_J)
                unit_cut(0)
                unit_cut(1)
                n = 6
                for u in range(2):
                    unit_cut(2 + u)
                    for m in range(MT):
                        jj = 12 + u * MT + m
                        act.wait_ge(job_done, h * R1_J + (J_R1 + jj + 1))
                        act.wait_ge(rstored[n % 4], h * (16 * 9) + 16 * (n // 4 + 1))
                        act.activation(rw[:, n % 4, 0:HC], ps[:, jj % NB, 0:HC], ACT.Copy).then_inc(drained[jj % NB], 1)
                        n += 1
                for u in range(2):
                    unit_cut(4 + u)
                    for q in range(6):
                        jj = 12 + 2 * MT + u * 6 + q
                        act.wait_ge(job_done, h * R1_J + (J_R1 + jj + 1))
                        act.wait_ge(rstored[n % 4], h * (16 * 9) + 16 * (n // 4 + 1))
                        act.activation(rw[:, n % 4, 0:TS], ps[:, jj % NB, 0:TS], ACT.Silu).then_inc(drained[jj % NB], 1)
                        n += 1

            act.wait_ge(table_loaded, 16 * 8)
            with act.Fori(0, RH) as h:
                act.wait_ge(head_loaded, h * 64 + 64)

                def y_cut(ch):
                    act.wait_ge(y_ready, h * 8 + (ch + 1))
                    act.activation(yH[:, :, NS + ch * P:NS + (ch + 1) * P], ry[:, ch % 2, :, :], ACT.Copy).then_inc(y_hi, 1)

                for ch in range(8):
                    k = ch % 2
                    act.wait_ge(k_up, h * 8 + (ch + 1))
                    if ch >= 2:
                        act.wait_ge(up_done, h * 8 + (ch - 1))
                    act.activation(kd[:, k, :, :], ps[:, 0, 0:2 * P].rearrange("p (f d) -> p f d", f=2), ACT.Copy,
                                   scale=kdec).then_inc(kd_ready, 1)
                    act.wait_ge(z_loaded[ch % RS], h * (32 * NS // RS) + 32 * (ch // RS + 1))
                    act.activation(zS[:, ch % RS, :, :], zS[:, ch % RS, :, :], ACT.Copy, scale=g1).then_inc(z_scaled, 1)
                    if ch:
                        y_cut(ch - 1)
                    act.wait_ge(ro_done, h * 8 + (ch + 1))
                    act.activation(rsq[:, :, :], ps[:, 4 + k, :].rearrange("p (e t) -> p e t", e=4), ACT.Square).then_inc(rsq_ready, 1)
                    act.wait_ge(rsum_done, h * 8 + (ch + 1))
                    act.activation(rr[:, k, :], ps[:, 6, 0:P], ACT.Sqrt, bias=epsb, scale=1.0 / RV).then_inc(rroot_ready, 1)
                y_cut(7)
                act.wait_ge(z_read, h * NS + (NS + RS))
                act.activation(zo[:, :], ps[0:NS, 7, :], ACT.Square, accum_out=zl[:, 0:1]).then_inc(zl_step, 1)
                act.wait_ge(zl_step, h * 2 + 1)
                act.activation(zl[:, 1:2], zl[:, 0:1], ACT.Sqrt, bias=epsb[0:NS], scale=1.0 / RV).then_inc(zl_step, 1)
                act.wait_ge(zr_ready, h + 1)
                act.activation(zo[:, :], ps[0:NS, 7, :], ACT.Copy, scale=zl[:, 2:3]).then_inc(zo_ready, 1)
                act.wait_ge(zy_step, h * 5 + 5)
                act.activation(yH[:, :, 0:NS], zy[:, 1, :, :], ACT.Copy).then_inc(zy_hi, 1)
                for u in range(3):
                    cut_hi(U_RO + u + 2, J_RO + (0, 9, 18)[u], h, 3, RO_J)
            for k in range(RS):
                act.wait_ge(z_stored[k], 16 * (RH * NS // RS + 1))
            act.wait_ge(state_stored, 16 * (RH + 1))
            norm(3)
            with act.Fori(0, FG - 1) as i:
                ffn_turn(i, J_FFN1, U_FFN1)
            ffn_turn(FG - 1, J_FFN1, U_FFN1, last=True)

        @block.tensor
        def _(pe):
            def norm(n):
                for t in range(TG):
                    b = 6 + (n * TG + t) % 2
                    if n * TG + t >= 2:
                        pe.wait_ge(root_ready, n * TG + t - 1)
                    for k in range(KC):
                        pe.wait_ge(sq_ready, (n * TG + t) * KC + k + 1)
                        mm = pe.matmul(ps[:, b, 0:TS], ones[:, :], sq[:, ((n * TG + t) * KC + k) % 4, :],
                                       start=(k == 0), stop=(k == KC - 1))
                        mm.then_inc(sq_used, 1)
                    pe.wait_ge(sq_used, (n * TG + t + 1) * KC)
                    pe.sem_inc(sum_done, 1)

            def bank_free(j, i=0, per=0):
                pe.wait_ge(drained[j % NB], free(j, i, per))
                return j % NB

            def passes(out, lhs, rhs):
                n = len(lhs)
                for k in range(n):
                    for q, (a, b) in enumerate(((0, 0), (0, 1), (1, 0))):
                        mm = pe.matmul(out, lhs[k][a], rhs[k][b], start=(k == 0 and q == 0), stop=(k == n - 1 and q == 2))
                return mm

            def unit_ready(u, i=0, per=0):
                pe.wait_ge(lo_ready[u % SLOTS], hi_ready_at(u, i, per))
                return u % SLOTS

            def tokens_stationary(s, m, b):
                c0 = tile_columns(m)
                wv = [[x_[:, s, :].rearrange("p (k n) -> p k n", k=KC)[:, k, :] for x_ in (wH, wL)] for k in range(KC)]
                return passes(ps[:, b, 0:HC], [[x_[:, k, c0:c0 + P] for x_ in (hH, hL)] for k in range(KC)], wv)

            def tokens_moving(s, f, t, b):
                wv = [[x_[:, s, :].rearrange("p (k n) -> p k n", k=KC)[:, k, f * P:(f + 1) * P] for x_ in (wH, wL)] for k in range(KC)]
                return passes(ps[:, b, 0:TS], wv, [[x_[:, k, tok(t)] for x_ in (hH, hL)] for k in range(KC)])

            def out_projection(u0, j0, oh, ol, i=0, per_u=0, per_j=0):
                j = j0
                for a, tiles in enumerate(OUT_TILES):
                    s = unit_ready(u0 + a, i, per_u)
                    for dl in range(len(tiles)):
                        for t in range(TG):
                            b = bank_free(j, i, per_j)
                            wv = [[x_[:, s, (dl * 4 + k) * P:(dl * 4 + k + 1) * P] for x_ in (wH, wL)] for k in range(4)]
                            passes(ps[:, b, 0:TS], wv, [[x_[:, k, tok(t)] for x_ in (oh, ol)] for k in range(4)])\
                                .then_inc(job_done, 1)
                            j += 1

            pe.wait_ge(ones_set, 1)
            norm(0)
            pe.wait_ge(h_lo, TG * KC)
            with pe.Fori(0, G) as g:
                for u in range(6):
                    s = unit_ready(u, g, 6)
                    for m in range(MT):
                        b = bank_free(u * MT + m, g, QKV_J)
                        tokens_stationary(s, m, b).then_inc(job_done, 1)

            def at_unit(k, a, i, prev):
                def n(x):
                    return i * (2 * x)
                halves = (0, 1) if prev else (1,)
                pe.wait_ge(at_loaded[k], i * AT_LOADS[a] + sum(AT_LOADS[k:a + 1:2]))
                if a:
                    pe.wait_ge(aq_ready, n(1) + a)
                for p in range(4):
                    mm = pe.transpose(ps[:, 0, p * P:(p + 1) * P], qkv[:, k, 0, p * P:(p + 1) * P], ident[:, :])
                mm.then_inc(q_turned, 1)
                if a:
                    pe.wait_ge(ak_ready, n(1) + a)
                for p in range(4):
                    mm = pe.transpose(ps[:, 1, p * P:(p + 1) * P], qkv[:, k, 1, p * P:(p + 1) * P], ident[:, :])
                mm.then_inc(k_turned, 1)
                pe.wait_ge(aq_ready, n(1) + (a + 1))
                pe.wait_ge(ak_ready, n(1) + (a + 1))
                if a:
                    pe.wait_ge(pt_ready, n(2) + 2 * a)
                    pe.wait_ge(pt_ready2, n(2) + 2 * a)
                for par in range(2):
                    for hp in range(4):
                        pp = slice(par * DH, (par + 1) * DH)
                        out = ps[:, 2 + 2 * par + hp // 2, (hp % 2) * 256:(hp % 2 + 1) * 256]
                        if prev:
                            mm = pe.matmul(out, aq[pp, hp, :], ak[pp, hp, :], start=True, stop=True)
                        else:
                            mm = pe.matmul(out[:, P:2 * P], aq[pp, hp, :], ak[pp, hp, P:2 * P], start=True, stop=True)
                    mm.then_inc(s_done, 1)
                for q in range(4):
                    pe.wait_ge(p_ready, n(8) + (8 * a + 2 * q + 2))
                    for x in (2 * q, 2 * q + 1):
                        for hf in halves:
                            mm = pe.transpose(ps[:, 2 + q, (x % 2) * 256 + hf * P:(x % 2) * 256 + (hf + 1) * P],
                                              sc[:, x, hf * P:(hf + 1) * P], ident[:, :])
                    mm.then_inc(p_turned, 1)
                if a:
                    pe.wait_ge(acc_ready, n(1) + a)
                for q in range(4):
                    pe.wait_ge((pt_ready, pt_ready2)[q % 2], n(2) + (2 * a + q // 2 + 1))
                    for x in (2 * q, 2 * q + 1):
                        hd = 2 * (x % 4) + x // 4
                        for hf in halves:
                            v_ = (vprev[:, k, :], qkv[:, k, 2, :])[hf]
                            mm = pe.matmul(ps[:, 6, x * DH:(x + 1) * DH], pt[:, x, hf, :], v_[:, hd * DH:(hd + 1) * DH],
                                           start=(hf == halves[0]), stop=(hf == 1))
                mm.then_inc(pv_done, 1)

            base = 0
            for g, lo, hi in AT_SEGMENTS:
                kinds = AT_PREV[base:base + 2]
                if hi - lo == 1:
                    for k in range(2):
                        at_unit(k, base + k, 0, kinds[k])
                else:
                    with pe.Fori(0, hi - lo) as i:
                        for k in range(2):
                            at_unit(k, base + k, i, kinds[k])
                base += 2 * (hi - lo)
            pe.wait_ge(ak_ready, base)
            for m in range(NP // P):
                pe.wait_ge(co_ready, m + 1)
                if m >= 2:
                    pe.wait_ge(o_lo, m - 1)
                for p in range(4):
                    mm = pe.transpose(ps[:, m % 2, p * P:(p + 1) * P], cp[:, 0, p * P:(p + 1) * P], ident[:, :])
                mm.then_inc(co_turned, 1)

            pe.wait_ge(b_scored, NS)
            pe.wait_ge(o_lo, NP // P)
            pe.transpose(ps[0:64, 0, 0:P], bS[:, 0, :], ident[:, :])
            pe.transpose(ps[0:64, 0, P:P + 83], bS[0:83, 1, :], ident[0:83, 0:83]).then_inc(b_turned, 1)
            pe.wait_ge(b_exp, 1)
            pe.transpose(ps[:, 1, 0:64], bP[:, 0:P], ident[0:64, 0:64])
            pe.transpose(ps[0:83, 1, 64:128], bP[:, P:P + 83], ident[0:64, 0:64]).then_inc(b_pturned, 1)
            pe.wait_ge(b_masked, 2)
            pe.wait_ge(bv_loaded, 16 * 4 * NS)
            for b in range(NS):
                pe.matmul(ps[0:64, 2, :], bT[:, 0, b, :], bV[:, b, 0, :], start=(b == 0), stop=False)
                mm = pe.matmul(ps[0:64, 2, :], bT[0:83, 1, b, :], bV[0:83, b, 1, :], start=False, stop=(b == NS - 1))
            mm.then_inc(b_pv, 1)
            pe.wait_ge(b_diag, 1)
            for p in range(4):
                mm = pe.matmul(ps[:, 3, p * NS:(p + 1) * NS], bA[:, p * P:(p + 1) * P], bE[:, :], start=True, stop=True)
            mm.then_inc(b_out, 1)

            pe.wait_ge(b_ol, 1)
            out_projection(U_WO, J_WO, oH, oL)
            norm(1)

            def ffn_turn(i, j0, u0):
                s0, s1 = unit_ready(u0, i, 3), unit_ready(u0 + 1, i, 3)
                j = j0
                for t in range(TG):
                    for f in range(2):
                        for s in (s0, s1):
                            tokens_moving(s, f, t, bank_free(j, i, FFN_J)).then_inc(job_done, 1)
                            j += 1
                s = unit_ready(u0 + 2, i, 3)
                for t in range(TG):
                    pe.wait_ge(hid_ready, i * 6 + (6 * FG * (j0 == J_FFN1) + 2 * t + 2))
                    for d in range(KC):
                        b = bank_free(j, i, FFN_J)
                        wv = [[x_[:, s, k * D + d * P:k * D + (d + 1) * P] for x_ in (wH, wL)] for k in range(2)]
                        passes(ps[:, b, 0:TS], wv, [[x_[:, k, tok(t)] for x_ in (hidH, hidL)] for k in range(2)])\
                            .then_inc(job_done, 1)
                        j += 1

            pe.wait_ge(h_lo, 2 * TG * KC)
            with pe.Fori(0, FG) as i:
                ffn_turn(i, J_FFN0, U_FFN0)
            norm(2)
            pe.wait_ge(h_lo, 3 * TG * KC)
            with pe.Fori(0, RH) as h:
                jj = 0
                for u in range(6):
                    s = unit_ready(U_R1 + u, h, 6)
                    if u in (2, 3):
                        for m in range(MT):
                            tokens_stationary(s, m, bank_free(J_R1 + jj, h, R1_J)).then_inc(job_done, 1)
                            jj += 1
                    else:
                        for t in range(TG):
                            for f in range(2):
                                tokens_moving(s, f, t, bank_free(J_R1 + jj, h, R1_J)).then_inc(job_done, 1)
                                jj += 1

            pe.wait_ge(table_loaded, 16 * 8)
            with pe.Fori(0, RH) as h:
                for q in range(NB):
                    pe.wait_ge(drained[q], free(J_RO + q, h, RO_J))

                def keys(ch):
                    k = ch % RS
                    pe.wait_ge(r_loaded[k], h * (64 * 8 // RS) + 64 * (ch // RS + 1))
                    pe.wait_ge(kd_ready, h * 8 + (ch + 1))
                    for f in range(2):
                        mm = pe.transpose(ps[:, 0, f * P:(f + 1) * P], rkT[:, k, f, :], ident[:, :])
                    mm.then_inc(k_up, 1)
                    pe.wait_ge(sT_ready, h * 8 + (ch + 1))
                    for f in range(2):
                        mm = pe.matmul(ps[:, 1, 0:P], rkT[:, k, f, :], rqT[:, k, f, :], start=(f == 0), stop=(f == 1))
                    mm.then_inc(rs_done, 1)

                keys(0)
                for ch in range(8):
                    k = ch % 2
                    pe.wait_ge(sT_ready, h * 8 + (ch + 2))
                    pe.wait_ge(qd_ready, h * 8 + (ch + 1))
                    if ch >= 2:
                        pe.wait_ge(y_ready, h * 8 + (ch - 1))
                    if ch:
                        pe.wait_ge(st_ready, h * 16 + 2 * ch)
                    for e in range(4):
                        out = ps[:, 4 + k, e * P:(e + 1) * P]
                        mm = pe.matmul(out, rv[:, ch % RS, e * P:(e + 1) * P], sT[:, k, :], start=True, stop=(ch == 0))
                        if ch:
                            for f in range(2):
                                mm = pe.matmul(out, state[:, f, e * P:(e + 1) * P], qd[:, k, f, :], start=False, stop=(f == 1))
                    mm.then_inc(ro_done, 1)
                    if ch < 7:
                        keys(ch + 1)
                    pe.wait_ge(kd_ready, h * 8 + (ch + 2))
                    if ch:
                        pe.wait_ge(st_ready, h * 16 + 2 * ch)
                    for f in range(2):
                        mm = pe.matmul(ps[:, 2 + f, :], kd[:, k, f, :], rv[:, ch % RS, :], start=True, stop=True)
                    mm.then_inc(up_done, 1)
                    if ch == 0:
                        pe.wait_ge(zm_ready, h + 1)
                        pe.wait_ge(zo_ready, h + 1)
                    pe.wait_ge(z_new, h * (2 * NS) + (2 * ch + 2))
                    for f in range(2):
                        mm = pe.matmul(ps[0:NS, 7, :], zm[:, f, ch, :], zS[:, ch % RS, f, :],
                                       start=(ch == 0 and f == 0), stop=(ch == NS - 1 and f == 1))
                    mm.then_inc(z_read, 1)
                    pe.wait_ge(rsq_ready, h * 8 + (ch + 1))
                    if ch:
                        pe.wait_ge(rroot_ready, h * 8 + ch)
                    for e in range(4):
                        mm = pe.matmul(ps[:, 6, 0:P], ones[:, :], rsq[:, e, :], start=(e == 0), stop=(e == 3))
                    mm.then_inc(rsum_done, 1)
                pe.wait_ge(zo_ready, h + 2)
                pe.wait_ge(y_ready, h * 8 + 8)
                pe.sem_inc(pe_gate, 1)
                for e in range(4):
                    mm = pe.transpose(ps[:, 6, e * NS:(e + 1) * NS], zo[:, e * P:(e + 1) * P], ident[0:NS, 0:NS])
                mm.then_inc(zo_turned, 1)
                pe.wait_ge(zy_lo, h + 2)
                pe.wait_ge(y_lo, h * 8 + (8 + RS))
                pe.wait_ge(st_ready, h * 16 + 16)
                out_projection(U_RO, J_RO, yH, yL, h, 3, RO_J)
            norm(3)
            pe.wait_ge(h_lo, 4 * TG * KC)
            with pe.Fori(0, FG) as i:
                ffn_turn(i, J_FFN1, U_FFN1)

        @block.vector
        def _(dve):
            tt, ts, stt = dve.tensor_tensor, dve.tensor_scalar, dve.scalar_tensor_tensor

            def cut_lo(u, i=0, per_u=0):
                s = u % SLOTS
                dve.wait_ge(hi_ready[s], hi_ready_at(u, i, per_u))
                tt(wL[:, s, :], raw[:, s, :], wH[:, s, :], ALU.subtract).then_inc(lo_ready[s], 1)

            def norm(n):
                def low(a):
                    k, t = a % KC, a // KC % TG
                    dve.wait_ge(h_hi, a + 1)
                    tt(hL[:, k, tok(t)], un[:, a % 4, :], hH[:, k, tok(t)], ALU.subtract).then_inc(h_lo, 1)
                for t in range(TG):
                    dve.wait_ge(root_ready, n * TG + t + 1)
                    dve.reciprocal(rt[:, t, :], rt[:, t, :]).then_inc(recip_ready, 1)
                    dve.wait_ge(recip_ready, n * TG + t + 1)
                    for k in range(KC):
                        a = (n * TG + t) * KC + k
                        if a >= 4:
                            dve.wait_ge(h_lo, a - 3)
                        stt(out=un[:, a % 4, :], in0=xT[:, k, tok(t)], scalar=gains[:, n, k:k + 1], in1=rt[:, t, :],
                            op0=ALU.mult, op1=ALU.mult).then_inc(normed, 1)
                        if a - n * TG * KC >= 2:
                            low(a - 2)
                low((n + 1) * TG * KC - 2)
                low((n + 1) * TG * KC - 1)

            dve.memset(ones[:, :], 1.0).then_inc(ones_set, 1)
            for b in range(NB):
                dve.sem_inc(drained[b], 1)
                dve.sem_inc(stored[b], 16)
            for b in range(4):
                dve.sem_inc(rstored[b], 16)
            for b in range(RS):
                dve.sem_inc(z_stored[b], 16)
            for s_, n_ in ((acc_stored[0], 16), (acc_stored[1], 16), (y_lo, RS), (zy_lo, 1), (z_read, RS), (kd_ready, 1), (sT_ready, 1), (rrope_done, 1), (zo_ready, 1), (state_stored, 16)):
                dve.sem_inc(s_, n_)
            dve.wait_ge(const_loaded, 96)
            cut_lo(0)
            cut_lo(1)
            dve.wait_ge(x_loaded, 16)
            norm(0)

            with dve.Fori(0, G) as g:
                for u in range(6):
                    cut_lo(u + 2, g, 6)
                    if u >= 4:
                        continue
                    for m in range(MT):
                        jj = u * MT + m
                        b, k = jj % NB, jj % 2
                        steps = g * (7 * 4 * MT) + 7 * jj
                        bank = ps[:, b, 0:HC].rearrange("p (h d) -> p h d", h=4)
                        dve.wait_ge(root_q, g * (4 * MT) + (jj + 1))
                        dve.reciprocal(ri[:, k, :], rq[:, k, :]).then_inc(rope_step, 1)
                        dve.wait_ge(rope_step, steps + 1)
                        for h in range(4):
                            mm = stt(out=qn[:, h, :], in0=bank[:, h, :], scalar=ri[:, k, h:h + 1],
                                     in1=qkg[:, bass.ds(g * 2 + u // 2, 1), :].rearrange("p a d -> p (a d)"),
                                     op0=ALU.mult, op1=ALU.mult)
                            mm.then_inc(*((rope_step, 1) if h < 3 else (drained[b], 1)))
                        dve.wait_ge(rope_step, steps + 4)
                        dve.wait_ge(drained[b], drain(jj, g, QKV_J))
                        tt(qc[:, :, :], qn[:, :, :], ropeC[:, m:m + 1, :].broadcast_to([P, 4, DH]), ALU.mult).then_inc(rope_step, 1)
                        for a in range(2):
                            tt(qs[:, :, a * 32:(a + 1) * 32], qn[:, :, (1 - a) * 32:(2 - a) * 32],
                               ropeS[:, m:m + 1, a * 32:(a + 1) * 32].broadcast_to([P, 4, 32]), ALU.mult).then_inc(rope_step, 1)
                        dve.wait_ge(rope_step, steps + 7)
                        dve.wait_ge(stored[b], g * (16 * (QKV_J // NB)) + 16 * (jj // NB + 1))
                        tt(ot[:, b, :].rearrange("p (h d) -> p h d", h=4), qc[:, :, :], qs[:, :, :], ALU.add).then_inc(rope_done, 1)

            def at_unit(k, a, i, prev, mask):
                def n(x):
                    return i * (2 * x)
                w0 = 0 if prev else P
                dve.wait_ge(k_turned, n(1) + (a + 1))
                if a:
                    dve.wait_ge(s_done, n(2) + 2 * a)
                if prev:
                    dve.wait_ge(ak_prev, PREVS(a, i))
                dve.tensor_copy(ak[:, :, P:2 * P], ps[:, 1, :].rearrange("p (c t) -> p c t", c=4)).then_inc(ak_ready, 1)
                dve.wait_ge(acc_stored[k], i * AT_STORES[a] + (16 + sum(AT_STORES[k:a:2])))
                if a:
                    dve.wait_ge(p_turned, n(4) + 4 * a)
                for q in range(4):
                    if q % 2 == 0:
                        dve.wait_ge(s_done, n(2) + (2 * a + q // 2 + 1))
                    tt(sc[:, 2 * q:2 * q + 2, w0:2 * P], ps[:, 2 + q, :].rearrange("p (x w) -> p x w", x=2)[:, :, w0:2 * P],
                       mask.rearrange("p (x w) -> p x w", x=1).broadcast_to([P, 2, 2 * P - w0]), ALU.add).then_inc(s_masked, 1)
                dve.wait_ge(s_masked, n(4) + (4 * a + 4))
                dve.tensor_reduce(al[:, k, :, DH:DH + 1], sc[:, :, w0:2 * P], AX.X, ALU.max, negate=True).then_inc(m_ready, 1)
                for q in (0, 2):
                    dve.wait_ge(p_turned, n(4) + (4 * a + q + 1))
                    src = ps[:, 2 + q, :].rearrange("p (x h t) -> p x h t", x=2, h=2)
                    if prev:
                        dve.tensor_copy(pt[:, 2 * q:2 * q + 2, :, :], src).then_inc(pt_ready, 1)
                    else:
                        dve.tensor_copy(pt[:, 2 * q:2 * q + 2, 1, :], src[:, :, 1, :]).then_inc(pt_ready, 1)
                dve.wait_ge(pv_done, n(1) + (a + 1))
                dve.tensor_copy(al[:, k, :, 0:DH], ps[:, 6, :].rearrange("p (x d) -> p x d", x=H)).then_inc(acc_ready, 1)

            dve.wait_ge(table_loaded, 32)
            base = prevs = 0
            for g, lo, hi in AT_SEGMENTS:
                kinds = AT_PREV[base:base + 2]
                masks = [maskD[:, :] if g == 2 else maskP[:, :] if kinds[k] else maskP[:, P:2 * P] for k in range(2)]
                per = sum(kinds)

                def PREVS(a, i, prevs=prevs, per=per, base=base, kinds=kinds):
                    return i * per + (prevs + sum(kinds[:a - base + 1]))
                if hi - lo == 1:
                    for k in range(2):
                        at_unit(k, base + k, 0, kinds[k], masks[k])
                else:
                    with dve.Fori(0, hi - lo) as i:
                        for k in range(2):
                            at_unit(k, base + k, i, kinds[k], masks[k])
                base += 2 * (hi - lo)
                prevs += per * (hi - lo)

            def low_o(m):
                dve.wait_ge(o_hi, m + 1)
                cols = slice(NS + m * P, NS + (m + 1) * P)
                tt(oL[:, :, cols], ps[:, m % 2, :].rearrange("p (c t) -> p c t", c=4), oH[:, :, cols], ALU.subtract).then_inc(o_lo, 1)

            for m in range(NP // P):
                k, n = m % 2, 7 * m
                dve.wait_ge(cb_loaded[k], 16 * (m // 2 + 1))
                nm = [cb[:, k, g, :, DH] for g in range(G)]
                tt(cm[:, 0, :], nm[0], nm[1], ALU.min).then_inc(c_step, 1)
                dve.wait_ge(c_step, n + 1)
                tt(cm[:, 1, :], cm[:, 0, :], nm[2], ALU.min).then_inc(c_step, 1)
                dve.wait_ge(c_step, n + 2)
                tt(cw[:, k, :, :], cm[:, 1:2, :].broadcast_to([P, G, H]), cb[:, k, :, :, DH], ALU.subtract).then_inc(c_step, 1)
                dve.wait_ge(cw_exp, m + 1)
                tt(cb[:, k, :, :, DH], cw[:, k, :, :], cb[:, k, :, :, DH + 1], ALU.mult).then_inc(c_step, 1)
                dve.wait_ge(c_step, n + 4)
                dve.tensor_reduce(cm[:, 2, :], cb[:, k, :, :, DH].rearrange("p g h -> p h g"), AX.X, ALU.add).then_inc(c_step, 1)
                dve.wait_ge(c_step, n + 5)
                dve.reciprocal(cm[:, 3, :], cm[:, 2, :]).then_inc(c_step, 1)
                dve.wait_ge(c_step, n + 6)
                tt(cw[:, k, :, :], cw[:, k, :, :], cm[:, 3:4, :].broadcast_to([P, G, H]), ALU.mult).then_inc(c_step, 1)
                dve.wait_ge(c_step, n + 7)
                for g in range(G):
                    tt(cb[:, k, g, :, 0:DH], cb[:, k, g, :, 0:DH],
                       cw[:, k, g, :].rearrange("p (h a) -> p h a", a=1).broadcast_to([P, H, DH]), ALU.mult)\
                        .then_inc(cm_done, 1)
                dve.wait_ge(cm_done, 4 * m + 3)
                tt(cp[:, 1, :].rearrange("p (h d) -> p h d", h=H), cb[:, k, 0, :, 0:DH], cb[:, k, 1, :, 0:DH], ALU.add).then_inc(cm_done, 1)
                dve.wait_ge(cm_done, 4 * m + 4)
                if m:
                    low_o(m - 1)
                tt(cp[:, 0, :].rearrange("p (hp par d) -> p par hp d", hp=4, par=2),
                   cp[:, 1, :].rearrange("p (par hp d) -> p par hp d", hp=4, par=2),
                   cb[:, k, 2, :, 0:DH].rearrange("p (par hp) d -> p par hp d", par=2), ALU.add).then_inc(co_ready, 1)
            low_o(NP // P - 1)

            for b in range(NS):
                k = b % 2
                dve.wait_ge(b_loaded[k], 16 * 8 * (b // 2 + 1))
                for tl, n in ((0, P), (1, 83)):
                    tt(bK[0:n, k, tl, :], bK[0:n, k, tl, :], bQ[0:n, k, tl, :], ALU.mult).then_inc(b_prod, 1)
                for tl, n in ((0, P), (1, 83)):
                    dve.wait_ge(b_prod, 2 * b + tl + 1)
                    dve.tensor_reduce(bS[0:n, tl, b * H:(b + 1) * H], bK[0:n, k, tl, :].rearrange("p (h d) -> p h d", h=H),
                                      AX.X, ALU.add).then_inc(*((b_red, 1) if tl == 0 else (b_scored, 1)))
            dve.wait_ge(b_red, NS)
            dve.wait_ge(b_turned, 1)
            dve.tensor_copy(bP[:, 0:211], ps[0:64, 0, 0:211]).then_inc(b_step, 1)
            dve.wait_ge(b_step, 1)
            dve.tensor_reduce(bl[:, 0:1], bP[:, 0:211], AX.X, ALU.max, negate=True).then_inc(b_step, 1)
            dve.wait_ge(b_exp, 1)
            dve.reciprocal(bl[:, 2:3], bl[:, 1:2]).then_inc(b_step, 1)
            dve.wait_ge(b_pturned, 1)
            dve.wait_ge(table_loaded, 16 * 5)
            for tl, n in ((0, P), (1, 83)):
                tt(bT[0:n, tl, :, :], ps[0:n, 1, tl * 64:(tl + 1) * 64].rearrange("p (a c) -> p a c", a=1).broadcast_to([n, NS, 64]),
                   bM[0:n, :, :], ALU.mult).then_inc(b_masked, 1)
            dve.wait_ge(b_pv, 1)
            dve.wait_ge(b_step, 3)
            stt(out=bA[:, :], in0=ps[0:64, 2, :], scalar=bl[:, 2:3], in1=bD[:, :], op0=ALU.mult, op1=ALU.mult).then_inc(b_diag, 1)
            dve.wait_ge(b_oh, 1)
            tt(oL[:, :, 0:NS], ps[:, 3, 0:4 * NS].rearrange("p (c t) -> p c t", c=4), oH[:, :, 0:NS], ALU.subtract).then_inc(b_ol, 1)

            def out_drain(u0, j0, i=0, per_u=0, per_j=0):
                j = j0
                for a, tiles in enumerate(OUT_TILES):
                    cut_lo(u0 + a + 2, i, per_u)
                    for d in tiles:
                        for t in range(TG):
                            dve.wait_ge(job_done, i * per_j + (j + 1))
                            tt(xT[:, d, tok(t)], ps[:, j % NB, 0:TS], xT[:, d, tok(t)], ALU.add).then_inc(drained[j % NB], 1)
                            j += 1

            out_drain(U_WO, J_WO)
            norm(1)

            def ffn_turn(i, j0, u0, last=False):
                cut_lo(u0 + 2, i, 3)
                h0 = 6 * FG * (j0 == J_FFN1)
                for p in range(6):
                    jg, ju = j0 + 2 * p, j0 + 2 * p + 1
                    t, f = p // 2, p % 2
                    dve.wait_ge(drained[jg % NB], drain(jg, i, FFN_J))
                    dve.wait_ge(job_done, i * FFN_J + (ju + 1))
                    if p >= 2:
                        dve.wait_ge(hid_ready, i * 6 + (h0 + p - 1))
                    tt(us[:, p % 2, :], ps[:, ju % NB, 0:TS], gs[:, p % 3, :], ALU.mult).then_inc(drained[ju % NB], 1)
                    dve.wait_ge(drained[ju % NB], drain(ju, i, FFN_J))
                    dve.tensor_copy(hidH[:, f, tok(t)], us[:, p % 2, :]).then_inc(hid_hi, 1)
                    dve.wait_ge(hid_hi, i * 6 + (h0 + p + 1))
                    tt(hidL[:, f, tok(t)], us[:, p % 2, :], hidH[:, f, tok(t)], ALU.subtract).then_inc(hid_ready, 1)
                if not last:
                    cut_lo(u0 + 3, i, 3)
                    cut_lo(u0 + 4, i, 3)
                j = j0 + 12
                for t in range(TG):
                    for d in range(KC):
                        dve.wait_ge(job_done, i * FFN_J + (j + 1))
                        tt(xT[:, d, tok(t)], ps[:, j % NB, 0:TS], xT[:, d, tok(t)], ALU.add).then_inc(drained[j % NB], 1)
                        j += 1

            with dve.Fori(0, FG) as i:
                ffn_turn(i, J_FFN0, U_FFN0)
            norm(2)

            dve.wait_ge(table_loaded, 16 * 7)
            with dve.Fori(0, RH) as h:
                n = 0
                for u, scale in ((0, 1.0), (1, RQ ** -0.5)):
                    cut_lo(U_R1 + u + 2, h, 6)
                    for t in range(TG):
                        j1 = J_R1 + u * 6 + 2 * t
                        b1, b2 = j1 % NB, (j1 + 1) % NB
                        x1, x2 = ps[:, b1, 0:TS], ps[:, b2, 0:TS]
                        steps = h * (6 * 3) + 3 * n
                        dve.wait_ge(job_done, h * R1_J + (j1 + 2))
                        dve.wait_ge(rrope_done, h * 6 + (n + 1))
                        stt(out=un[:, 0, :], in0=x1, scalar=scale, in1=cosR[:, tok(t)], op0=ALU.mult, op1=ALU.mult).then_inc(rrope_step, 1)
                        stt(out=un[:, 1, :], in0=x2, scalar=scale, in1=sinR[:, tok(t)], op0=ALU.mult, op1=ALU.mult).then_inc(rrope_step, 1)
                        stt(out=un[:, 2, :], in0=x2, scalar=scale, in1=cosR[:, tok(t)], op0=ALU.mult, op1=ALU.mult).then_inc(drained[b2], 1)
                        stt(out=un[:, 3, :], in0=x1, scalar=scale, in1=sinR[:, tok(t)], op0=ALU.mult, op1=ALU.mult).then_inc(drained[b1], 1)
                        dve.wait_ge(rstored[n % 4], h * (16 * 9) + 16 * (n // 4 + 1))
                        dve.wait_ge(rrope_step, steps + 2)
                        tt(rw[:, n % 4, 0:TS], un[:, 0, :], un[:, 1, :], ALU.subtract).then_inc(rrope_step, 1)
                        dve.wait_ge(drained[b2], drain(j1 + 1, h, R1_J))
                        dve.wait_ge(drained[b1], drain(j1, h, R1_J))
                        dve.wait_ge(rrope_step, steps + 3)
                        tt(rw[:, n % 4, TS:2 * TS], un[:, 2, :], un[:, 3, :], ALU.add).then_inc(rrope_done, 1)
                        n += 1
                for u in range(2, 6):
                    cut_lo(U_R1 + u + 2, h, 6)

            dve.wait_ge(table_loaded, 16 * 8)
            with dve.Fori(0, RH) as h:
                dve.wait_ge(head_loaded, h * 64 + 64)

                def y_rest(ch):
                    k = ch % 2
                    n = h * (8 * 5) + 5 * ch
                    dve.wait_ge(rroot_ready, h * 8 + (ch + 1))
                    dve.reciprocal(rr[:, k, :], rr[:, k, :]).then_inc(rstep, 1)
                    dve.wait_ge(rstep, n + 1)
                    for e in range(4):
                        stt(out=ry[:, k, e, :], in0=ps[:, 4 + k, e * P:(e + 1) * P], scalar=ron[:, e:e + 1],
                            in1=rr[:, k, :], op0=ALU.mult, op1=ALU.mult).then_inc(rstep, 1)
                    dve.wait_ge(rstep, n + 5)
                    tt(ry[:, k, :, :], ry[:, k, :, :], rg[:, ch % RS, :, :], ALU.mult).then_inc(y_ready, 1)

                def y_low(ch):
                    dve.wait_ge(y_hi, h * 8 + (ch + 1))
                    cols = slice(NS + ch * P, NS + (ch + 1) * P)
                    tt(yL[:, :, cols], ry[:, ch % 2, :, :], yH[:, :, cols], ALU.subtract).then_inc(y_lo, 1)

                dve.wait_ge(zqg_loaded, h * 48 + 48)
                for f in range(2):
                    ins = tt(zm[:, f, :, :], zq[:, 0, f, :].rearrange("p (a b) -> p b a", a=1).broadcast_to([P, NS, NS]), eye8[:, :, :],
                             ALU.mult)
                    ins.then_inc(*((zm_half, 1) if f == 0 else (zm_ready, 1)))
                for ch in range(8):
                    k = ch % 2
                    dve.wait_ge(r_loaded[ch % RS], h * (64 * 8 // RS) + 64 * (ch // RS + 1))
                    tt(qd[:, k, :, :], rqT[:, ch % RS, :, :], qdec[:, :].rearrange("p (a t) -> p a t", a=1).broadcast_to([P, 2, P]), ALU.mult).then_inc(qd_ready, 1)
                    dve.wait_ge(rs_done, h * 8 + (ch + 1))
                    tt(sT[:, k, :], ps[:, 1, 0:P], dmask[:, :], ALU.mult).then_inc(sT_ready, 1)
                    if ch:
                        y_rest(ch - 1)
                        y_low(ch - 1)
                    dve.wait_ge(z_scaled, h * NS + (ch + 1))
                    for f in range(2):
                        stt(out=zS[:, ch % RS, f, :], in0=zV[:, ch % RS, :], scalar=zq[:, 1, f, ch:ch + 1], in1=zS[:, ch % RS, f, :],
                            op0=ALU.mult, op1=ALU.add).then_inc(z_new, 1)
                    dve.wait_ge(up_done, h * 8 + (ch + 1))
                    if ch == 0:
                        dve.wait_ge(state_stored, h * 16 + 16)
                    for f in range(2):
                        if ch == 0:
                            dve.tensor_copy(state[:, f, :], ps[:, 2 + f, :]).then_inc(st_ready, 1)
                        else:
                            if f == 0:
                                dve.wait_ge(st_ready, h * 16 + 2 * ch)
                            stt(out=state[:, f, :], in0=state[:, f, :], scalar=gC, in1=ps[:, 2 + f, :],
                                op0=ALU.mult, op1=ALU.add).then_inc(st_ready, 1)
                y_rest(7)
                y_low(7)
                dve.wait_ge(zl_step, h * 2 + 2)
                dve.reciprocal(zl[:, 2:3], zl[:, 1:2]).then_inc(zr_ready, 1)
                dve.wait_ge(zo_turned, h + 1)
                for e in range(4):
                    ts(zy[:, 0, e, :], ps[:, 6, e * NS:(e + 1) * NS], ron[:, e:e + 1], None, ALU.mult).then_inc(zy_step, 1)
                dve.wait_ge(zy_step, h * 5 + 4)
                tt(zy[:, 1, :, :], zy[:, 0, :, :], zg[:, :, :], ALU.mult).then_inc(zy_step, 1)
                dve.wait_ge(zy_hi, h + 1)
                tt(yL[:, :, 0:NS], zy[:, 1, :, :], yH[:, :, 0:NS], ALU.subtract).then_inc(zy_lo, 1)
                out_drain(U_RO, J_RO, h, 3, RO_J)
            norm(3)
            with dve.Fori(0, FG - 1) as i:
                ffn_turn(i, J_FFN1, U_FFN1)
            ffn_turn(FG - 1, J_FFN1, U_FFN1, last=True)
    ctx.close()


def weight_units(a_w_qkv, a_w_o, r_w_in, r_w_o, f_w_gate, f_w_up, f_w_down):
    import numpy as np
    out = np.zeros((UNITS, P, UW), np.float32)
    n = 0

    def put(block):
        nonlocal n
        block = block.reshape(P, -1)
        out[n, :, :block.shape[1]] = block
        n += 1

    def columns(w, c0):
        put(w[:, c0:c0 + HC].reshape(KC, P, HC).transpose(1, 0, 2))

    def out_rows(w):
        blocks = w.reshape(4, P, KC, P).transpose(1, 2, 0, 3)
        for tiles in OUT_TILES:
            put(blocks[:, tiles[0]:tiles[-1] + 1])

    def ffn(layer):
        for i in range(FG):
            columns(f_w_gate[layer], i * HC)
            columns(f_w_up[layer], i * HC)
            put(f_w_down[layer][i * HC:(i + 1) * HC].reshape(2, P, D).transpose(1, 0, 2))

    for c0 in range(0, 3 * G * AW, HC):
        columns(a_w_qkv[0], c0)
    out_rows(a_w_o[0])
    ffn(0)
    for h in range(RH):
        for c0 in (h * RQ, D + h * RQ, 2 * D + h * RV, 2 * D + h * RV + HC, 4 * D + h * RV, 4 * D + h * RV + HC):
            columns(r_w_in[0], c0)
    for h in range(RH):
        out_rows(r_w_o[0][h * RV:(h + 1) * RV])
    ffn(1)
    assert n == UNITS
    return out


def tables():
    import numpy as np
    f = np.float32

    def angles(pos, half):
        inv = (10000.0 ** (-np.arange(half, dtype=f) / f(half)).astype(np.float64)).astype(f)
        ang = (pos.astype(f)[:, None] * inv[None, :]).astype(f).astype(np.float64)
        return np.cos(ang).astype(f), np.sin(ang).astype(f)

    pos = np.concatenate([np.full(NS, 256), np.arange(NP)])
    out = {}
    cos, sin = angles(pos, DH // 2)
    cols = np.stack([tile_columns(m) + np.arange(P) for m in range(MT)], 1)
    out["ropeC"] = np.concatenate([cos[cols], cos[cols]], -1)
    out["ropeS"] = np.concatenate([-sin[cols], sin[cols]], -1)
    cos, sin = angles(pos, RQ // 2)
    out["cosR"], out["sinR"] = cos.T, sin.T
    i = np.arange(P)
    ok_self = i[None, :] <= i[:, None]
    out["maskP"] = np.where(np.concatenate([i[None, :] >= i[:, None], ok_self], 1), 0.0, -1e38)
    out["maskD"] = np.where(ok_self & (i[None, :] // 64 == i[:, None] // 64), 0.0, -1e38)
    out["ident"] = np.eye(P)
    lg = np.log1p(-np.exp2(-5.0 - np.arange(RH))).astype(f).astype(np.float64)
    out["small"] = np.broadcast_to([EPS, 64 * EPS], (P, 2))
    decay = np.zeros((RH, P, 4))
    decay[:, :, 0] = np.exp(lg)[:, None]
    decay[:, :, 1] = np.exp(P * lg)[:, None]
    decay[:, :, 2] = np.exp((P - 1.0 - i)[None, :] * lg[:, None])
    out["decay"] = decay
    rel = (i[None, None, :] - i[None, :, None]).astype(np.float64)
    out["dmask"] = np.where(rel >= 0, np.exp(np.maximum(rel, 0) * lg[:, None, None]), 0.0)
    out["qdec"] = np.broadcast_to(np.exp((i + 1.0)[None, :] * lg[:, None])[:, None], (RH, P, P))
    out["eye8"] = np.broadcast_to(np.eye(NS)[None], (P, NS, NS))
    b, h = np.arange(NS * H) // H, np.arange(NS * H) % H
    out["blockmask"] = np.broadcast_to((b[None, :] == np.arange(NS)[:, None])[None], (P, NS, NS * H))
    out["diagmask"] = h[:, None] == np.arange(AW)[None, :] // DH
    out["select"] = b[:, None] == np.arange(NS)[None, :]
    return {k: np.ascontiguousarray(v, dtype=f) for k, v in out.items()}


def kernel(x_prompt, x_sample, cache_kv_g0, cache_kv_g1, cache_kv_g2, state_retention,
           mix_norm, ffn_norm, a_w_qkv, a_q_norm, a_k_norm, a_w_o,
           r_w_in, r_out_norm, r_w_o, f_w_gate, f_w_up, f_w_down):
    import numpy as np
    import concourse.bacc as bacc
    from concourse.bass_utils import run_bass_kernel_spmd

    nc = bacc.Bacc("TRN2", target_bir_lowering=False, num_devices=1)
    arrays = {}

    def given(name, a):
        arrays["in_" + name] = np.ascontiguousarray(a)
        return nc.dram_tensor("in_" + name, a.shape, F32, kind="ExternalInput").ap()

    def result(name, shape):
        return nc.dram_tensor(name, shape, F32, kind="ExternalOutput").ap()

    def kept(name, shape):
        return nc.dram_tensor(name, shape, F32).ap()

    def chunked(a):
        return np.asarray(a).reshape(-1, KC, P).transpose(2, 0, 1)

    x = np.concatenate([np.asarray(x_sample)[:, 0], np.asarray(x_prompt)[0]], 0)
    x_in = given("x", x.T.reshape(KC, P, T).transpose(1, 0, 2))
    w = given("w", weight_units(*(np.asarray(a) for a in (a_w_qkv, a_w_o, r_w_in, r_w_o, f_w_gate, f_w_up, f_w_down))))
    c = {name: given(name, a) for name, a in tables().items()}
    norms = np.stack([np.asarray(a)[i] for i in range(2) for a in (mix_norm, ffn_norm)])
    c["gains"] = given("gains", chunked(norms))
    qk = np.stack([np.asarray(a_q_norm)[0], np.asarray(a_k_norm)[0]], 1).reshape(2 * G, DH)
    c["qkg"] = given("qkg", np.broadcast_to(qk[None], (P, 2 * G, DH)))
    c["ron"] = given("ron", np.asarray(r_out_norm)[0].reshape(RH, 4, P).transpose(0, 2, 1))
    caches = [np.asarray(a)[0] for a in (cache_kv_g0, cache_kv_g1, cache_kv_g2)]
    kv_cache = [given(f"cache{g}", a.reshape(NS, -1, 2 * AW)) for g, a in enumerate(caches)]
    state_in = given("state_in", np.asarray(state_retention)[0])
    y = result("y", (P, KC, T))
    keep = (128, 512, 1024)
    kv_p = [result(f"kv_p{g}", (keep[g], 2, AW)) for g in range(G)]
    kv_s = [result(f"kv_s{g}", (NS, a.shape[1], 2 * AW)) for g, a in enumerate(caches)]
    ret_p = result("ret_p", (RH, RQ, RV))
    ret_s = result("ret_s", (NS, RH, RQ, RV))
    scratch = (kept("qkv_rows", (G, 3, T, AW)), kept("acc_rows", (G, NP, H * (DH + 2))), kept("q_cols", (RH, P, 2, T)),
               kept("k_cols", (RH, P, 2, T)), kept("v_rows", (RH, T, RV)), kept("g_cols", (RH, P, 4, T)))
    trunk(nc, x_in, w, c, kv_cache, state_in, y, kv_p, kv_s, ret_p, ret_s, scratch)
    r = run_bass_kernel_spmd(nc, [arrays], core_ids=[0]).results[0]
    rows = r["y"].transpose(1, 0, 2).reshape(D, T).T
    out = [rows[NS:][None], rows[:NS][:, None]]
    for g in range(G):
        out.append(r[f"kv_p{g}"].reshape(1, 1, keep[g], 2, H, DH))
        out.append(r[f"kv_s{g}"].reshape(1, NS, -1, 2, H, DH))
    out.append(r["ret_p"][None, None])
    out.append(r["ret_s"][None])
    return tuple(out)
```

```python
from contextlib import ExitStack

import concourse.bass as bass
from concourse import mybir

F32 = mybir.dt.float32
F32R = mybir.dt.float32r
ALU = mybir.AluOpType
ACT = mybir.ActivationFunctionType
AX = mybir.AxisListType

P = 128
D = 1024
KC = D // P
NS, NP = 8, 1024
T = NS + NP
TG = 3
TS = T // TG
MT = 1 + NP // P
UW = 2048
HC = UW // KC
G, H, DH = 3, 8, 64
AW = H * DH
RH, RQ, RV = 4, 256, 512
FF = 2816
FG = FF // HC
EPS = 1e-6
NB = 6
SLOTS = 3
RS = 4

QKV_J, WO_J, FFN_J, R1_J, RO_J = 6 * MT, 8 * TG, 12 + 8 * TG, 12 + 2 * MT + 12, 8 * TG
J_QKV = 0
J_WO = J_QKV + G * QKV_J
J_FFN0 = J_WO + WO_J
J_R1 = J_FFN0 + FG * FFN_J
J_RO = J_R1 + RH * R1_J
J_FFN1 = J_RO + RH * RO_J
U_QKV = 0
U_WO = U_QKV + 6 * G
U_FFN0 = U_WO + 3
U_R1 = U_FFN0 + 3 * FG
U_RO = U_R1 + 6 * RH
U_FFN1 = U_RO + 3 * RH
UNITS = U_FFN1 + 3 * FG
AU = G * NP // P
AT_PIECES = [2 if a // 8 == 2 else 1 for a in range(AU)]
AT_PREV = [1 <= a < 8 or 8 <= a < 16 and a % 2 == 1 for a in range(AU)]
AT_RUNS = [(0, 1, 1), (1, 2, 3), (7, 1, 1), (8, 2, 3), (14, 2, 1), (16, 2, 3), (22, 2, 1)]
OUT_TILES = [(0, 1, 2), (3, 4, 5), (6, 7)]


def free(j, i=0, per=0):
    return i * (per // NB) + (j // NB + 1)


def drain(j, i=0, per=0):
    return i * (per // NB) + (j // NB + 2)


def tile_columns(m):
    return 0 if m == 0 else NS + P * (m - 1)


def trunk(nc, x, w, c, kv_cache, state_in, y, kv_p, kv_s, ret_p, ret_s, scratch):
    qkv_dram, acc_dram, q_dram, k_dram, v_dram, g_dram = scratch
    ctx = ExitStack()

    def sb(name, shape, dt=F32, scope=None):
        return (scope or ctx).enter_context(nc.sbuf_tensor(name, shape, dt))

    def sem(name):
        return ctx.enter_context(nc.semaphore(name))

    xT = sb("xT", [P, KC, T])
    raw = sb("raw", [P, SLOTS, UW])
    wH = sb("wH", [P, SLOTS, UW], F32R)
    wL = sb("wL", [P, SLOTS, UW], F32R)
    gains = sb("gains", [P, 4, KC])
    small = sb("small", [P, 2])
    epsb = small[:, 0:1]
    eps64 = small[:, 1:2]
    ones = sb("ones", [P, P])
    ident = sb("ident", [P, P])

    A = ExitStack()
    hH = sb("hH", [P, KC, T], F32R, A)
    hL = sb("hL", [P, KC, T], F32R, A)
    sq = sb("sq", [P, 4, TS], scope=A)
    un = sb("un", [P, 4, TS], scope=A)
    rt = sb("rt", [P, TG, TS], scope=A)
    B = ExitStack()
    ropeC = sb("ropeC", [P, MT, DH], scope=B)
    ropeS = sb("ropeS", [P, MT, DH], scope=B)
    qkg = sb("qkg", [P, 2 * G, DH], scope=B)
    junk = sb("junk", [P, 2, HC], scope=B)
    ss = sb("ss", [P, 2, 4], scope=B)
    rq = sb("rq", [P, 2, 4], scope=B)
    ri = sb("ri", [P, 2, 4], scope=B)
    qn = sb("qn", [P, 4, DH], scope=B)
    qc = sb("qc", [P, 4, DH], scope=B)
    qs = sb("qs", [P, 4, DH], scope=B)
    ot = sb("ot", [P, NB, HC], scope=B)
    B.close()
    B = ExitStack()
    hidH = sb("hidH", [P, 2, T], F32R, B)
    hidL = sb("hidL", [P, 2, T], F32R, B)
    gs = sb("gs", [P, 3, TS], scope=B)
    us = sb("us", [P, 2, TS], scope=B)
    B.close()
    B = ExitStack()
    cosR = sb("cosR", [P, T], scope=B)
    sinR = sb("sinR", [P, T], scope=B)
    rw = sb("rw", [P, 4, 2 * TS], scope=B)
    B.close()
    A.close()

    A = ExitStack()
    oH = sb("oH", [P, 4, T], F32R, A)
    oL = sb("oL", [P, 4, T], F32R, A)
    B = ExitStack()
    maskP = sb("maskP", [P, 2 * P], scope=B)
    maskD = sb("maskD", [P, P], scope=B)
    qkv = sb("qkv", [P, 2, 3, AW], scope=B)
    aq = sb("aq", [P, H, P], scope=B)
    ak = sb("ak", [P, 2, 4, P], scope=B)
    sc = sb("sc", [P, 2, H, 2 * P], scope=B)
    pt = sb("pt", [P, H, 2, P], scope=B)
    al = sb("al", [P, 2, H, DH + 2], scope=B)
    cb = sb("cb", [P, 2, G, H, DH + 2], scope=B)
    cw = sb("cw", [P, 2, G, H], scope=B)
    cm = sb("cm", [P, 4, H], scope=B)
    cp = sb("cp", [P, 2, AW], scope=B)
    B.close()
    B = ExitStack()
    bK = sb("bK", [P, 2, 2, AW], scope=B)
    bQ = sb("bQ", [P, 2, 2, AW], scope=B)
    bV = sb("bV", [P, NS, 2, AW], scope=B)
    bS = sb("bS", [P, 2, NS * H], scope=B)
    bP = sb("bP", [NS * H, 2 * P], scope=B)
    bM = sb("bM", [P, NS, NS * H], scope=B)
    bT = sb("bT", [P, 2, NS, NS * H], scope=B)
    bD = sb("bD", [NS * H, AW], scope=B)
    bE = sb("bE", [NS * H, NS], scope=B)
    bA = sb("bA", [NS * H, AW], scope=B)
    bl = sb("bl", [NS * H, 4], scope=B)
    B.close()
    A.close()

    A = ExitStack()
    yH = sb("yH", [P, 4, T], F32R, A)
    yL = sb("yL", [P, 4, T], F32R, A)
    dmask = sb("dmask", [P, P], scope=A)
    qdec = sb("qdec", [P, P], scope=A)
    decay = sb("decay", [P, 4], scope=A)
    ron = sb("ron", [P, 4], scope=A)
    eye8 = sb("eye8", [P, NS, NS], scope=A)
    g1, gC, kdec = decay[:, 0:1], decay[:, 1:2], decay[:, 2:3]
    rqT = sb("rqT", [P, RS, 2, P], scope=A)
    rkT = sb("rkT", [P, RS, 2, P], scope=A)
    rv = sb("rv", [P, RS, RV], scope=A)
    rg = sb("rg", [P, RS, 4, P], scope=A)
    kd = sb("kd", [P, 2, 2, P], scope=A)
    qd = sb("qd", [P, 2, 2, P], scope=A)
    sT = sb("sT", [P, 2, P], scope=A)
    state = sb("state", [P, 2, RV], scope=A)
    rsq = sb("rsq", [P, 4, P], scope=A)
    rr = sb("rr", [P, 2, P], scope=A)
    ry = sb("ry", [P, 2, 4, P], scope=A)
    zS = sb("zS", [P, RS, 2, RV], scope=A)
    zV = sb("zV", [P, RS, RV], scope=A)
    zq = sb("zq", [P, 2, 2, NS], scope=A)
    zg = sb("zg", [P, 4, NS], scope=A)
    zm = sb("zm", [P, 2, NS, NS], scope=A)
    zo = sb("zo", [NS, RV], scope=A)
    zl = sb("zl", [NS, 4], scope=A)
    zy = sb("zy", [P, 2, 4, NS], scope=A)
    A.close()

    ps = ctx.enter_context(nc.psum_tensor("ps", [P, 8, 512], F32))

    raw_loaded = [sem(f"raw_loaded{s}") for s in range(SLOTS)]
    hi_ready = [sem(f"hi_ready{s}") for s in range(SLOTS)]
    lo_ready = [sem(f"lo_ready{s}") for s in range(SLOTS)]
    job_done = sem("job_done")
    drained = [sem(f"drained{b}") for b in range(NB)]
    x_loaded = sem("x_loaded")
    const_loaded = sem("const_loaded")
    table_loaded = sem("table_loaded")
    ones_set = sem("ones_set")
    sq_ready, sq_used, sum_done = sem("sq_ready"), sem("sq_used"), sem("sum_done")
    root_ready, recip_ready = sem("root_ready"), sem("recip_ready")
    normed, h_hi, h_lo = sem("normed"), sem("h_hi"), sem("h_lo")
    head_sq, root_q = sem("head_sq"), sem("root_q")
    rope_step, rope_done = sem("rope_step"), sem("rope_done")
    stored = [sem(f"stored{b}") for b in range(NB)]
    hid_hi, hid_ready = sem("hid_hi"), sem("hid_ready")
    rrope_step, rrope_done = sem("rrope_step"), sem("rrope_done")
    rstored = [sem(f"rstored{b}") for b in range(4)]
    aqk_loaded = [sem(f"aqk_loaded{b}") for b in range(2)]
    av_loaded = [sem(f"av_loaded{b}") for b in range(2)]
    q_turned, k_turned, aq_ready, ak_ready, aq_zeroed = (sem(n) for n in ("q_turned", "k_turned", "aq_ready", "ak_ready", "aq_zeroed"))
    s_done, s_masked, m_ready, p_ready = sem("s_done"), sem("s_masked"), sem("m_ready"), sem("p_ready")
    p_turned, pt_ready, pt_ready2, pv_done, acc_ready = (sem(n) for n in ("p_turned", "pt_ready", "pt_ready2", "pv_done", "acc_ready"))
    acc_stored = [sem(f"acc_stored{b}") for b in range(2)]
    cb_loaded = [sem(f"cb_loaded{b}") for b in range(2)]
    c_step, cm_done, cw_exp, co_ready, co_turned, o_hi, o_lo = (sem(n) for n in ("c_step", "cm_done", "cw_exp", "co_ready", "co_turned", "o_hi", "o_lo"))
    b_loaded = [sem(f"b_loaded{b}") for b in range(2)]
    b_prod, b_red = sem("b_prod"), sem("b_red")
    bv_loaded, b_scored, b_turned, b_step, b_exp, b_pturned, b_masked, b_pv, b_diag, b_out, b_oh, b_ol = (
        sem(n) for n in ("bv_loaded", "b_scored", "b_turned", "b_step", "b_exp", "b_pturned", "b_masked", "b_pv",
                         "b_diag", "b_out", "b_oh", "b_ol"))
    r_loaded = [sem(f"r_loaded{b}") for b in range(RS)]
    k_up, kd_ready, rs_done, sT_ready, qd_ready, ro_done, up_done, st_ready = (
        sem(n) for n in ("k_up", "kd_ready", "rs_done", "sT_ready", "qd_ready", "ro_done", "up_done", "st_ready"))
    rsq_ready, rsum_done, rroot_ready, rstep, y_ready, y_hi, y_lo = (
        sem(n) for n in ("rsq_ready", "rsum_done", "rroot_ready", "rstep", "y_ready", "y_hi", "y_lo"))
    head_loaded, sp_gate, pe_gate = sem("head_loaded"), sem("sp_gate"), sem("pe_gate")
    z_loaded = [sem(f"z_loaded{b}") for b in range(RS)]
    zm_half = sem("zm_half")
    zqg_loaded, zm_ready, z_scaled, z_new, z_read = (sem(n) for n in ("zqg_loaded", "zm_ready", "z_scaled", "z_new", "z_read"))
    z_stored = [sem(f"z_stored{b}") for b in range(RS)]
    zl_step, zr_ready, zo_ready, zo_turned, zy_step, zy_hi, zy_lo = (
        sem(n) for n in ("zl_step", "zr_ready", "zo_ready", "zo_turned", "zy_step", "zy_hi", "zy_lo"))
    state_stored = sem("state_stored")
    copied = sem("copied")
    y_stored = sem("y_stored")


    def hi_ready_at(u, i=0, per=0):
        return i * (per // SLOTS) + (u // SLOTS + 1)

    def norm_x_wait(eng, n, t):
        if n == 0:
            eng.wait_ge(x_loaded, 16)
            return
        if n == 1 or n == 3:
            j = (J_WO + WO_J if n == 1 else J_RO + RH * RO_J) - 1
        else:
            j = J_FFN0 + FG * FFN_J - 1 - 8 * (TG - 1 - t)
        for jj in range(j - NB + 1, j + 1):
            eng.wait_ge(drained[jj % NB], drain(jj))

    def tok(t):
        return slice(t * TS, (t + 1) * TS)

    with nc.Block() as block:

        @block.gpsimd
        def _(pool):
            for s in range(SLOTS):
                pool.dma_start(raw[:, s, :], w[s]).then_inc(raw_loaded[s], 16)
            with pool.Fori(1, UNITS // SLOTS) as r:
                for s in range(SLOTS):
                    pool.wait_ge(lo_ready[s], r)
                    pool.dma_start(raw[:, s, :], w[bass.ds(r * SLOTS + s, 1)].rearrange("a p n -> (a p) n"))\
                        .then_inc(raw_loaded[s], 16)

        @block.sync
        def _(sp):
            sp.dma_start(xT[:, :, :], x).then_inc(x_loaded, 16)
            for dst, src in ((gains[:, :, :], c["gains"]), (small[:, :], c["small"]), (ident[:, :], c["ident"]),
                             (ropeC[:, :, :], c["ropeC"]), (ropeS[:, :, :], c["ropeS"]), (qkg[:, :, :], c["qkg"])):
                sp.dma_start(dst, src).then_inc(const_loaded, 16)
            for g in range(G):
                sp.dma_start(kv_s[g][:, 0:kv_s[g].shape[1] - 1, :], kv_cache[g][:, 1:, :]).then_inc(copied, 16)

            with sp.Fori(0, G) as g:
                for u in range(6):
                    for m in range(MT):
                        jj = u * MT + m
                        b = jj % NB
                        rows = NS if m == 0 else P
                        dst = qkv_dram[bass.ds(g, 1), u // 2, tile_columns(m):tile_columns(m) + rows,
                                       (u % 2) * HC:(u % 2 + 1) * HC].rearrange("a t n -> (a t) n")
                        if u < 4:
                            sp.wait_ge(rope_done, g * (4 * MT) + (jj + 1))
                        else:
                            sp.wait_ge(drained[b], drain(jj, g, QKV_J))
                        sp.sem_inc(sp_gate, 1)
                        sp.dma_start(dst, ot[0:rows, b, :]).then_inc(stored[b], 16)
            for b in range(NB):
                sp.wait_ge(stored[b], 16 * (G * QKV_J // NB + 1))
            sp.wait_ge(job_done, J_WO)
            sp.wait_ge(rope_done, G * 4 * MT)
            sp.dma_start(maskP[:, :], c["maskP"]).then_inc(table_loaded, 16)
            sp.dma_start(maskD[:, :], c["maskD"]).then_inc(table_loaded, 16)

            def pieces(src, a):
                g, i = a // 8, a % 8
                if g == 0:
                    return [(slice(0, P), src[i * P:(i + 1) * P, :])]
                if g == 1:
                    return [(slice(0, P), src.rearrange("(l r) n -> r l n", r=4)[i // 2, i % 2 * P:(i % 2 + 1) * P, :])]
                by_residue = src.rearrange("(l r) n -> r l n", r=16)
                return [(slice(q * 64, (q + 1) * 64), by_residue[2 * i + q, :, :]) for q in range(2)]

            def at_load(a, tensors, loaded):
                for s in tensors:
                    for part, src in pieces(qkv_dram[a // 8, s, NS:T, :], a):
                        sp.dma_start(qkv[part, a % 2, s, :], src).then_inc(loaded[a % 2], 16)

            for a in range(2):
                at_load(a, (0, 1), aqk_loaded)
                at_load(a, (2,), av_loaded)
            for a in range(AU):
                if a + 2 < AU:
                    sp.wait_ge(q_turned, a + 1)
                    at_load(a + 2, (0, 1), aqk_loaded)
                if 1 <= a < AU - 1:
                    sp.wait_ge(pv_done, a + 1)
                    at_load(a + 1, (2,), av_loaded)
                sp.wait_ge(acc_ready, a + 1)
                for part, dst in pieces(acc_dram[a // 8], a):
                    sp.dma_start(dst, al[part, a % 2, :, :].rearrange("p h n -> p (h n)")).then_inc(acc_stored[a % 2], 16)
            for k in range(2):
                sp.wait_ge(acc_stored[k], 16 + 16 * sum(AT_PIECES[k::2]))
            for m in range(NP // P):
                if m >= 2:
                    sp.wait_ge(co_ready, m - 1)
                sp.dma_start(cb[:, m % 2, :, :, :].rearrange("p g h n -> p g (h n)"),
                             acc_dram[:, m * P:(m + 1) * P, :].rearrange("g p n -> p g n")).then_inc(cb_loaded[m % 2], 16)

            sp.wait_ge(co_ready, NP // P)
            sp.wait_ge(co_turned, NP // P)
            sp.dma_start(bM[:, :, :], c["blockmask"]).then_inc(table_loaded, 16)
            sp.dma_start(bD[:, :], c["diagmask"]).then_inc(table_loaded, 16)
            sp.dma_start(bE[:, :], c["select"]).then_inc(table_loaded, 16)

            def cache_rows(b, s):
                cols = slice(s * AW, (s + 1) * AW)
                return ((slice(0, P), 0, kv_cache[0][b, :, cols]),
                        (slice(0, 64), 1, kv_cache[1][b, :, cols].rearrange("(l r) n -> l r n", r=4)[:, 0, :]),
                        (slice(64, 80), 1, kv_cache[2][b, :, cols].rearrange("(l r) n -> l r n", r=16)[:, 0, :]),
                        (slice(80, 83), 1, qkv_dram[:, 1 + s, b, :]))

            for b in range(NS):
                if b >= 2:
                    sp.wait_ge(b_scored, b - 1)
                for part, tl, src in cache_rows(b, 0):
                    sp.dma_start(bK[part, b % 2, tl, :], src).then_inc(b_loaded[b % 2], 16)
                for part, tl, g in ((slice(0, P), 0, 0), (slice(0, 64), 1, 1), (slice(64, 80), 1, 2)):
                    n = part.stop - part.start
                    sp.dma_start(bQ[part, b % 2, tl, :], qkv_dram[g, 0, b, :].partition_broadcast(n)).then_inc(b_loaded[b % 2], 16)
                sp.dma_start(bQ[80:83, b % 2, 1, :], qkv_dram[:, 0, b, :]).then_inc(b_loaded[b % 2], 16)
                for part, tl, src in cache_rows(b, 1):
                    sp.dma_start(bV[part, b, tl, :], src).then_inc(bv_loaded, 16)

            for g in range(G):
                n = kv_p[g].shape[0]
                for s in range(2):
                    sp.dma_start(kv_p[g][:, s, :], qkv_dram[g, 1 + s, T - n:T, :]).then_inc(copied, 16)
                    sp.dma_start(kv_s[g][:, kv_s[g].shape[1] - 1, s * AW:(s + 1) * AW], qkv_dram[g, 1 + s, 0:NS, :]).then_inc(copied, 16)

            sp.wait_ge(job_done, J_R1)
            sp.dma_start(cosR[:, :], c["cosR"]).then_inc(table_loaded, 16)
            sp.dma_start(sinR[:, :], c["sinR"]).then_inc(table_loaded, 16)
            with sp.Fori(0, RH) as h:
                n = 0
                for dst in (q_dram, k_dram):
                    for t in range(TG):
                        sp.wait_ge(rrope_done, h * (2 * TG) + (n + 2))
                        sp.sem_inc(sp_gate, 1)
                        sp.dma_start(dst[bass.ds(h, 1), :, :, tok(t)].rearrange("a p f t -> (a p) f t"),
                                     rw[:, n % 4, :].rearrange("p (f t) -> p f t", f=2)).then_inc(rstored[n % 4], 16)
                        n += 1
                for u in range(2):
                    for m in range(MT):
                        rows = NS if m == 0 else P
                        jj = 12 + u * MT + m
                        sp.wait_ge(drained[jj % NB], drain(J_R1 + jj, h, R1_J))
                        sp.sem_inc(sp_gate, 1)
                        sp.dma_start(v_dram[bass.ds(h, 1), tile_columns(m):tile_columns(m) + rows,
                                            u * HC:(u + 1) * HC].rearrange("a t n -> (a t) n"),
                                     rw[0:rows, n % 4, 0:HC]).then_inc(rstored[n % 4], 16)
                        n += 1
                for u in range(2):
                    for t in range(TG):
                        for f in range(2):
                            jj = 12 + 2 * MT + u * 6 + t * 2 + f
                            sp.wait_ge(drained[jj % NB], drain(J_R1 + jj, h, R1_J))
                            sp.sem_inc(sp_gate, 1)
                            sp.dma_start(g_dram[bass.ds(h, 1), :, 2 * u + f, tok(t)].rearrange("a p t -> (a p) t"),
                                         rw[:, n % 4, 0:TS]).then_inc(rstored[n % 4], 16)
                            n += 1
            for b in range(4):
                sp.wait_ge(rstored[b], 16 * (RH * 36 // 4 + 1))

            sp.wait_ge(job_done, J_RO)
            sp.dma_start(eye8[:, :, :], c["eye8"]).then_inc(table_loaded, 16)
            with sp.Fori(0, RH) as h:
                head = bass.ds(h, 1)

                def chunk_load(ch):
                    k = ch % RS
                    cols = slice(NS + ch * P, NS + (ch + 1) * P)
                    sp.wait_ge(y_lo, h * 8 + (ch + 1))
                    sp.sem_inc(sp_gate, 1)
                    sp.dma_start(rqT[:, k, :, :], q_dram[head, :, :, cols].rearrange("a p f t -> (a p) f t")).then_inc(r_loaded[k], 16)
                    sp.dma_start(rkT[:, k, :, :], k_dram[head, :, :, cols].rearrange("a p f t -> (a p) f t")).then_inc(r_loaded[k], 16)
                    sp.dma_start(rv[:, k, :], v_dram[head, cols, :].rearrange("a t n -> (a t) n")).then_inc(r_loaded[k], 16)
                    sp.dma_start(rg[:, k, :, :], g_dram[head, :, :, cols].rearrange("a p f t -> (a p) f t")).then_inc(r_loaded[k], 16)

                def z_load(b):
                    k = b % RS
                    sp.wait_ge(z_stored[k], h * (16 * NS // RS) + 16 * (b // RS + 1))
                    sp.wait_ge(z_read, h * NS + (b + 1))
                    sp.sem_inc(sp_gate, 1)
                    sp.dma_start(zS[:, k, :, :], state_in[b, head, :, :].rearrange("a (f p) n -> (a p) f n", p=P))\
                        .then_inc(z_loaded[k], 16)
                    sp.dma_start(zV[:, k, :], v_dram[head, b:b + 1, :].rearrange("a t n -> (a t n)").partition_broadcast(P))\
                        .then_inc(z_loaded[k], 16)

                for n in range(RS):
                    chunk_load(n)
                    z_load(n)
                sp.wait_ge(zy_lo, h + 1)
                sp.sem_inc(sp_gate, 1)
                sp.dma_start(dmask[:, :], c["dmask"][head, :, :].rearrange("a p t -> (a p) t")).then_inc(head_loaded, 16)
                sp.dma_start(qdec[:, :], c["qdec"][head, :, :].rearrange("a p t -> (a p) t")).then_inc(head_loaded, 16)
                sp.dma_start(decay[:, :], c["decay"][head, :, :].rearrange("a p t -> (a p) t")).then_inc(head_loaded, 16)
                sp.dma_start(ron[:, :], c["ron"][head, :, :].rearrange("a p t -> (a p) t")).then_inc(head_loaded, 16)
                sp.dma_start(zq[:, 0, :, :], q_dram[head, :, :, 0:NS].rearrange("a p f t -> (a p) f t")).then_inc(zqg_loaded, 16)
                sp.dma_start(zq[:, 1, :, :], k_dram[head, :, :, 0:NS].rearrange("a p f t -> (a p) f t")).then_inc(zqg_loaded, 16)
                sp.dma_start(zg[:, :, :], g_dram[head, :, :, 0:NS].rearrange("a p f t -> (a p) f t")).then_inc(zqg_loaded, 16)
                for b in range(NS):
                    sp.wait_ge(z_new, h * (2 * NS) + (2 * b + 2))
                    sp.sem_inc(sp_gate, 1)
                    sp.dma_start(ret_s[b, head, :, :].rearrange("a (f p) n -> (a p) f n", p=P), zS[:, b % RS, :, :])\
                        .then_inc(z_stored[b % RS], 16)
                    if b + RS < NS:
                        chunk_load(b + RS)
                        z_load(b + RS)
                sp.wait_ge(st_ready, h * 16 + 16)
                sp.sem_inc(sp_gate, 1)
                sp.dma_start(ret_p[head, :, :].rearrange("a (f p) n -> (a p) f n", p=P), state[:, :, :]).then_inc(state_stored, 16)

            last = J_FFN1 + FG * FFN_J
            for jj in range(last - NB, last):
                sp.wait_ge(drained[jj % NB], drain(jj))
            sp.dma_start(y, xT[:, :, :]).then_inc(y_stored, 16)
            sp.wait_ge(y_stored, 16)
            sp.wait_ge(copied, 16 * (G + 4 * G))
            sp.wait_ge(state_stored, 16 * (RH + 1))
            for k in range(RS):
                sp.wait_ge(z_stored[k], 16 * (RH * NS // RS + 1))

        @block.scalar
        def _(act):
            def cut_hi(u, jobs, i=0, per_u=0, per_j=0):
                s = u % SLOTS
                act.wait_ge(raw_loaded[s], i * (16 * (per_u // SLOTS)) + 16 * (u // SLOTS + 1))
                if jobs:
                    act.wait_ge(job_done, i * per_j + jobs)
                act.activation(wH[:, s, :], raw[:, s, :], ACT.Copy).then_inc(hi_ready[s], 1)

            def norm(n):
                def squares(t):
                    norm_x_wait(act, n, t)
                    for k in range(KC):
                        a = (n * TG + t) * KC + k
                        if a >= 4:
                            act.wait_ge(sq_used, a - 3)
                        act.activation(sq[:, a % 4, :], xT[:, k, tok(t)], ACT.Square).then_inc(sq_ready, 1)

                def root(t):
                    b = 6 + (n * TG + t) % 2
                    act.wait_ge(sum_done, n * TG + t + 1)
                    act.activation(rt[:, t, :], ps[:, b, 0:TS], ACT.Sqrt, bias=epsb, scale=1.0 / D).then_inc(root_ready, 1)

                squares(0)
                squares(1)
                root(0)
                squares(2)
                root(1)
                root(2)
                for t in range(TG):
                    for k in range(KC):
                        a = (n * TG + t) * KC + k
                        act.wait_ge(normed, a + 1)
                        act.activation(hH[:, k, tok(t)], un[:, a % 4, :], ACT.Copy).then_inc(h_hi, 1)

            act.wait_ge(const_loaded, 96)
            cut_hi(0, 0)
            cut_hi(1, 0)
            norm(0)

            with act.Fori(0, G) as g:
                for u in range(6):
                    if u == 0:
                        act.wait_ge(drained[NB - 1], free(NB - 1, g, QKV_J))
                    cut_hi(U_QKV + u + 2, u * MT, g, 6, QKV_J)
                    for m in range(MT):
                        jj = u * MT + m
                        b = jj % NB
                        act.wait_ge(job_done, g * QKV_J + (jj + 1))
                        if u < 4:
                            k = jj % 2
                            bank = ps[:, b, 0:HC].rearrange("p (h d) -> p h d", h=4)
                            for h in range(4):
                                act.activation(junk[:, k, h * DH:(h + 1) * DH], bank[:, h, :], ACT.Square,
                                               accum_out=ss[:, k, h:h + 1]).then_inc(head_sq, 1)
                            act.wait_ge(head_sq, g * (16 * MT) + 4 * (jj + 1))
                            if jj >= 2:
                                act.wait_ge(rope_done, g * (4 * MT) + (jj - 1))
                            if u < 2:
                                act.activation(rq[:, k, :], ss[:, k, :], ACT.Sqrt, bias=eps64, scale=1.0).then_inc(root_q, 1)
                            else:
                                act.activation(rq[:, k, :], ss[:, k, :], ACT.Sqrt, bias=epsb, scale=1.0 / DH).then_inc(root_q, 1)
                        else:
                            act.wait_ge(stored[b], g * (16 * (QKV_J // NB)) + 16 * (jj // NB + 1))
                            act.activation(ot[:, b, :], ps[:, b, 0:HC], ACT.Copy).then_inc(drained[b], 1)

            def queries(f, i):
                act.wait_ge(q_turned, i * 2 + (f + 1))
                for par in range(2):
                    half = slice(par * DH, (par + 1) * DH)
                    act.activation(aq[half, 4 * par:4 * par + 4, :], ps[half, 0, :].rearrange("p (c t) -> p c t", c=4), ACT.Copy)\
                        .then_inc(aq_ready, 1)

            def exps(f, i):
                act.wait_ge(m_ready, i * 2 + (f + 1))
                for x in range(H):
                    w_ = sc[:, f % 2, x, (0 if AT_PREV[f] else P):2 * P]
                    act.activation(w_, w_, ACT.Exp, bias=al[:, f % 2, x, DH:DH + 1],
                                   accum_out=al[:, f % 2, x, DH + 1:DH + 2]).then_inc(p_ready, 1)

            def at_step(a, i):
                if a + 1 < AU:
                    queries(a + 1, i)
                for q in (1, 3):
                    act.wait_ge(p_turned, i * 8 + (4 * a + q + 1))
                    src = ps[:, 7, :].rearrange("p (x h t) -> p x h t", x=2, h=2)
                    if AT_PREV[a]:
                        act.activation(pt[:, 2 * q:2 * q + 2, :, :], src, ACT.Copy).then_inc(pt_ready2, 1)
                    else:
                        act.activation(pt[:, 2 * q:2 * q + 2, 1, :], src[:, :, 1, :], ACT.Copy).then_inc(pt_ready2, 1)
                if a + 1 < AU:
                    exps(a + 1, i)

            act.wait_ge(table_loaded, 32)
            act.wait_ge(aq_zeroed, 1)
            queries(0, 0)
            exps(0, 0)
            for first, n, turns in AT_RUNS:
                if turns == 1:
                    for a in range(first, first + n):
                        at_step(a, 0)
                else:
                    with act.Fori(0, turns) as i:
                        for a in range(first, first + n):
                            at_step(a, i)
            for m in range(NP // P):
                act.wait_ge(c_step, 7 * m + 3)
                act.activation(cw[:, m % 2, :, :], cw[:, m % 2, :, :], ACT.Exp).then_inc(cw_exp, 1)
                act.wait_ge(co_turned, m + 1)
                act.activation(oH[:, :, NS + m * P:NS + (m + 1) * P], ps[:, m % 2, :].rearrange("p (c t) -> p c t", c=4),
                               ACT.Copy).then_inc(o_hi, 1)
            act.wait_ge(b_step, 2)
            act.activation(bP[:, 0:211], bP[:, 0:211], ACT.Exp, bias=bl[:, 0:1], accum_out=bl[:, 1:2]).then_inc(b_exp, 1)
            act.wait_ge(b_out, 1)
            act.activation(oH[:, :, 0:NS], ps[:, 3, 0:4 * NS].rearrange("p (c t) -> p c t", c=4), ACT.Copy).then_inc(b_oh, 1)

            for u in range(3):
                cut_hi(U_WO + u + 2, J_WO + (0, 9, 18)[u])
            norm(1)

            def ffn_turn(i, j0, u0, last=False):
                cut_hi(u0 + 2, j0, i, 3, FFN_J)
                for p in range(6):
                    jg, ju = j0 + 2 * p, j0 + 2 * p + 1
                    act.wait_ge(job_done, i * FFN_J + (jg + 1))
                    act.wait_ge(drained[ju % NB], free(ju, i, FFN_J))
                    act.activation(gs[:, p % 3, :], ps[:, jg % NB, 0:TS], ACT.Silu).then_inc(drained[jg % NB], 1)
                if not last:
                    cut_hi(u0 + 3, j0 + 12, i, 3, FFN_J)
                    cut_hi(u0 + 4, j0 + 12, i, 3, FFN_J)

            with act.Fori(0, FG) as i:
                ffn_turn(i, J_FFN0, U_FFN0)
            norm(2)

            act.wait_ge(const_loaded, 96)
            with act.Fori(0, RH) as h:
                def unit_cut(u):
                    cut_hi(U_R1 + u + 2, J_R1 + (0, 6, 12, 12 + MT, 12 + 2 * MT, 18 + 2 * MT)[u], h, 6, R1_J)
                unit_cut(0)
                unit_cut(1)
                n = 6
                for u in range(2):
                    unit_cut(2 + u)
                    for m in range(MT):
                        jj = 12 + u * MT + m
                        act.wait_ge(job_done, h * R1_J + (J_R1 + jj + 1))
                        act.wait_ge(rstored[n % 4], h * (16 * 9) + 16 * (n // 4 + 1))
                        act.activation(rw[:, n % 4, 0:HC], ps[:, jj % NB, 0:HC], ACT.Copy).then_inc(drained[jj % NB], 1)
                        n += 1
                for u in range(2):
                    unit_cut(4 + u)
                    for q in range(6):
                        jj = 12 + 2 * MT + u * 6 + q
                        act.wait_ge(job_done, h * R1_J + (J_R1 + jj + 1))
                        act.wait_ge(rstored[n % 4], h * (16 * 9) + 16 * (n // 4 + 1))
                        act.activation(rw[:, n % 4, 0:TS], ps[:, jj % NB, 0:TS], ACT.Silu).then_inc(drained[jj % NB], 1)
                        n += 1

            act.wait_ge(table_loaded, 16 * 8)
            with act.Fori(0, RH) as h:
                act.wait_ge(head_loaded, h * 64 + 64)

                def y_cut(ch):
                    act.wait_ge(y_ready, h * 8 + (ch + 1))
                    act.activation(yH[:, :, NS + ch * P:NS + (ch + 1) * P], ry[:, ch % 2, :, :], ACT.Copy).then_inc(y_hi, 1)

                for ch in range(8):
                    k = ch % 2
                    act.wait_ge(k_up, h * 8 + (ch + 1))
                    if ch >= 2:
                        act.wait_ge(up_done, h * 8 + (ch - 1))
                    act.activation(kd[:, k, :, :], ps[:, 0, 0:2 * P].rearrange("p (f d) -> p f d", f=2), ACT.Copy,
                                   scale=kdec).then_inc(kd_ready, 1)
                    act.wait_ge(z_loaded[ch % RS], h * (32 * NS // RS) + 32 * (ch // RS + 1))
                    act.activation(zS[:, ch % RS, :, :], zS[:, ch % RS, :, :], ACT.Copy, scale=g1).then_inc(z_scaled, 1)
                    if ch:
                        y_cut(ch - 1)
                    act.wait_ge(ro_done, h * 8 + (ch + 1))
                    act.activation(rsq[:, :, :], ps[:, 4 + k, :].rearrange("p (e t) -> p e t", e=4), ACT.Square).then_inc(rsq_ready, 1)
                    act.wait_ge(rsum_done, h * 8 + (ch + 1))
                    act.activation(rr[:, k, :], ps[:, 6, 0:P], ACT.Sqrt, bias=epsb, scale=1.0 / RV).then_inc(rroot_ready, 1)
                y_cut(7)
                act.wait_ge(z_read, h * NS + (NS + RS))
                act.activation(zo[:, :], ps[0:NS, 7, :], ACT.Square, accum_out=zl[:, 0:1]).then_inc(zl_step, 1)
                act.wait_ge(zl_step, h * 2 + 1)
                act.activation(zl[:, 1:2], zl[:, 0:1], ACT.Sqrt, bias=epsb[0:NS], scale=1.0 / RV).then_inc(zl_step, 1)
                act.wait_ge(zr_ready, h + 1)
                act.activation(zo[:, :], ps[0:NS, 7, :], ACT.Copy, scale=zl[:, 2:3]).then_inc(zo_ready, 1)
                act.wait_ge(zy_step, h * 5 + 5)
                act.activation(yH[:, :, 0:NS], zy[:, 1, :, :], ACT.Copy).then_inc(zy_hi, 1)
                for u in range(3):
                    cut_hi(U_RO + u + 2, J_RO + (0, 9, 18)[u], h, 3, RO_J)
            for k in range(RS):
                act.wait_ge(z_stored[k], 16 * (RH * NS // RS + 1))
            act.wait_ge(state_stored, 16 * (RH + 1))
            norm(3)
            with act.Fori(0, FG - 1) as i:
                ffn_turn(i, J_FFN1, U_FFN1)
            ffn_turn(FG - 1, J_FFN1, U_FFN1, last=True)

        @block.tensor
        def _(pe):
            def norm(n):
                for t in range(TG):
                    b = 6 + (n * TG + t) % 2
                    if n * TG + t >= 2:
                        pe.wait_ge(root_ready, n * TG + t - 1)
                    for k in range(KC):
                        pe.wait_ge(sq_ready, (n * TG + t) * KC + k + 1)
                        mm = pe.matmul(ps[:, b, 0:TS], ones[:, :], sq[:, ((n * TG + t) * KC + k) % 4, :],
                                       start=(k == 0), stop=(k == KC - 1))
                        mm.then_inc(sq_used, 1)
                    pe.wait_ge(sq_used, (n * TG + t + 1) * KC)
                    pe.sem_inc(sum_done, 1)

            def bank_free(j, i=0, per=0):
                pe.wait_ge(drained[j % NB], free(j, i, per))
                return j % NB

            def passes(out, lhs, rhs):
                n = len(lhs)
                for k in range(n):
                    for q, (a, b) in enumerate(((0, 0), (0, 1), (1, 0))):
                        mm = pe.matmul(out, lhs[k][a], rhs[k][b], start=(k == 0 and q == 0), stop=(k == n - 1 and q == 2))
                return mm

            def unit_ready(u, i=0, per=0):
                pe.wait_ge(lo_ready[u % SLOTS], hi_ready_at(u, i, per))
                return u % SLOTS

            def tokens_stationary(s, m, b):
                c0 = tile_columns(m)
                wv = [[x_[:, s, :].rearrange("p (k n) -> p k n", k=KC)[:, k, :] for x_ in (wH, wL)] for k in range(KC)]
                return passes(ps[:, b, 0:HC], [[x_[:, k, c0:c0 + P] for x_ in (hH, hL)] for k in range(KC)], wv)

            def tokens_moving(s, f, t, b):
                wv = [[x_[:, s, :].rearrange("p (k n) -> p k n", k=KC)[:, k, f * P:(f + 1) * P] for x_ in (wH, wL)] for k in range(KC)]
                return passes(ps[:, b, 0:TS], wv, [[x_[:, k, tok(t)] for x_ in (hH, hL)] for k in range(KC)])

            def out_projection(u0, j0, oh, ol, i=0, per_u=0, per_j=0):
                j = j0
                for a, tiles in enumerate(OUT_TILES):
                    s = unit_ready(u0 + a, i, per_u)
                    for dl in range(len(tiles)):
                        for t in range(TG):
                            b = bank_free(j, i, per_j)
                            wv = [[x_[:, s, (dl * 4 + k) * P:(dl * 4 + k + 1) * P] for x_ in (wH, wL)] for k in range(4)]
                            passes(ps[:, b, 0:TS], wv, [[x_[:, k, tok(t)] for x_ in (oh, ol)] for k in range(4)])\
                                .then_inc(job_done, 1)
                            j += 1

            pe.wait_ge(ones_set, 1)
            norm(0)
            with pe.Fori(0, G) as g:
                for u in range(6):
                    s = unit_ready(u, g, 6)
                    for m in range(MT):
                        if u == 0:
                            pe.wait_ge(h_lo, ((tile_columns(m) + P - 1) // TS + 1) * KC)
                        b = bank_free(u * MT + m, g, QKV_J)
                        tokens_stationary(s, m, b).then_inc(job_done, 1)

            def turn(f, i):
                k = f % 2
                pe.wait_ge(aqk_loaded[k], i * (32 * AT_PIECES[f]) + 32 * sum(AT_PIECES[k:f + 1:2]))
                if f:
                    pe.wait_ge(ak_ready, i * 2 + f)
                for p in range(4):
                    mm = pe.transpose(ps[:, 1, p * P:(p + 1) * P], qkv[:, k, 1, p * P:(p + 1) * P], ident[:, :])
                mm.then_inc(k_turned, 1)
                if f >= 2:
                    pe.wait_ge(acc_ready, i * 2 + (f - 1))
                if f == 1:
                    pe.wait_ge(aq_ready, 2)
                for p in range(4):
                    mm = pe.transpose(ps[:, 0, p * P:(p + 1) * P], qkv[:, k, 0, p * P:(p + 1) * P], ident[:, :])
                mm.then_inc(q_turned, 1)

            def scores(f, i):
                pe.wait_ge(aq_ready, i * 4 + (2 * f + 2))
                pe.wait_ge(ak_ready, i * 2 + (f + 1))
                if f:
                    pe.wait_ge(s_masked, i * 8 + 4 * f)
                for x in range(H):
                    for hf in ((0, 1) if AT_PREV[f] else (1,)):
                        mm = pe.matmul(ps[:, 2 + x // 2, (x % 2) * 256 + hf * P:(x % 2) * 256 + (hf + 1) * P],
                                       aq[:, x, :], ak[:, (f + 1 + hf) % 2, x % 4, :], start=True, stop=True)
                    if x in (3, 7):
                        mm.then_inc(s_done, 1)

            def turn_p(a, i, q):
                pe.wait_ge(p_ready, i * 16 + (8 * a + 2 * q + 2))
                if a or q >= 2:
                    pe.wait_ge((pt_ready, pt_ready2)[q % 2], i * 4 + (2 * a + q // 2))
                for x in (2 * q, 2 * q + 1):
                    for hf in ((0, 1) if AT_PREV[a] else (1,)):
                        mm = pe.transpose(ps[:, 6 + q % 2, (x % 2) * 256 + hf * P:(x % 2) * 256 + (hf + 1) * P],
                                          sc[:, a % 2, x, hf * P:(hf + 1) * P], ident[:, :])
                mm.then_inc(p_turned, 1)

            def values(a, i):
                k = a % 2
                halves = (0, 1) if AT_PREV[a] else (1,)
                pe.wait_ge(av_loaded[k], i * (16 * AT_PIECES[a]) + 16 * sum(AT_PIECES[k:a + 1:2]))
                for q in range(4):
                    pe.wait_ge((pt_ready, pt_ready2)[q % 2], i * 4 + (2 * a + q // 2 + 1))
                    for x in (2 * q, 2 * q + 1):
                        hd = 2 * (x % 4) + x // 4
                        for hf in halves:
                            mm = pe.matmul(ps[:, 0, x * DH:(x + 1) * DH], pt[:, x, hf, :],
                                           qkv[:, (k + 1 + hf) % 2, 2, hd * DH:(hd + 1) * DH],
                                           start=(hf == halves[0]), stop=(hf == 1))
                mm.then_inc(pv_done, 1)

            def at_step(a, i):
                if a + 1 < AU:
                    turn(a + 1, i)
                turn_p(a, i, 0)
                turn_p(a, i, 1)
                if a + 1 < AU:
                    scores(a + 1, i)
                turn_p(a, i, 2)
                turn_p(a, i, 3)
                values(a, i)

            for b in range(NB):
                pe.wait_ge(drained[b], drain(J_WO - NB + b))
            turn(0, 0)
            scores(0, 0)
            for first, n, turns in AT_RUNS:
                if turns == 1:
                    for a in range(first, first + n):
                        at_step(a, 0)
                else:
                    with pe.Fori(0, turns) as i:
                        for a in range(first, first + n):
                            at_step(a, i)
            for m in range(NP // P):
                pe.wait_ge(co_ready, m + 1)
                if m >= 2:
                    pe.wait_ge(o_lo, m - 1)
                for p in range(4):
                    mm = pe.transpose(ps[:, m % 2, p * P:(p + 1) * P], cp[:, 0, p * P:(p + 1) * P], ident[:, :])
                mm.then_inc(co_turned, 1)

            pe.wait_ge(b_scored, NS)
            pe.wait_ge(o_lo, NP // P)
            pe.transpose(ps[0:64, 0, 0:P], bS[:, 0, :], ident[:, :])
            pe.transpose(ps[0:64, 0, P:P + 83], bS[0:83, 1, :], ident[0:83, 0:83]).then_inc(b_turned, 1)
            pe.wait_ge(b_exp, 1)
            pe.transpose(ps[:, 1, 0:64], bP[:, 0:P], ident[0:64, 0:64])
            pe.transpose(ps[0:83, 1, 64:128], bP[:, P:P + 83], ident[0:64, 0:64]).then_inc(b_pturned, 1)
            pe.wait_ge(b_masked, 2)
            pe.wait_ge(bv_loaded, 16 * 4 * NS)
            for b in range(NS):
                pe.matmul(ps[0:64, 2, :], bT[:, 0, b, :], bV[:, b, 0, :], start=(b == 0), stop=False)
                mm = pe.matmul(ps[0:64, 2, :], bT[0:83, 1, b, :], bV[0:83, b, 1, :], start=False, stop=(b == NS - 1))
            mm.then_inc(b_pv, 1)
            pe.wait_ge(b_diag, 1)
            for p in range(4):
                mm = pe.matmul(ps[:, 3, p * NS:(p + 1) * NS], bA[:, p * P:(p + 1) * P], bE[:, :], start=True, stop=True)
            mm.then_inc(b_out, 1)

            pe.wait_ge(b_ol, 1)
            out_projection(U_WO, J_WO, oH, oL)
            norm(1)

            def ffn_turn(i, j0, u0):
                s0, s1 = unit_ready(u0, i, 3), unit_ready(u0 + 1, i, 3)
                j = j0
                for t in range(TG):
                    pe.wait_ge(h_lo, ((2 if j0 == J_FFN0 else 4) * TG - (TG - 1 - t)) * KC)
                    for f in range(2):
                        for s in (s0, s1):
                            tokens_moving(s, f, t, bank_free(j, i, FFN_J)).then_inc(job_done, 1)
                            j += 1
                s = unit_ready(u0 + 2, i, 3)
                for t in range(TG):
                    pe.wait_ge(hid_ready, i * 6 + (6 * FG * (j0 == J_FFN1) + 2 * t + 2))
                    for d in range(KC):
                        b = bank_free(j, i, FFN_J)
                        wv = [[x_[:, s, k * D + d * P:k * D + (d + 1) * P] for x_ in (wH, wL)] for k in range(2)]
                        passes(ps[:, b, 0:TS], wv, [[x_[:, k, tok(t)] for x_ in (hidH, hidL)] for k in range(2)])\
                            .then_inc(job_done, 1)
                        j += 1

            with pe.Fori(0, FG) as i:
                ffn_turn(i, J_FFN0, U_FFN0)
            norm(2)
            with pe.Fori(0, RH) as h:
                jj = 0
                for u in range(6):
                    s = unit_ready(U_R1 + u, h, 6)
                    if u in (2, 3):
                        for m in range(MT):
                            tokens_stationary(s, m, bank_free(J_R1 + jj, h, R1_J)).then_inc(job_done, 1)
                            jj += 1
                    else:
                        for t in range(TG):
                            if u == 0:
                                pe.wait_ge(h_lo, (3 * TG - (TG - 1 - t)) * KC)
                            for f in range(2):
                                tokens_moving(s, f, t, bank_free(J_R1 + jj, h, R1_J)).then_inc(job_done, 1)
                                jj += 1

            pe.wait_ge(table_loaded, 16 * 8)
            with pe.Fori(0, RH) as h:
                for q in range(NB):
                    pe.wait_ge(drained[q], free(J_RO + q, h, RO_J))

                def keys(ch):
                    k = ch % RS
                    pe.wait_ge(r_loaded[k], h * (64 * 8 // RS) + 64 * (ch // RS + 1))
                    pe.wait_ge(kd_ready, h * 8 + (ch + 1))
                    for f in range(2):
                        mm = pe.transpose(ps[:, 0, f * P:(f + 1) * P], rkT[:, k, f, :], ident[:, :])
                    mm.then_inc(k_up, 1)
                    pe.wait_ge(sT_ready, h * 8 + (ch + 1))
                    for f in range(2):
                        mm = pe.matmul(ps[:, 1, 0:P], rkT[:, k, f, :], rqT[:, k, f, :], start=(f == 0), stop=(f == 1))
                    mm.then_inc(rs_done, 1)

                keys(0)
                for ch in range(8):
                    k = ch % 2
                    pe.wait_ge(sT_ready, h * 8 + (ch + 2))
                    pe.wait_ge(qd_ready, h * 8 + (ch + 1))
                    if ch >= 2:
                        pe.wait_ge(y_ready, h * 8 + (ch - 1))
                    if ch:
                        pe.wait_ge(st_ready, h * 16 + 2 * ch)
                    for e in range(4):
                        out = ps[:, 4 + k, e * P:(e + 1) * P]
                        mm = pe.matmul(out, rv[:, ch % RS, e * P:(e + 1) * P], sT[:, k, :], start=True, stop=(ch == 0))
                        if ch:
                            for f in range(2):
                                mm = pe.matmul(out, state[:, f, e * P:(e + 1) * P], qd[:, k, f, :], start=False, stop=(f == 1))
                    mm.then_inc(ro_done, 1)
                    if ch < 7:
                        keys(ch + 1)
                    pe.wait_ge(kd_ready, h * 8 + (ch + 2))
                    if ch:
                        pe.wait_ge(st_ready, h * 16 + 2 * ch)
                    for f in range(2):
                        mm = pe.matmul(ps[:, 2 + f, :], kd[:, k, f, :], rv[:, ch % RS, :], start=True, stop=True)
                    mm.then_inc(up_done, 1)
                    if ch == 0:
                        pe.wait_ge(zm_ready, h + 1)
                        pe.wait_ge(zo_ready, h + 1)
                    pe.wait_ge(z_new, h * (2 * NS) + (2 * ch + 2))
                    for f in range(2):
                        mm = pe.matmul(ps[0:NS, 7, :], zm[:, f, ch, :], zS[:, ch % RS, f, :],
                                       start=(ch == 0 and f == 0), stop=(ch == NS - 1 and f == 1))
                    mm.then_inc(z_read, 1)
                    pe.wait_ge(rsq_ready, h * 8 + (ch + 1))
                    if ch:
                        pe.wait_ge(rroot_ready, h * 8 + ch)
                    for e in range(4):
                        mm = pe.matmul(ps[:, 6, 0:P], ones[:, :], rsq[:, e, :], start=(e == 0), stop=(e == 3))
                    mm.then_inc(rsum_done, 1)
                pe.wait_ge(zo_ready, h + 2)
                pe.wait_ge(y_ready, h * 8 + 8)
                pe.sem_inc(pe_gate, 1)
                for e in range(4):
                    mm = pe.transpose(ps[:, 6, e * NS:(e + 1) * NS], zo[:, e * P:(e + 1) * P], ident[0:NS, 0:NS])
                mm.then_inc(zo_turned, 1)
                pe.wait_ge(zy_lo, h + 2)
                pe.wait_ge(y_lo, h * 8 + (8 + RS))
                pe.wait_ge(st_ready, h * 16 + 16)
                out_projection(U_RO, J_RO, yH, yL, h, 3, RO_J)
            norm(3)
            with pe.Fori(0, FG) as i:
                ffn_turn(i, J_FFN1, U_FFN1)

        @block.vector
        def _(dve):
            tt, ts, stt = dve.tensor_tensor, dve.tensor_scalar, dve.scalar_tensor_tensor

            def cut_lo(u, i=0, per_u=0):
                s = u % SLOTS
                dve.wait_ge(hi_ready[s], hi_ready_at(u, i, per_u))
                tt(wL[:, s, :], raw[:, s, :], wH[:, s, :], ALU.subtract).then_inc(lo_ready[s], 1)

            def norm(n):
                def low(a):
                    k, t = a % KC, a // KC % TG
                    dve.wait_ge(h_hi, a + 1)
                    tt(hL[:, k, tok(t)], un[:, a % 4, :], hH[:, k, tok(t)], ALU.subtract).then_inc(h_lo, 1)
                for t in range(TG):
                    dve.wait_ge(root_ready, n * TG + t + 1)
                    dve.reciprocal(rt[:, t, :], rt[:, t, :]).then_inc(recip_ready, 1)
                    dve.wait_ge(recip_ready, n * TG + t + 1)
                    for k in range(KC):
                        a = (n * TG + t) * KC + k
                        if a >= 4:
                            dve.wait_ge(h_lo, a - 3)
                        stt(out=un[:, a % 4, :], in0=xT[:, k, tok(t)], scalar=gains[:, n, k:k + 1], in1=rt[:, t, :],
                            op0=ALU.mult, op1=ALU.mult).then_inc(normed, 1)
                        if a - n * TG * KC >= 2:
                            low(a - 2)
                low((n + 1) * TG * KC - 2)
                low((n + 1) * TG * KC - 1)

            dve.memset(ones[:, :], 1.0).then_inc(ones_set, 1)
            for b in range(NB):
                dve.sem_inc(drained[b], 1)
                dve.sem_inc(stored[b], 16)
            for b in range(4):
                dve.sem_inc(rstored[b], 16)
            for b in range(RS):
                dve.sem_inc(z_stored[b], 16)
            for s_, n_ in ((acc_stored[0], 16), (acc_stored[1], 16), (y_lo, RS), (zy_lo, 1), (z_read, RS), (kd_ready, 1), (sT_ready, 1), (rrope_done, 1), (zo_ready, 1), (state_stored, 16)):
                dve.sem_inc(s_, n_)
            dve.wait_ge(const_loaded, 96)
            cut_lo(0)
            cut_lo(1)
            dve.wait_ge(x_loaded, 16)
            norm(0)

            with dve.Fori(0, G) as g:
                for u in range(6):
                    cut_lo(u + 2, g, 6)
                    if u >= 4:
                        continue
                    for m in range(MT):
                        jj = u * MT + m
                        b, k = jj % NB, jj % 2
                        steps = g * (7 * 4 * MT) + 7 * jj
                        bank = ps[:, b, 0:HC].rearrange("p (h d) -> p h d", h=4)
                        dve.wait_ge(root_q, g * (4 * MT) + (jj + 1))
                        dve.reciprocal(ri[:, k, :], rq[:, k, :]).then_inc(rope_step, 1)
                        dve.wait_ge(rope_step, steps + 1)
                        for h in range(4):
                            mm = stt(out=qn[:, h, :], in0=bank[:, h, :], scalar=ri[:, k, h:h + 1],
                                     in1=qkg[:, bass.ds(g * 2 + u // 2, 1), :].rearrange("p a d -> p (a d)"),
                                     op0=ALU.mult, op1=ALU.mult)
                            mm.then_inc(*((rope_step, 1) if h < 3 else (drained[b], 1)))
                        dve.wait_ge(rope_step, steps + 4)
                        dve.wait_ge(drained[b], drain(jj, g, QKV_J))
                        tt(qc[:, :, :], qn[:, :, :], ropeC[:, m:m + 1, :].broadcast_to([P, 4, DH]), ALU.mult).then_inc(rope_step, 1)
                        for a in range(2):
                            tt(qs[:, :, a * 32:(a + 1) * 32], qn[:, :, (1 - a) * 32:(2 - a) * 32],
                               ropeS[:, m:m + 1, a * 32:(a + 1) * 32].broadcast_to([P, 4, 32]), ALU.mult).then_inc(rope_step, 1)
                        dve.wait_ge(rope_step, steps + 7)
                        dve.wait_ge(stored[b], g * (16 * (QKV_J // NB)) + 16 * (jj // NB + 1))
                        tt(ot[:, b, :].rearrange("p (h d) -> p h d", h=4), qc[:, :, :], qs[:, :, :], ALU.add).then_inc(rope_done, 1)

            def keys(f, i):
                dve.wait_ge(k_turned, i * 2 + (f + 1))
                dve.tensor_copy(ak[:, f % 2, :, :], ps[:, 1, :].rearrange("p (c t) -> p c t", c=4)).then_inc(ak_ready, 1)

            def masked(f, i):
                w0 = 0 if AT_PREV[f] else P
                mask = maskD[:, :] if f >= 16 else maskP[:, w0:2 * P]
                for q in range(4):
                    if q % 2 == 0:
                        dve.wait_ge(s_done, i * 4 + (2 * f + q // 2 + 1))
                    tt(sc[:, f % 2, 2 * q:2 * q + 2, w0:2 * P], ps[:, 2 + q, :].rearrange("p (x w) -> p x w", x=2)[:, :, w0:2 * P],
                       mask.rearrange("p (x w) -> p x w", x=1).broadcast_to([P, 2, 2 * P - w0]), ALU.add).then_inc(s_masked, 1)

            def maxima(f, i):
                k = f % 2
                dve.wait_ge(acc_stored[k], i * (16 * AT_PIECES[f]) + (16 + 16 * sum(AT_PIECES[k:f:2])))
                dve.wait_ge(s_masked, i * 8 + (4 * f + 4))
                dve.tensor_reduce(al[:, k, :, DH:DH + 1], sc[:, k, :, (0 if AT_PREV[f] else P):2 * P], AX.X, ALU.max, negate=True)\
                    .then_inc(m_ready, 1)

            def turned_p(a, i, q):
                dve.wait_ge(p_turned, i * 8 + (4 * a + q + 1))
                src = ps[:, 6, :].rearrange("p (x h t) -> p x h t", x=2, h=2)
                if AT_PREV[a]:
                    dve.tensor_copy(pt[:, 2 * q:2 * q + 2, :, :], src).then_inc(pt_ready, 1)
                else:
                    dve.tensor_copy(pt[:, 2 * q:2 * q + 2, 1, :], src[:, :, 1, :]).then_inc(pt_ready, 1)

            def at_step(a, i):
                if a + 1 < AU:
                    keys(a + 1, i)
                turned_p(a, i, 0)
                if a + 1 < AU:
                    masked(a + 1, i)
                turned_p(a, i, 2)
                if a + 1 < AU:
                    maxima(a + 1, i)
                dve.wait_ge(pv_done, i * 2 + (a + 1))
                dve.tensor_copy(al[:, a % 2, :, 0:DH], ps[:, 0, :].rearrange("p (x d) -> p x d", x=H)).then_inc(acc_ready, 1)

            dve.wait_ge(job_done, J_WO)
            dve.memset(aq[:, :, :], 0.0).then_inc(aq_zeroed, 1)
            dve.wait_ge(table_loaded, 32)
            keys(0, 0)
            masked(0, 0)
            maxima(0, 0)
            for first, n, turns in AT_RUNS:
                if turns == 1:
                    for a in range(first, first + n):
                        at_step(a, 0)
                else:
                    with dve.Fori(0, turns) as i:
                        for a in range(first, first + n):
                            at_step(a, i)

            def low_o(m):
                dve.wait_ge(o_hi, m + 1)
                cols = slice(NS + m * P, NS + (m + 1) * P)
                tt(oL[:, :, cols], ps[:, m % 2, :].rearrange("p (c t) -> p c t", c=4), oH[:, :, cols], ALU.subtract).then_inc(o_lo, 1)

            for m in range(NP // P):
                k, n = m % 2, 7 * m
                dve.wait_ge(cb_loaded[k], 16 * (m // 2 + 1))
                nm = [cb[:, k, g, :, DH] for g in range(G)]
                tt(cm[:, 0, :], nm[0], nm[1], ALU.min).then_inc(c_step, 1)
                dve.wait_ge(c_step, n + 1)
                tt(cm[:, 1, :], cm[:, 0, :], nm[2], ALU.min).then_inc(c_step, 1)
                dve.wait_ge(c_step, n + 2)
                tt(cw[:, k, :, :], cm[:, 1:2, :].broadcast_to([P, G, H]), cb[:, k, :, :, DH], ALU.subtract).then_inc(c_step, 1)
                dve.wait_ge(cw_exp, m + 1)
                tt(cb[:, k, :, :, DH], cw[:, k, :, :], cb[:, k, :, :, DH + 1], ALU.mult).then_inc(c_step, 1)
                dve.wait_ge(c_step, n + 4)
                dve.tensor_reduce(cm[:, 2, :], cb[:, k, :, :, DH].rearrange("p g h -> p h g"), AX.X, ALU.add).then_inc(c_step, 1)
                dve.wait_ge(c_step, n + 5)
                dve.reciprocal(cm[:, 3, :], cm[:, 2, :]).then_inc(c_step, 1)
                dve.wait_ge(c_step, n + 6)
                tt(cw[:, k, :, :], cw[:, k, :, :], cm[:, 3:4, :].broadcast_to([P, G, H]), ALU.mult).then_inc(c_step, 1)
                dve.wait_ge(c_step, n + 7)
                for g in range(G):
                    tt(cb[:, k, g, :, 0:DH], cb[:, k, g, :, 0:DH],
                       cw[:, k, g, :].rearrange("p (h a) -> p h a", a=1).broadcast_to([P, H, DH]), ALU.mult)\
                        .then_inc(cm_done, 1)
                dve.wait_ge(cm_done, 4 * m + 3)
                tt(cp[:, 1, :].rearrange("p (h d) -> p h d", h=H), cb[:, k, 0, :, 0:DH], cb[:, k, 1, :, 0:DH], ALU.add).then_inc(cm_done, 1)
                dve.wait_ge(cm_done, 4 * m + 4)
                if m:
                    low_o(m - 1)
                tt(cp[:, 0, :].rearrange("p (hp par d) -> p par hp d", hp=4, par=2),
                   cp[:, 1, :].rearrange("p (par hp d) -> p par hp d", hp=4, par=2),
                   cb[:, k, 2, :, 0:DH].rearrange("p (par hp) d -> p par hp d", par=2), ALU.add).then_inc(co_ready, 1)
            low_o(NP // P - 1)

            for b in range(NS):
                k = b % 2
                dve.wait_ge(b_loaded[k], 16 * 8 * (b // 2 + 1))
                for tl, n in ((0, P), (1, 83)):
                    tt(bK[0:n, k, tl, :], bK[0:n, k, tl, :], bQ[0:n, k, tl, :], ALU.mult).then_inc(b_prod, 1)
                for tl, n in ((0, P), (1, 83)):
                    dve.wait_ge(b_prod, 2 * b + tl + 1)
                    dve.tensor_reduce(bS[0:n, tl, b * H:(b + 1) * H], bK[0:n, k, tl, :].rearrange("p (h d) -> p h d", h=H),
                                      AX.X, ALU.add).then_inc(*((b_red, 1) if tl == 0 else (b_scored, 1)))
            dve.wait_ge(b_red, NS)
            dve.wait_ge(b_turned, 1)
            dve.tensor_copy(bP[:, 0:211], ps[0:64, 0, 0:211]).then_inc(b_step, 1)
            dve.wait_ge(b_step, 1)
            dve.tensor_reduce(bl[:, 0:1], bP[:, 0:211], AX.X, ALU.max, negate=True).then_inc(b_step, 1)
            dve.wait_ge(b_exp, 1)
            dve.reciprocal(bl[:, 2:3], bl[:, 1:2]).then_inc(b_step, 1)
            dve.wait_ge(b_pturned, 1)
            dve.wait_ge(table_loaded, 16 * 5)
            for tl, n in ((0, P), (1, 83)):
                tt(bT[0:n, tl, :, :], ps[0:n, 1, tl * 64:(tl + 1) * 64].rearrange("p (a c) -> p a c", a=1).broadcast_to([n, NS, 64]),
                   bM[0:n, :, :], ALU.mult).then_inc(b_masked, 1)
            dve.wait_ge(b_pv, 1)
            dve.wait_ge(b_step, 3)
            stt(out=bA[:, :], in0=ps[0:64, 2, :], scalar=bl[:, 2:3], in1=bD[:, :], op0=ALU.mult, op1=ALU.mult).then_inc(b_diag, 1)
            dve.wait_ge(b_oh, 1)
            tt(oL[:, :, 0:NS], ps[:, 3, 0:4 * NS].rearrange("p (c t) -> p c t", c=4), oH[:, :, 0:NS], ALU.subtract).then_inc(b_ol, 1)

            def out_drain(u0, j0, i=0, per_u=0, per_j=0):
                j = j0
                for a, tiles in enumerate(OUT_TILES):
                    cut_lo(u0 + a + 2, i, per_u)
                    for d in tiles:
                        for t in range(TG):
                            dve.wait_ge(job_done, i * per_j + (j + 1))
                            tt(xT[:, d, tok(t)], ps[:, j % NB, 0:TS], xT[:, d, tok(t)], ALU.add).then_inc(drained[j % NB], 1)
                            j += 1

            out_drain(U_WO, J_WO)
            norm(1)

            def ffn_turn(i, j0, u0, last=False):
                cut_lo(u0 + 2, i, 3)
                h0 = 6 * FG * (j0 == J_FFN1)
                for p in range(6):
                    jg, ju = j0 + 2 * p, j0 + 2 * p + 1
                    t, f = p // 2, p % 2
                    dve.wait_ge(drained[jg % NB], drain(jg, i, FFN_J))
                    dve.wait_ge(job_done, i * FFN_J + (ju + 1))
                    if p >= 2:
                        dve.wait_ge(hid_ready, i * 6 + (h0 + p - 1))
                    tt(us[:, p % 2, :], ps[:, ju % NB, 0:TS], gs[:, p % 3, :], ALU.mult).then_inc(drained[ju % NB], 1)
                    dve.wait_ge(drained[ju % NB], drain(ju, i, FFN_J))
                    dve.tensor_copy(hidH[:, f, tok(t)], us[:, p % 2, :]).then_inc(hid_hi, 1)
                    dve.wait_ge(hid_hi, i * 6 + (h0 + p + 1))
                    tt(hidL[:, f, tok(t)], us[:, p % 2, :], hidH[:, f, tok(t)], ALU.subtract).then_inc(hid_ready, 1)
                j = j0 + 12
                for t in range(TG):
                    for d in range(KC):
                        if t < 2 and d == 3 and not last:
                            cut_lo(u0 + 3 + t, i, 3)
                        dve.wait_ge(job_done, i * FFN_J + (j + 1))
                        tt(xT[:, d, tok(t)], ps[:, j % NB, 0:TS], xT[:, d, tok(t)], ALU.add).then_inc(drained[j % NB], 1)
                        j += 1

            with dve.Fori(0, FG) as i:
                ffn_turn(i, J_FFN0, U_FFN0)
            norm(2)

            dve.wait_ge(table_loaded, 16 * 7)
            dve.wait_ge(h_lo, 3 * TG * KC)
            with dve.Fori(0, RH) as h:
                n = 0
                for u, scale in ((0, 1.0), (1, RQ ** -0.5)):
                    cut_lo(U_R1 + u + 2, h, 6)
                    for t in range(TG):
                        j1 = J_R1 + u * 6 + 2 * t
                        b1, b2 = j1 % NB, (j1 + 1) % NB
                        x1, x2 = ps[:, b1, 0:TS], ps[:, b2, 0:TS]
                        steps = h * (6 * 3) + 3 * n
                        dve.wait_ge(job_done, h * R1_J + (j1 + 2))
                        dve.wait_ge(rrope_done, h * 6 + (n + 1))
                        stt(out=un[:, 0, :], in0=x1, scalar=scale, in1=cosR[:, tok(t)], op0=ALU.mult, op1=ALU.mult).then_inc(rrope_step, 1)
                        stt(out=un[:, 1, :], in0=x2, scalar=scale, in1=sinR[:, tok(t)], op0=ALU.mult, op1=ALU.mult).then_inc(rrope_step, 1)
                        stt(out=un[:, 2, :], in0=x2, scalar=scale, in1=cosR[:, tok(t)], op0=ALU.mult, op1=ALU.mult).then_inc(drained[b2], 1)
                        stt(out=un[:, 3, :], in0=x1, scalar=scale, in1=sinR[:, tok(t)], op0=ALU.mult, op1=ALU.mult).then_inc(drained[b1], 1)
                        dve.wait_ge(rstored[n % 4], h * (16 * 9) + 16 * (n // 4 + 1))
                        dve.wait_ge(rrope_step, steps + 2)
                        tt(rw[:, n % 4, 0:TS], un[:, 0, :], un[:, 1, :], ALU.subtract).then_inc(rrope_step, 1)
                        dve.wait_ge(drained[b2], drain(j1 + 1, h, R1_J))
                        dve.wait_ge(drained[b1], drain(j1, h, R1_J))
                        dve.wait_ge(rrope_step, steps + 3)
                        tt(rw[:, n % 4, TS:2 * TS], un[:, 2, :], un[:, 3, :], ALU.add).then_inc(rrope_done, 1)
                        n += 1
                for u in range(2, 6):
                    cut_lo(U_R1 + u + 2, h, 6)

            dve.wait_ge(table_loaded, 16 * 8)
            with dve.Fori(0, RH) as h:
                dve.wait_ge(head_loaded, h * 64 + 64)

                def y_rest(ch):
                    k = ch % 2
                    n = h * (8 * 5) + 5 * ch
                    dve.wait_ge(rroot_ready, h * 8 + (ch + 1))
                    dve.reciprocal(rr[:, k, :], rr[:, k, :]).then_inc(rstep, 1)
                    dve.wait_ge(rstep, n + 1)
                    for e in range(4):
                        stt(out=ry[:, k, e, :], in0=ps[:, 4 + k, e * P:(e + 1) * P], scalar=ron[:, e:e + 1],
                            in1=rr[:, k, :], op0=ALU.mult, op1=ALU.mult).then_inc(rstep, 1)
                    dve.wait_ge(rstep, n + 5)
                    tt(ry[:, k, :, :], ry[:, k, :, :], rg[:, ch % RS, :, :], ALU.mult).then_inc(y_ready, 1)

                def y_low(ch):
                    dve.wait_ge(y_hi, h * 8 + (ch + 1))
                    cols = slice(NS + ch * P, NS + (ch + 1) * P)
                    tt(yL[:, :, cols], ry[:, ch % 2, :, :], yH[:, :, cols], ALU.subtract).then_inc(y_lo, 1)

                dve.wait_ge(zqg_loaded, h * 48 + 48)
                for f in range(2):
                    ins = tt(zm[:, f, :, :], zq[:, 0, f, :].rearrange("p (a b) -> p b a", a=1).broadcast_to([P, NS, NS]), eye8[:, :, :],
                             ALU.mult)
                    ins.then_inc(*((zm_half, 1) if f == 0 else (zm_ready, 1)))
                for ch in range(8):
                    k = ch % 2
                    dve.wait_ge(r_loaded[ch % RS], h * (64 * 8 // RS) + 64 * (ch // RS + 1))
                    tt(qd[:, k, :, :], rqT[:, ch % RS, :, :], qdec[:, :].rearrange("p (a t) -> p a t", a=1).broadcast_to([P, 2, P]), ALU.mult).then_inc(qd_ready, 1)
                    dve.wait_ge(rs_done, h * 8 + (ch + 1))
                    tt(sT[:, k, :], ps[:, 1, 0:P], dmask[:, :], ALU.mult).then_inc(sT_ready, 1)
                    if ch:
                        y_rest(ch - 1)
                        y_low(ch - 1)
                    dve.wait_ge(z_scaled, h * NS + (ch + 1))
                    for f in range(2):
                        stt(out=zS[:, ch % RS, f, :], in0=zV[:, ch % RS, :], scalar=zq[:, 1, f, ch:ch + 1], in1=zS[:, ch % RS, f, :],
                            op0=ALU.mult, op1=ALU.add).then_inc(z_new, 1)
                    dve.wait_ge(up_done, h * 8 + (ch + 1))
                    if ch == 0:
                        dve.wait_ge(state_stored, h * 16 + 16)
                    for f in range(2):
                        if ch == 0:
                            dve.tensor_copy(state[:, f, :], ps[:, 2 + f, :]).then_inc(st_ready, 1)
                        else:
                            if f == 0:
                                dve.wait_ge(st_ready, h * 16 + 2 * ch)
                            stt(out=state[:, f, :], in0=state[:, f, :], scalar=gC, in1=ps[:, 2 + f, :],
                                op0=ALU.mult, op1=ALU.add).then_inc(st_ready, 1)
                y_rest(7)
                y_low(7)
                dve.wait_ge(zl_step, h * 2 + 2)
                dve.reciprocal(zl[:, 2:3], zl[:, 1:2]).then_inc(zr_ready, 1)
                dve.wait_ge(zo_turned, h + 1)
                for e in range(4):
                    ts(zy[:, 0, e, :], ps[:, 6, e * NS:(e + 1) * NS], ron[:, e:e + 1], None, ALU.mult).then_inc(zy_step, 1)
                dve.wait_ge(zy_step, h * 5 + 4)
                tt(zy[:, 1, :, :], zy[:, 0, :, :], zg[:, :, :], ALU.mult).then_inc(zy_step, 1)
                dve.wait_ge(zy_hi, h + 1)
                tt(yL[:, :, 0:NS], zy[:, 1, :, :], yH[:, :, 0:NS], ALU.subtract).then_inc(zy_lo, 1)
                out_drain(U_RO, J_RO, h, 3, RO_J)
            norm(3)
            with dve.Fori(0, FG - 1) as i:
                ffn_turn(i, J_FFN1, U_FFN1)
            ffn_turn(FG - 1, J_FFN1, U_FFN1, last=True)
    ctx.close()


def weight_units(a_w_qkv, a_w_o, r_w_in, r_w_o, f_w_gate, f_w_up, f_w_down):
    import numpy as np
    out = np.zeros((UNITS, P, UW), np.float32)
    n = 0

    def put(block):
        nonlocal n
        block = block.reshape(P, -1)
        out[n, :, :block.shape[1]] = block
        n += 1

    def columns(w, c0):
        put(w[:, c0:c0 + HC].reshape(KC, P, HC).transpose(1, 0, 2))

    def out_rows(w):
        blocks = w.reshape(4, P, KC, P).transpose(1, 2, 0, 3)
        for tiles in OUT_TILES:
            put(blocks[:, tiles[0]:tiles[-1] + 1])

    def ffn(layer):
        for i in range(FG):
            columns(f_w_gate[layer], i * HC)
            columns(f_w_up[layer], i * HC)
            put(f_w_down[layer][i * HC:(i + 1) * HC].reshape(2, P, D).transpose(1, 0, 2))

    for c0 in range(0, 3 * G * AW, HC):
        columns(a_w_qkv[0], c0)
    out_rows(a_w_o[0])
    ffn(0)
    for h in range(RH):
        for c0 in (h * RQ, D + h * RQ, 2 * D + h * RV, 2 * D + h * RV + HC, 4 * D + h * RV, 4 * D + h * RV + HC):
            columns(r_w_in[0], c0)
    for h in range(RH):
        out_rows(r_w_o[0][h * RV:(h + 1) * RV])
    ffn(1)
    assert n == UNITS
    return out


def tables():
    import numpy as np
    f = np.float32

    def angles(pos, half):
        inv = (10000.0 ** (-np.arange(half, dtype=f) / f(half)).astype(np.float64)).astype(f)
        ang = (pos.astype(f)[:, None] * inv[None, :]).astype(f).astype(np.float64)
        return np.cos(ang).astype(f), np.sin(ang).astype(f)

    pos = np.concatenate([np.full(NS, 256), np.arange(NP)])
    out = {}
    cos, sin = angles(pos, DH // 2)
    cols = np.stack([tile_columns(m) + np.arange(P) for m in range(MT)], 1)
    out["ropeC"] = np.concatenate([cos[cols], cos[cols]], -1)
    out["ropeS"] = np.concatenate([-sin[cols], sin[cols]], -1)
    cos, sin = angles(pos, RQ // 2)
    out["cosR"], out["sinR"] = cos.T, sin.T
    i = np.arange(P)
    ok_self = i[None, :] <= i[:, None]
    out["maskP"] = np.where(np.concatenate([i[None, :] >= i[:, None], ok_self], 1), 0.0, -1e38)
    out["maskD"] = np.where(ok_self & (i[None, :] // 64 == i[:, None] // 64), 0.0, -1e38)
    out["ident"] = np.eye(P)
    lg = np.log1p(-np.exp2(-5.0 - np.arange(RH))).astype(f).astype(np.float64)
    out["small"] = np.broadcast_to([EPS, 64 * EPS], (P, 2))
    decay = np.zeros((RH, P, 4))
    decay[:, :, 0] = np.exp(lg)[:, None]
    decay[:, :, 1] = np.exp(P * lg)[:, None]
    decay[:, :, 2] = np.exp((P - 1.0 - i)[None, :] * lg[:, None])
    out["decay"] = decay
    rel = (i[None, None, :] - i[None, :, None]).astype(np.float64)
    out["dmask"] = np.where(rel >= 0, np.exp(np.maximum(rel, 0) * lg[:, None, None]), 0.0)
    out["qdec"] = np.broadcast_to(np.exp((i + 1.0)[None, :] * lg[:, None])[:, None], (RH, P, P))
    out["eye8"] = np.broadcast_to(np.eye(NS)[None], (P, NS, NS))
    b, h = np.arange(NS * H) // H, np.arange(NS * H) % H
    out["blockmask"] = np.broadcast_to((b[None, :] == np.arange(NS)[:, None])[None], (P, NS, NS * H))
    out["diagmask"] = h[:, None] == np.arange(AW)[None, :] // DH
    out["select"] = b[:, None] == np.arange(NS)[None, :]
    return {k: np.ascontiguousarray(v, dtype=f) for k, v in out.items()}


def kernel(x_prompt, x_sample, cache_kv_g0, cache_kv_g1, cache_kv_g2, state_retention,
           mix_norm, ffn_norm, a_w_qkv, a_q_norm, a_k_norm, a_w_o,
           r_w_in, r_out_norm, r_w_o, f_w_gate, f_w_up, f_w_down):
    import numpy as np
    import concourse.bacc as bacc
    from concourse.bass_utils import run_bass_kernel_spmd

    nc = bacc.Bacc("TRN2", target_bir_lowering=False, num_devices=1)
    arrays = {}

    def given(name, a):
        arrays["in_" + name] = np.ascontiguousarray(a)
        return nc.dram_tensor("in_" + name, a.shape, F32, kind="ExternalInput").ap()

    def result(name, shape):
        return nc.dram_tensor(name, shape, F32, kind="ExternalOutput").ap()

    def kept(name, shape):
        return nc.dram_tensor(name, shape, F32).ap()

    def chunked(a):
        return np.asarray(a).reshape(-1, KC, P).transpose(2, 0, 1)

    x = np.concatenate([np.asarray(x_sample)[:, 0], np.asarray(x_prompt)[0]], 0)
    x_in = given("x", x.T.reshape(KC, P, T).transpose(1, 0, 2))
    w = given("w", weight_units(*(np.asarray(a) for a in (a_w_qkv, a_w_o, r_w_in, r_w_o, f_w_gate, f_w_up, f_w_down))))
    c = {name: given(name, a) for name, a in tables().items()}
    norms = np.stack([np.asarray(a)[i] for i in range(2) for a in (mix_norm, ffn_norm)])
    c["gains"] = given("gains", chunked(norms))
    qk = np.stack([np.asarray(a_q_norm)[0], np.asarray(a_k_norm)[0]], 1).reshape(2 * G, DH)
    c["qkg"] = given("qkg", np.broadcast_to(qk[None], (P, 2 * G, DH)))
    c["ron"] = given("ron", np.asarray(r_out_norm)[0].reshape(RH, 4, P).transpose(0, 2, 1))
    caches = [np.asarray(a)[0] for a in (cache_kv_g0, cache_kv_g1, cache_kv_g2)]
    kv_cache = [given(f"cache{g}", a.reshape(NS, -1, 2 * AW)) for g, a in enumerate(caches)]
    state_in = given("state_in", np.asarray(state_retention)[0])
    y = result("y", (P, KC, T))
    keep = (128, 512, 1024)
    kv_p = [result(f"kv_p{g}", (keep[g], 2, AW)) for g in range(G)]
    kv_s = [result(f"kv_s{g}", (NS, a.shape[1], 2 * AW)) for g, a in enumerate(caches)]
    ret_p = result("ret_p", (RH, RQ, RV))
    ret_s = result("ret_s", (NS, RH, RQ, RV))
    scratch = (kept("qkv_rows", (G, 3, T, AW)), kept("acc_rows", (G, NP, H * (DH + 2))), kept("q_cols", (RH, P, 2, T)),
               kept("k_cols", (RH, P, 2, T)), kept("v_rows", (RH, T, RV)), kept("g_cols", (RH, P, 4, T)))
    trunk(nc, x_in, w, c, kv_cache, state_in, y, kv_p, kv_s, ret_p, ret_s, scratch)
    r = run_bass_kernel_spmd(nc, [arrays], core_ids=[0]).results[0]
    rows = r["y"].transpose(1, 0, 2).reshape(D, T).T
    out = [rows[NS:][None], rows[:NS][:, None]]
    for g in range(G):
        out.append(r[f"kv_p{g}"].reshape(1, 1, keep[g], 2, H, DH))
        out.append(r[f"kv_s{g}"].reshape(1, NS, -1, 2, H, DH))
    out.append(r["ret_p"][None, None])
    out.append(r["ret_s"][None])
    return tuple(out)
```

```python
from contextlib import ExitStack

import concourse.bass as bass
from concourse import mybir

F32 = mybir.dt.float32
F32R = mybir.dt.float32r
ALU = mybir.AluOpType
ACT = mybir.ActivationFunctionType
AX = mybir.AxisListType

P = 128
D = 1024
KC = D // P
NS, NP = 8, 1024
T = NS + NP
TG = 3
TS = T // TG
MT = 1 + NP // P
UW = 2048
HC = UW // KC
G, H, DH = 3, 8, 64
AW = H * DH
RH, RQ, RV = 4, 256, 512
FF = 2816
FG = FF // HC
EPS = 1e-6
NB = 6
SLOTS = 3
CS = 3
RS = 4

QKV_J, WO_J, FFN_J, R1_J, RO_J = 6 * MT, 8 * TG, 12 + 8 * TG, 12 + 2 * MT + 12, 8 * TG
J_QKV = 0
J_WO = J_QKV + G * QKV_J
J_FFN0 = J_WO + WO_J
J_R1 = J_FFN0 + FG * FFN_J
J_RO = J_R1 + RH * R1_J
J_FFN1 = J_RO + RH * RO_J
U_QKV = 0
U_WO = U_QKV + 6 * G
U_FFN0 = U_WO + 3
U_R1 = U_FFN0 + 3 * FG
U_RO = U_R1 + 6 * RH
U_FFN1 = U_RO + 3 * RH
UNITS = U_FFN1 + 3 * FG
AU = G * NP // P
AT_PIECES = [2 if a // 8 == 2 else 1 for a in range(AU)]
AT_PREV = [1 <= a < 8 or 8 <= a < 16 and a % 2 == 1 for a in range(AU)]
AT_RUNS = [(0, 1, 1), (1, 2, 3), (7, 1, 1), (8, 2, 3), (14, 2, 1), (16, 2, 3), (22, 2, 1)]
OUT_ORDER = (1, 2, 0)
OUT_TILES = [(0, 1, 2), (3, 4, 5), (6, 7)]


def free(j, i=0, per=0):
    return i * (per // NB) + (j // NB + 1)


def drain(j, i=0, per=0):
    return i * (per // NB) + (j // NB + 2)


def tile_columns(m):
    return 0 if m == 0 else NS + P * (m - 1)


def trunk(nc, x, w, c, kv_cache, state_in, y, kv_p, kv_s, ret_p, ret_s, scratch):
    qkv_dram, acc_dram, q_dram, k_dram, v_dram, g_dram = scratch
    ctx = ExitStack()

    def sb(name, shape, dt=F32, scope=None):
        return (scope or ctx).enter_context(nc.sbuf_tensor(name, shape, dt))

    def sem(name):
        return ctx.enter_context(nc.semaphore(name))

    xT = sb("xT", [P, KC, T])
    raw = sb("raw", [P, SLOTS, UW])
    wH = sb("wH", [P, SLOTS, UW], F32R)
    wL = sb("wL", [P, SLOTS, UW], F32R)
    gains = sb("gains", [P, 4, KC])
    small = sb("small", [P, 2])
    epsb = small[:, 0:1]
    eps64 = small[:, 1:2]
    ones = sb("ones", [P, P])
    ident = sb("ident", [P, P])

    A = ExitStack()
    hH = sb("hH", [P, KC, T], F32R, A)
    hL = sb("hL", [P, KC, T], F32R, A)
    sq = sb("sq", [P, 4, TS], scope=A)
    un = sb("un", [P, 4, TS], scope=A)
    rt = sb("rt", [P, TG, TS], scope=A)
    B = ExitStack()
    ropeC = sb("ropeC", [P, MT, DH], scope=B)
    ropeS = sb("ropeS", [P, MT, DH], scope=B)
    qkg = sb("qkg", [P, 2 * G, DH], scope=B)
    junk = sb("junk", [P, 2, HC], scope=B)
    ss = sb("ss", [P, 2, 4], scope=B)
    rq = sb("rq", [P, 2, 4], scope=B)
    ri = sb("ri", [P, 2, 4], scope=B)
    qn = sb("qn", [P, 4, DH], scope=B)
    qc = sb("qc", [P, 4, DH], scope=B)
    qs = sb("qs", [P, 4, DH], scope=B)
    ot = sb("ot", [P, NB, HC], scope=B)
    B.close()
    B = ExitStack()
    hidH = sb("hidH", [P, 2, T], F32R, B)
    hidL = sb("hidL", [P, 2, T], F32R, B)
    gs = sb("gs", [P, 3, TS], scope=B)
    us = sb("us", [P, 2, TS], scope=B)
    B.close()
    B = ExitStack()
    cosR = sb("cosR", [P, T], scope=B)
    sinR = sb("sinR", [P, T], scope=B)
    rw = sb("rw", [P, 4, 2 * TS], scope=B)
    B.close()
    A.close()

    A = ExitStack()
    oH = sb("oH", [P, 4, T], F32R, A)
    oL = sb("oL", [P, 4, T], F32R, A)
    bS = sb("bS", [P, 2, NS, H], scope=A)
    bl = sb("bl", [NS * H, 4], scope=A)
    B = ExitStack()
    bK = sb("bK", [P, 2, 2, AW], scope=B)
    bQ = sb("bQ", [P, 2, 2, AW], scope=B)
    B2 = ExitStack()
    maskP = sb("maskP", [P, 2 * P], scope=B2)
    maskD = sb("maskD", [P, P], scope=B2)
    qkv = sb("qkv", [P, 2, 3, AW], scope=B2)
    aq = sb("aq", [P, H, P], scope=B2)
    ak = sb("ak", [P, 2, 4, P], scope=B2)
    sc = sb("sc", [P, 2, H, 2 * P], scope=B2)
    pt = sb("pt", [P, H, 2, P], scope=B2)
    al = sb("al", [P, 2, H, DH + 2], scope=B2)
    B2.close()
    B2 = ExitStack()
    cb = sb("cb", [P, CS, G, H, DH + 2], scope=B2)
    cw = sb("cw", [P, 2, G, H], scope=B2)
    cm = sb("cm", [P, 4, H], scope=B2)
    cp = sb("cp", [P, AW], scope=B2)
    bV = sb("bV", [P, NS, 2, AW], scope=B2)
    B2.close()
    B.close()
    B = ExitStack()
    bP = sb("bP", [NS * H, 2 * P], scope=B)
    bM = sb("bM", [P, NS, NS * H], scope=B)
    bT = sb("bT", [P, 2, NS, NS * H], scope=B)
    bD = sb("bD", [NS * H, AW], scope=B)
    bE = sb("bE", [NS * H, NS], scope=B)
    bA = sb("bA", [NS * H, AW], scope=B)
    B.close()
    A.close()

    A = ExitStack()
    yH = sb("yH", [P, 4, T], F32R, A)
    yL = sb("yL", [P, 4, T], F32R, A)
    dmask = sb("dmask", [P, P], scope=A)
    qdec = sb("qdec", [P, P], scope=A)
    decay = sb("decay", [P, 4], scope=A)
    ron = sb("ron", [P, 4], scope=A)
    eye8 = sb("eye8", [P, NS, NS], scope=A)
    g1, gC, kdec = decay[:, 0:1], decay[:, 1:2], decay[:, 2:3]
    rqT = sb("rqT", [P, RS, 2, P], scope=A)
    rkT = sb("rkT", [P, RS, 2, P], scope=A)
    rv = sb("rv", [P, RS, RV], scope=A)
    rg = sb("rg", [P, RS, 4, P], scope=A)
    kd = sb("kd", [P, 2, 2, P], scope=A)
    qd = sb("qd", [P, 2, 2, P], scope=A)
    sT = sb("sT", [P, 2, P], scope=A)
    state = sb("state", [P, 2, RV], scope=A)
    rsq = sb("rsq", [P, 4, P], scope=A)
    rr = sb("rr", [P, 2, P], scope=A)
    ry = sb("ry", [P, 2, 4, P], scope=A)
    zS = sb("zS", [P, RS, 2, RV], scope=A)
    zV = sb("zV", [P, RS, RV], scope=A)
    zq = sb("zq", [P, 2, 2, NS], scope=A)
    zg = sb("zg", [P, 4, NS], scope=A)
    zm = sb("zm", [P, 2, NS, NS], scope=A)
    zo = sb("zo", [NS, RV], scope=A)
    zl = sb("zl", [NS, 4], scope=A)
    zy = sb("zy", [P, 2, 4, NS], scope=A)
    A.close()

    ps = ctx.enter_context(nc.psum_tensor("ps", [P, 8, 512], F32))

    raw_loaded = [sem(f"raw_loaded{s}") for s in range(SLOTS)]
    hi_ready = [sem(f"hi_ready{s}") for s in range(SLOTS)]
    lo_ready = [sem(f"lo_ready{s}") for s in range(SLOTS)]
    job_done = sem("job_done")
    drained = [sem(f"drained{b}") for b in range(NB)]
    x_loaded = [sem(f"x_loaded{t}") for t in range(TG)]
    const_loaded = sem("const_loaded")
    table_loaded = sem("table_loaded")
    ones_set = sem("ones_set")
    table_ready = sem("table_ready")
    sq_ready, sq_used, sum_done = sem("sq_ready"), sem("sq_used"), sem("sum_done")
    root_ready, recip_ready = sem("root_ready"), sem("recip_ready")
    normed, h_hi, h_lo = sem("normed"), sem("h_hi"), sem("h_lo")
    head_sq, root_q = sem("head_sq"), sem("root_q")
    rope_step, rope_done = sem("rope_step"), sem("rope_done")
    stored = [sem(f"stored{b}") for b in range(NB)]
    hid_hi, hid_ready = sem("hid_hi"), sem("hid_ready")
    rrope_step, rrope_done = sem("rrope_step"), sem("rrope_done")
    rstored = [sem(f"rstored{b}") for b in range(4)]
    aqk_loaded = [sem(f"aqk_loaded{b}") for b in range(2)]
    av_loaded = [sem(f"av_loaded{b}") for b in range(2)]
    q_turned, k_turned, aq_ready, aq_ready2, ak_ready, aq_zeroed = (sem(n) for n in ("q_turned", "k_turned", "aq_ready", "aq_ready2", "ak_ready", "aq_zeroed"))
    s_done, s_masked, m_ready, p_ready = sem("s_done"), sem("s_masked"), sem("m_ready"), sem("p_ready")
    p_turned, pt_ready, pt_ready2, pv_done, acc_ready = (sem(n) for n in ("p_turned", "pt_ready", "pt_ready2", "pv_done", "acc_ready"))
    acc_stored = [sem(f"acc_stored{b}") for b in range(2)]
    cb_loaded = [sem(f"cb_loaded{b}") for b in range(CS)]
    c_max, c_step, cm_done, cw_exp, co_ready, co_turned, o_hi, o_lo = (sem(n) for n in ("c_max", "c_step", "cm_done", "cw_exp", "co_ready", "co_turned", "o_hi", "o_lo"))
    b_loaded = [sem(f"b_loaded{b}") for b in range(2)]
    b_prod, b_red = sem("b_prod"), sem("b_red")
    bv_loaded = [sem(f"bv_loaded{b}") for b in range(NS)]
    b_scored, b_turned, b_step, b_exp, b_pturned, b_masked, b_pv, b_diag, b_out, b_oh, b_ol = (
        sem(n) for n in ("b_scored", "b_turned", "b_step", "b_exp", "b_pturned", "b_masked", "b_pv",
                         "b_diag", "b_out", "b_oh", "b_ol"))
    r_loaded = [sem(f"r_loaded{b}") for b in range(RS)]
    k_up, kd_ready, rs_done, sT_ready, qd_ready, ro_done, up_done, st_ready = (
        sem(n) for n in ("k_up", "kd_ready", "rs_done", "sT_ready", "qd_ready", "ro_done", "up_done", "st_ready"))
    rsq_half, rsq_added = sem("rsq_half"), sem("rsq_added")
    rsq_ready, rsum_done, rroot_ready, rstep, y_ready, y_hi, y_lo = (
        sem(n) for n in ("rsq_ready", "rsum_done", "rroot_ready", "rstep", "y_ready", "y_hi", "y_lo"))
    head_loaded, sp_gate, pe_gate = sem("head_loaded"), sem("sp_gate"), sem("pe_gate")
    z_loaded = [sem(f"z_loaded{b}") for b in range(RS)]
    zm_half = sem("zm_half")
    zqg_loaded, zm_ready, z_scaled, z_new, z_read = (sem(n) for n in ("zqg_loaded", "zm_ready", "z_scaled", "z_new", "z_read"))
    z_stored = [sem(f"z_stored{b}") for b in range(RS)]
    zl_step, zr_ready, zo_ready, zo_turned, zy_step, zy_hi, zy_lo = (
        sem(n) for n in ("zl_step", "zr_ready", "zo_ready", "zo_turned", "zy_step", "zy_hi", "zy_lo"))
    state_stored = sem("state_stored")
    copied = sem("copied")
    y_stored = sem("y_stored")


    def hi_ready_at(u, i=0, per=0):
        return i * (per // SLOTS) + (u // SLOTS + 1)

    def norm_x_wait(eng, n, t):
        if n == 0:
            eng.wait_ge(x_loaded[t], 16)
            return
        if n == 1 or n == 3:
            j = (J_WO + WO_J if n == 1 else J_RO + RH * RO_J) - 1
        else:
            j = J_FFN0 + FG * FFN_J - 1 - 8 * (TG - 1 - t)
        for jj in range(j - NB + 1, j + 1):
            eng.wait_ge(drained[jj % NB], drain(jj))

    def tok(t):
        return slice(t * TS, (t + 1) * TS)

    with nc.Block() as block:

        @block.gpsimd
        def _(pool):
            for s in range(SLOTS):
                pool.wait_ge(x_loaded[min(s, 1)], 16)
                pool.dma_start(raw[:, s, :], w[s]).then_inc(raw_loaded[s], 16)

            def load(r, s, before=0):
                pool.wait_ge(lo_ready[s], r + before)
                pool.dma_start(raw[:, s, :], w[bass.ds(r * SLOTS + (before * SLOTS + s), 1)].rearrange("a p n -> (a p) n"))\
                    .then_inc(raw_loaded[s], 16)

            first = U_RO // SLOTS + 1
            with pool.Fori(1, first) as r:
                for s in range(SLOTS):
                    load(r, s)
            with pool.Fori(0, RH) as h:
                load(h, 0, first)
                load(h, 1, first)
                for ch in range(8):
                    pool.wait_ge(rsq_ready, h * 8 + (ch + 1))
                    pool.tensor_tensor(rsq[:, 0:2, :], rsq[:, 0:2, :], rsq[:, 2:4, :], ALU.add).then_inc(rsq_half, 1)
                    pool.wait_ge(rsq_half, h * 8 + (ch + 1))
                    pool.tensor_tensor(rsq[:, 0, :], rsq[:, 0, :], rsq[:, 1, :], ALU.add).then_inc(rsq_added, 1)
                load(h, 2, first)
            with pool.Fori(first + RH, UNITS // SLOTS) as r:
                for s in range(SLOTS):
                    load(r, s)

        @block.sync
        def _(sp):
            sp.dma_start(xT[:, :, tok(0)], x[:, :, tok(0)]).then_inc(x_loaded[0], 16)
            for dst, src in ((gains[:, :, :], c["gains"]), (small[:, :], c["small"]), (ident[:, :], c["ident"]),
                             (ropeC[:, :, :], c["ropeC"]), (ropeS[:, :, :], c["ropeS"]), (qkg[:, :, :], c["qkg"])):
                sp.dma_start(dst, src).then_inc(const_loaded, 16)
            for t in range(1, TG):
                sp.dma_start(xT[:, :, tok(t)], x[:, :, tok(t)]).then_inc(x_loaded[t], 16)

            with sp.Fori(0, G) as g:
                for u in range(6):
                    for m in range(MT):
                        jj = u * MT + m
                        b = jj % NB
                        rows = NS if m == 0 else P
                        dst = qkv_dram[bass.ds(g, 1), u // 2, tile_columns(m):tile_columns(m) + rows,
                                       (u % 2) * HC:(u % 2 + 1) * HC].rearrange("a t n -> (a t) n")
                        if u < 4:
                            sp.wait_ge(rope_done, g * (4 * MT) + (jj + 1))
                        else:
                            sp.wait_ge(drained[b], drain(jj, g, QKV_J))
                        sp.sem_inc(sp_gate, 1)
                        sp.dma_start(dst, ot[0:rows, b, :]).then_inc(stored[b], 16)
            sp.wait_ge(job_done, J_WO)
            sp.wait_ge(rope_done, G * 4 * MT)
            sp.dma_start(maskP[:, :], c["maskP"]).then_inc(table_loaded, 16)
            sp.dma_start(maskD[:, :], c["maskD"]).then_inc(table_loaded, 16)

            def pieces(src, a):
                g, i = a // 8, a % 8
                if g == 0:
                    return [(slice(0, P), src[i * P:(i + 1) * P, :])]
                if g == 1:
                    return [(slice(0, P), src.rearrange("(l r) n -> r l n", r=4)[i // 2, i % 2 * P:(i % 2 + 1) * P, :])]
                by_residue = src.rearrange("(l r) n -> r l n", r=16)
                return [(slice(q * 64, (q + 1) * 64), by_residue[2 * i + q, :, :]) for q in range(2)]

            def at_load(a, tensors, loaded):
                for s in tensors:
                    for part, src in pieces(qkv_dram[a // 8, s, NS:T, :], a):
                        sp.dma_start(qkv[part, a % 2, s, :], src).then_inc(loaded[a % 2], 16)

            def cache_rows(b, s):
                cols = slice(s * AW, (s + 1) * AW)
                return ((slice(0, P), 0, kv_cache[0][b, :, cols]),
                        (slice(0, 64), 1, kv_cache[1][b, :, cols].rearrange("(l r) n -> l r n", r=4)[:, 0, :]),
                        (slice(64, 80), 1, kv_cache[2][b, :, cols].rearrange("(l r) n -> l r n", r=16)[:, 0, :]),
                        (slice(80, 83), 1, qkv_dram[:, 1 + s, b, :]))

            def sample_load(b):
                if b >= 2:
                    sp.wait_ge(b_scored, b - 1)
                for part, tl, src in cache_rows(b, 0):
                    sp.dma_start(bK[part, b % 2, tl, :], src).then_inc(b_loaded[b % 2], 16)
                for part, tl, g in ((slice(0, P), 0, 0), (slice(0, 64), 1, 1), (slice(64, 80), 1, 2)):
                    n = part.stop - part.start
                    sp.dma_start(bQ[part, b % 2, tl, :], qkv_dram[g, 0, b, :].partition_broadcast(n)).then_inc(b_loaded[b % 2], 16)
                sp.dma_start(bQ[80:83, b % 2, 1, :], qkv_dram[:, 0, b, :]).then_inc(b_loaded[b % 2], 16)

            for b in range(NB):
                sp.wait_ge(stored[b], 16 * ((G - 1) * QKV_J // NB + 1))
            for a in range(2):
                at_load(a, (0, 1), aqk_loaded)
                at_load(a, (2,), av_loaded)
            for b in range(NB):
                sp.wait_ge(stored[b], 16 * (G * QKV_J // NB + 1))
            sample_load(0)
            sample_load(1)
            for a in range(AU):
                if a + 2 < AU:
                    sp.wait_ge(q_turned, a + 1)
                    at_load(a + 2, (0, 1), aqk_loaded)
                if 1 <= a < AU - 1:
                    sp.wait_ge(pv_done, a + 1)
                    at_load(a + 1, (2,), av_loaded)
                sp.wait_ge(acc_ready, a + 1)
                for part, dst in pieces(acc_dram[a // 8], a):
                    sp.dma_start(dst, al[part, a % 2, :, :].rearrange("p h n -> p (h n)")).then_inc(acc_stored[a % 2], 16)
                if a + 2 < NS:
                    sample_load(a + 2)
                if a == NS + 1:
                    sp.wait_ge(b_scored, NS)
                    sp.dma_start(bM[:, :, :], c["blockmask"]).then_inc(table_loaded, 16)
                    sp.dma_start(bD[:, :], c["diagmask"]).then_inc(table_loaded, 16)
                    sp.dma_start(bE[:, :], c["select"]).then_inc(table_loaded, 16)
            for k in range(2):
                sp.wait_ge(acc_stored[k], 16 + 16 * sum(AT_PIECES[k::2]))
            for m in range(NP // P):
                if m >= CS:
                    sp.wait_ge(co_ready, m - CS + 1)
                sp.dma_start(cb[:, m % CS, :, :, :].rearrange("p g h n -> p g (h n)"),
                             acc_dram[:, m * P:(m + 1) * P, :].rearrange("g p n -> p g n")).then_inc(cb_loaded[m % CS], 16)
                if m >= 1:
                    for b in (range(2) if m == 1 else range(m, m + 1)):
                        for part, tl, src in cache_rows(b, 1):
                            sp.dma_start(bV[part, b, tl, :], src).then_inc(bv_loaded[b], 16)

            for g in range(G):
                sp.dma_start(kv_s[g][:, 0:kv_s[g].shape[1] - 1, :], kv_cache[g][:, 1:, :]).then_inc(copied, 16)
            for g in range(G):
                n = kv_p[g].shape[0]
                for s in range(2):
                    sp.dma_start(kv_p[g][:, s, :], qkv_dram[g, 1 + s, T - n:T, :]).then_inc(copied, 16)
                    sp.dma_start(kv_s[g][:, kv_s[g].shape[1] - 1, s * AW:(s + 1) * AW], qkv_dram[g, 1 + s, 0:NS, :]).then_inc(copied, 16)

            sp.wait_ge(job_done, J_R1)
            sp.dma_start(cosR[:, :], c["cosR"]).then_inc(table_loaded, 16)
            sp.dma_start(sinR[:, :], c["sinR"]).then_inc(table_loaded, 16)
            with sp.Fori(0, RH) as h:
                n = 0
                for dst in (q_dram, k_dram):
                    for t in range(TG):
                        sp.wait_ge(rrope_done, h * (2 * TG) + (n + 2))
                        sp.sem_inc(sp_gate, 1)
                        sp.dma_start(dst[bass.ds(h, 1), :, :, tok(t)].rearrange("a p f t -> (a p) f t"),
                                     rw[:, n % 4, :].rearrange("p (f t) -> p f t", f=2)).then_inc(rstored[n % 4], 16)
                        n += 1
                for u in range(2):
                    for m in range(MT):
                        rows = NS if m == 0 else P
                        jj = 12 + u * MT + m
                        sp.wait_ge(drained[jj % NB], drain(J_R1 + jj, h, R1_J))
                        sp.sem_inc(sp_gate, 1)
                        sp.dma_start(v_dram[bass.ds(h, 1), tile_columns(m):tile_columns(m) + rows,
                                            u * HC:(u + 1) * HC].rearrange("a t n -> (a t) n"),
                                     rw[0:rows, n % 4, 0:HC]).then_inc(rstored[n % 4], 16)
                        n += 1
                for u in range(2):
                    for t in range(TG):
                        for f in range(2):
                            jj = 12 + 2 * MT + u * 6 + t * 2 + f
                            sp.wait_ge(drained[jj % NB], drain(J_R1 + jj, h, R1_J))
                            sp.sem_inc(sp_gate, 1)
                            sp.dma_start(g_dram[bass.ds(h, 1), :, 2 * u + f, tok(t)].rearrange("a p t -> (a p) t"),
                                         rw[:, n % 4, 0:TS]).then_inc(rstored[n % 4], 16)
                            n += 1
            for b in range(4):
                sp.wait_ge(rstored[b], 16 * (RH * 36 // 4 + 1))

            sp.wait_ge(job_done, J_RO)
            sp.dma_start(eye8[:, :, :], c["eye8"]).then_inc(table_loaded, 16)
            with sp.Fori(0, RH) as h:
                head = bass.ds(h, 1)

                def chunk_load(ch):
                    k = ch % RS
                    cols = slice(NS + ch * P, NS + (ch + 1) * P)
                    sp.wait_ge(y_lo, h * 8 + (ch + 1))
                    sp.sem_inc(sp_gate, 1)
                    sp.dma_start(rqT[:, k, :, :], q_dram[head, :, :, cols].rearrange("a p f t -> (a p) f t")).then_inc(r_loaded[k], 16)
                    sp.dma_start(rkT[:, k, :, :], k_dram[head, :, :, cols].rearrange("a p f t -> (a p) f t")).then_inc(r_loaded[k], 16)
                    sp.dma_start(rv[:, k, :], v_dram[head, cols, :].rearrange("a t n -> (a t) n")).then_inc(r_loaded[k], 16)
                    sp.dma_start(rg[:, k, :, :], g_dram[head, :, :, cols].rearrange("a p f t -> (a p) f t")).then_inc(r_loaded[k], 16)

                def z_load(b):
                    k = b % RS
                    sp.wait_ge(z_stored[k], h * (16 * NS // RS) + 16 * (b // RS + 1))
                    sp.wait_ge(z_read, h * NS + (b + 1))
                    sp.sem_inc(sp_gate, 1)
                    sp.dma_start(zS[:, k, :, :], state_in[b, head, :, :].rearrange("a (f p) n -> (a p) f n", p=P))\
                        .then_inc(z_loaded[k], 16)
                    sp.dma_start(zV[:, k, :], v_dram[head, b:b + 1, :].rearrange("a t n -> (a t n)").partition_broadcast(P))\
                        .then_inc(z_loaded[k], 16)

                chunk_load(0)
                sp.wait_ge(zy_lo, h + 1)
                sp.sem_inc(sp_gate, 1)
                sp.dma_start(dmask[:, :], c["dmask"][head, :, :].rearrange("a p t -> (a p) t")).then_inc(head_loaded, 16)
                sp.dma_start(qdec[:, :], c["qdec"][head, :, :].rearrange("a p t -> (a p) t")).then_inc(head_loaded, 16)
                sp.dma_start(decay[:, :], c["decay"][head, :, :].rearrange("a p t -> (a p) t")).then_inc(head_loaded, 16)
                sp.dma_start(ron[:, :], c["ron"][head, :, :].rearrange("a p t -> (a p) t")).then_inc(head_loaded, 16)
                sp.dma_start(zq[:, 0, :, :], q_dram[head, :, :, 0:NS].rearrange("a p f t -> (a p) f t")).then_inc(zqg_loaded, 16)
                sp.dma_start(zq[:, 1, :, :], k_dram[head, :, :, 0:NS].rearrange("a p f t -> (a p) f t")).then_inc(zqg_loaded, 16)
                sp.dma_start(zg[:, :, :], g_dram[head, :, :, 0:NS].rearrange("a p f t -> (a p) f t")).then_inc(zqg_loaded, 16)
                z_load(0)
                for n in range(1, RS):
                    chunk_load(n)
                    z_load(n)
                for b in range(NS):
                    sp.wait_ge(z_new, h * (2 * NS) + (2 * b + 2))
                    sp.sem_inc(sp_gate, 1)
                    sp.dma_start(ret_s[b, head, :, :].rearrange("a (f p) n -> (a p) f n", p=P), zS[:, b % RS, :, :])\
                        .then_inc(z_stored[b % RS], 16)
                    if b + RS < NS:
                        chunk_load(b + RS)
                        z_load(b + RS)
                sp.wait_ge(st_ready, h * 16 + 16)
                sp.sem_inc(sp_gate, 1)
                sp.dma_start(ret_p[head, :, :].rearrange("a (f p) n -> (a p) f n", p=P), state[:, :, :]).then_inc(state_stored, 16)

            for t in range(TG):
                last = J_FFN1 + FG * FFN_J - KC * (TG - 1 - t)
                for jj in range(last - NB, last):
                    sp.wait_ge(drained[jj % NB], drain(jj))
                sp.dma_start(y[:, :, tok(t)], xT[:, :, tok(t)]).then_inc(y_stored, 16)
            sp.wait_ge(y_stored, 16 * TG)
            sp.wait_ge(copied, 16 * (G + 4 * G))
            sp.wait_ge(state_stored, 16 * (RH + 1))
            for k in range(RS):
                sp.wait_ge(z_stored[k], 16 * (RH * NS // RS + 1))

        @block.scalar
        def _(act):
            def cut_hi(u, jobs, i=0, per_u=0, per_j=0):
                s = u % SLOTS
                act.wait_ge(raw_loaded[s], i * (16 * (per_u // SLOTS)) + 16 * (u // SLOTS + 1))
                if jobs:
                    act.wait_ge(job_done, i * per_j + jobs)
                act.activation(wH[:, s, :], raw[:, s, :], ACT.Copy).then_inc(hi_ready[s], 1)

            def norm(n):
                def squares(t, ks):
                    if ks[0] == 0:
                        norm_x_wait(act, n, t)
                    for k in ks:
                        a = (n * TG + t) * KC + k
                        if a >= 4:
                            act.wait_ge(sq_used, a - 3)
                        act.activation(sq[:, a % 4, :], xT[:, k, tok(t)], ACT.Square).then_inc(sq_ready, 1)

                def root(t):
                    b = 6 + (n * TG + t) % 2
                    if n == 0:
                        act.wait_ge(const_loaded, 96)
                    else:
                        act.wait_ge(table_ready, n)
                    act.wait_ge(sum_done, n * TG + t + 1)
                    act.activation(rt[:, t, :], ps[:, b, 0:TS], ACT.Sqrt, bias=epsb, scale=1.0 / D).then_inc(root_ready, 1)

                if n:
                    act.wait_ge(root_ready, n * TG)
                    act.activation(rt[:, 0, 0:1], small[:, 0:1], ACT.Sqrt).then_inc(table_ready, 1)
                squares(0, range(KC))
                for t in range(TG):
                    if t + 1 < TG:
                        squares(t + 1, range(2))
                    root(t)
                    if t + 1 < TG:
                        squares(t + 1, range(2, KC))
                    if n == 0 and t < 2:
                        cut_hi(t, 0)
                for t in range(1, TG):
                    for k in range(KC):
                        a = (n * TG + t) * KC + k
                        act.wait_ge(normed, a + 1)
                        act.activation(hH[:, k, tok(t)], un[:, a % 4, :], ACT.Copy).then_inc(h_hi, 1)

            norm(0)

            with act.Fori(0, G) as g:
                for u in range(6):
                    if u == 0:
                        act.wait_ge(drained[NB - 1], free(NB - 1, g, QKV_J))
                    cut_hi(U_QKV + u + 2, u * MT, g, 6, QKV_J)
                    for m in range(MT):
                        jj = u * MT + m
                        b = jj % NB
                        act.wait_ge(job_done, g * QKV_J + (jj + 1))
                        if u < 4:
                            k = jj % 2
                            bank = ps[:, b, 0:HC].rearrange("p (h d) -> p h d", h=4)
                            for h in range(4):
                                act.activation(junk[:, k, h * DH:(h + 1) * DH], bank[:, h, :], ACT.Square,
                                               accum_out=ss[:, k, h:h + 1]).then_inc(head_sq, 1)
                            act.wait_ge(head_sq, g * (16 * MT) + 4 * (jj + 1))
                            if jj >= 2:
                                act.wait_ge(rope_done, g * (4 * MT) + (jj - 1))
                            if u < 2:
                                act.activation(rq[:, k, :], ss[:, k, :], ACT.Sqrt, bias=eps64, scale=1.0).then_inc(root_q, 1)
                            else:
                                act.activation(rq[:, k, :], ss[:, k, :], ACT.Sqrt, bias=epsb, scale=1.0 / DH).then_inc(root_q, 1)
                        else:
                            act.wait_ge(stored[b], g * (16 * (QKV_J // NB)) + 16 * (jj // NB + 1))
                            act.activation(ot[:, b, :], ps[:, b, 0:HC], ACT.Copy).then_inc(drained[b], 1)

            def queries(f, i):
                act.wait_ge(q_turned, i * 2 + (f + 1))
                act.activation(aq[0:DH, 0:4, :], ps[0:DH, 0, :].rearrange("p (c t) -> p c t", c=4), ACT.Copy).then_inc(aq_ready, 1)

            def exps(f, i, half):
                act.wait_ge(m_ready, i * 2 + (f + 1))
                for x in range(half * H // 2, (half + 1) * H // 2):
                    w_ = sc[:, f % 2, x, (0 if AT_PREV[f] else P):2 * P]
                    act.activation(w_, w_, ACT.Exp, bias=al[:, f % 2, x, DH:DH + 1],
                                   accum_out=al[:, f % 2, x, DH + 1:DH + 2]).then_inc(p_ready, 1)

            def at_step(a, i):
                if a + 1 < AU:
                    queries(a + 1, i)
                exps(a, i, 1)
                for q in (1, 3):
                    act.wait_ge(p_turned, i * 8 + (4 * a + q + 1))
                    src = ps[:, 7, :].rearrange("p (x h t) -> p x h t", x=2, h=2)
                    if AT_PREV[a]:
                        act.activation(pt[:, 2 * q:2 * q + 2, :, :], src, ACT.Copy).then_inc(pt_ready2, 1)
                    else:
                        act.activation(pt[:, 2 * q:2 * q + 2, 1, :], src[:, :, 1, :], ACT.Copy).then_inc(pt_ready2, 1)
                if a + 1 < AU:
                    exps(a + 1, i, 0)

            act.wait_ge(table_loaded, 32)
            act.wait_ge(aq_zeroed, 1)
            queries(0, 0)
            exps(0, 0, 0)
            for first, n, turns in AT_RUNS:
                if turns == 1:
                    for a in range(first, first + n):
                        at_step(a, 0)
                else:
                    with act.Fori(0, turns) as i:
                        for a in range(first, first + n):
                            at_step(a, i)
            act.wait_ge(b_step, 2)
            act.activation(bP[:, 0:211], bP[:, 0:211], ACT.Exp, bias=bl[:, 0:1], accum_out=bl[:, 1:2]).then_inc(b_exp, 1)
            for m in range(NP // P):
                act.wait_ge(c_max, 3 * m + 3)
                act.activation(cw[:, m % 2, :, :], cw[:, m % 2, :, :], ACT.Exp).then_inc(cw_exp, 1)
                if m:
                    act.wait_ge(co_turned, m)
                    act.activation(oH[:, :, NS + (m - 1) * P:NS + m * P], ps[:, (m - 1) % 2, :].rearrange("p (c t) -> p c t", c=4),
                                   ACT.Copy).then_inc(o_hi, 1)
            act.wait_ge(co_turned, NP // P)
            act.activation(oH[:, :, T - P:T], ps[:, (NP // P - 1) % 2, :].rearrange("p (c t) -> p c t", c=4), ACT.Copy).then_inc(o_hi, 1)
            act.wait_ge(b_out, 1)
            act.activation(oH[:, :, 0:NS], ps[:, 5, 0:4 * NS].rearrange("p (c t) -> p c t", c=4), ACT.Copy).then_inc(b_oh, 1)

            for u in range(3):
                cut_hi(U_WO + u + 2, J_WO + (0, 9, 18)[u])
            norm(1)

            def ffn_turn(i, j0, u0, last=False):
                cut_hi(u0 + 2, j0, i, 3, FFN_J)
                for p in range(6):
                    jg, ju = j0 + 2 * p, j0 + 2 * p + 1
                    act.wait_ge(job_done, i * FFN_J + (jg + 1))
                    act.wait_ge(drained[ju % NB], free(ju, i, FFN_J))
                    act.activation(gs[:, p % 3, :], ps[:, jg % NB, 0:TS], ACT.Silu).then_inc(drained[jg % NB], 1)
                if not last:
                    cut_hi(u0 + 3, j0 + 12, i, 3, FFN_J)
                    cut_hi(u0 + 4, j0 + 12, i, 3, FFN_J)

            with act.Fori(0, FG) as i:
                ffn_turn(i, J_FFN0, U_FFN0)
            norm(2)

            act.wait_ge(const_loaded, 96)
            with act.Fori(0, RH) as h:
                def unit_cut(u):
                    cut_hi(U_R1 + u + 2, J_R1 + (0, 6, 12, 12 + MT, 12 + 2 * MT, 18 + 2 * MT)[u], h, 6, R1_J)
                unit_cut(0)
                unit_cut(1)
                n = 6
                for u in range(2):
                    unit_cut(2 + u)
                    for m in range(MT):
                        jj = 12 + u * MT + m
                        act.wait_ge(job_done, h * R1_J + (J_R1 + jj + 1))
                        act.wait_ge(rstored[n % 4], h * (16 * 9) + 16 * (n // 4 + 1))
                        act.activation(rw[:, n % 4, 0:HC], ps[:, jj % NB, 0:HC], ACT.Copy).then_inc(drained[jj % NB], 1)
                        n += 1
                for u in range(2):
                    unit_cut(4 + u)
                    for q in range(6):
                        jj = 12 + 2 * MT + u * 6 + q
                        act.wait_ge(job_done, h * R1_J + (J_R1 + jj + 1))
                        act.wait_ge(rstored[n % 4], h * (16 * 9) + 16 * (n // 4 + 1))
                        act.activation(rw[:, n % 4, 0:TS], ps[:, jj % NB, 0:TS], ACT.Silu).then_inc(drained[jj % NB], 1)
                        n += 1

            act.wait_ge(table_loaded, 16 * 8)
            with act.Fori(0, RH) as h:
                act.wait_ge(head_loaded, h * 64 + 64)

                def y_cut(ch):
                    act.wait_ge(y_ready, h * 8 + (ch + 1))
                    act.activation(yH[:, :, NS + ch * P:NS + (ch + 1) * P], ry[:, ch % 2, :, :], ACT.Copy).then_inc(y_hi, 1)

                def z_scale(b):
                    act.wait_ge(z_loaded[b % RS], h * (32 * NS // RS) + 32 * (b // RS + 1))
                    act.activation(zS[:, b % RS, :, :], zS[:, b % RS, :, :], ACT.Copy, scale=g1).then_inc(z_scaled, 1)

                z_scale(0)
                for ch in range(8):
                    k = ch % 2
                    act.wait_ge(k_up, h * 8 + (ch + 1))
                    if ch >= 2:
                        act.wait_ge(up_done, h * 8 + (ch - 1))
                    act.activation(kd[:, k, :, :], ps[:, 0, 0:2 * P].rearrange("p (f d) -> p f d", f=2), ACT.Copy,
                                   scale=kdec).then_inc(kd_ready, 1)
                    act.wait_ge(ro_done, h * 8 + (ch + 1))
                    act.activation(rsq[:, :, :], ps[:, 4 + k, :].rearrange("p (e t) -> p e t", e=4), ACT.Square).then_inc(rsq_ready, 1)
                    if ch:
                        y_cut(ch - 1)
                    if ch + 1 < NS:
                        z_scale(ch + 1)
                    act.wait_ge(rsum_done, h * 8 + (ch + 1))
                    act.activation(rr[:, k, :], ps[:, 6, 0:P], ACT.Sqrt, bias=epsb, scale=1.0 / RV).then_inc(rroot_ready, 1)
                y_cut(7)
                act.wait_ge(z_read, h * NS + (NS + RS))
                act.activation(zo[:, :], ps[0:NS, 7, :], ACT.Square, accum_out=zl[:, 0:1]).then_inc(zl_step, 1)
                act.wait_ge(zl_step, h * 2 + 1)
                act.activation(zl[:, 1:2], zl[:, 0:1], ACT.Sqrt, bias=epsb[0:NS], scale=1.0 / RV).then_inc(zl_step, 1)
                act.wait_ge(zr_ready, h + 1)
                act.activation(zo[:, :], ps[0:NS, 7, :], ACT.Copy, scale=zl[:, 2:3]).then_inc(zo_ready, 1)
                act.wait_ge(zy_step, h * 5 + 5)
                act.activation(yH[:, :, 0:NS], zy[:, 1, :, :], ACT.Copy).then_inc(zy_hi, 1)
                for u in range(3):
                    cut_hi(U_RO + u + 2, J_RO + (0, 9, 18)[u], h, 3, RO_J)
            for k in range(RS):
                act.wait_ge(z_stored[k], 16 * (RH * NS // RS + 1))
            act.wait_ge(state_stored, 16 * (RH + 1))
            norm(3)
            with act.Fori(0, FG - 1) as i:
                ffn_turn(i, J_FFN1, U_FFN1)
            ffn_turn(FG - 1, J_FFN1, U_FFN1, last=True)

        @block.tensor
        def _(pe):
            def norm(n):
                for t in range(TG):
                    b = 6 + (n * TG + t) % 2
                    if n * TG + t >= 2:
                        pe.wait_ge(root_ready, n * TG + t - 1)
                    for k in range(KC):
                        pe.wait_ge(sq_ready, (n * TG + t) * KC + k + 1)
                        mm = pe.matmul(ps[:, b, 0:TS], ones[:, :], sq[:, ((n * TG + t) * KC + k) % 4, :],
                                       start=(k == 0), stop=(k == KC - 1))
                        mm.then_inc(sq_used, 1)
                    pe.wait_ge(sq_used, (n * TG + t + 1) * KC)
                    pe.sem_inc(sum_done, 1)

            def bank_free(j, i=0, per=0):
                pe.wait_ge(drained[j % NB], free(j, i, per))
                return j % NB

            def passes(out, lhs, rhs):
                n = len(lhs)
                for k in range(n):
                    for q, (a, b) in enumerate(((0, 0), (0, 1), (1, 0))):
                        mm = pe.matmul(out, lhs[k][a], rhs[k][b], start=(k == 0 and q == 0), stop=(k == n - 1 and q == 2))
                return mm

            def unit_ready(u, i=0, per=0):
                pe.wait_ge(lo_ready[u % SLOTS], hi_ready_at(u, i, per))
                return u % SLOTS

            def tokens_stationary(s, m, b):
                c0 = tile_columns(m)
                wv = [[x_[:, s, :].rearrange("p (k n) -> p k n", k=KC)[:, k, :] for x_ in (wH, wL)] for k in range(KC)]
                return passes(ps[:, b, 0:HC], [[x_[:, k, c0:c0 + P] for x_ in (hH, hL)] for k in range(KC)], wv)

            def tokens_moving(s, f, t, b):
                wv = [[x_[:, s, :].rearrange("p (k n) -> p k n", k=KC)[:, k, f * P:(f + 1) * P] for x_ in (wH, wL)] for k in range(KC)]
                return passes(ps[:, b, 0:TS], wv, [[x_[:, k, tok(t)] for x_ in (hH, hL)] for k in range(KC)])

            def out_projection(u0, j0, oh, ol, i=0, per_u=0, per_j=0, before=None):
                j = j0
                for a, tiles in enumerate(OUT_TILES):
                    s = unit_ready(u0 + a, i, per_u)
                    for t in OUT_ORDER:
                        for dl in range(len(tiles)):
                            if before:
                                before(j - j0)
                            b = bank_free(j, i, per_j)
                            wv = [[x_[:, s, (dl * 4 + k) * P:(dl * 4 + k + 1) * P] for x_ in (wH, wL)] for k in range(4)]
                            passes(ps[:, b, 0:TS], wv, [[x_[:, k, tok(t)] for x_ in (oh, ol)] for k in range(4)])\
                                .then_inc(job_done, 1)
                            j += 1

            pe.wait_ge(ones_set, 1)
            norm(0)
            with pe.Fori(0, G) as g:
                for u in range(6):
                    s = unit_ready(u, g, 6)
                    for m in range(MT):
                        if u == 0:
                            pe.wait_ge(h_lo, ((tile_columns(m) + P - 1) // TS + 1) * KC)
                        b = bank_free(u * MT + m, g, QKV_J)
                        tokens_stationary(s, m, b).then_inc(job_done, 1)

            def turn(f, i):
                k = f % 2
                pe.wait_ge(aqk_loaded[k], i * (32 * AT_PIECES[f]) + 32 * sum(AT_PIECES[k:f + 1:2]))
                if f:
                    pe.wait_ge(ak_ready, i * 2 + f)
                for p in range(4):
                    mm = pe.transpose(ps[:, 1, p * P:(p + 1) * P], qkv[:, k, 1, p * P:(p + 1) * P], ident[:, :])
                mm.then_inc(k_turned, 1)
                if f >= 2:
                    pe.wait_ge(acc_ready, i * 2 + (f - 1))
                if f == 1:
                    pe.wait_ge(aq_ready, 1)
                    pe.wait_ge(aq_ready2, 1)
                for p in range(4):
                    mm = pe.transpose(ps[:, 0, p * P:(p + 1) * P], qkv[:, k, 0, p * P:(p + 1) * P], ident[:, :])
                mm.then_inc(q_turned, 1)

            def scores(f, i):
                pe.wait_ge(aq_ready, i * 2 + (f + 1))
                pe.wait_ge(aq_ready2, i * 2 + (f + 1))
                pe.wait_ge(ak_ready, i * 2 + (f + 1))
                if f:
                    pe.wait_ge(s_masked, i * 8 + 4 * f)
                for x in range(H):
                    for hf in ((0, 1) if AT_PREV[f] else (1,)):
                        mm = pe.matmul(ps[:, 2 + x // 2, (x % 2) * 256 + hf * P:(x % 2) * 256 + (hf + 1) * P],
                                       aq[:, x, :], ak[:, (f + 1 + hf) % 2, x % 4, :], start=True, stop=True)
                    if x in (3, 7):
                        mm.then_inc(s_done, 1)

            def turn_p(a, i, q):
                pe.wait_ge(p_ready, i * 16 + (8 * a + 2 * q + 2))
                if a or q >= 2:
                    pe.wait_ge((pt_ready, pt_ready2)[q % 2], i * 4 + (2 * a + q // 2))
                for x in (2 * q, 2 * q + 1):
                    for hf in ((0, 1) if AT_PREV[a] else (1,)):
                        mm = pe.transpose(ps[:, 6 + q % 2, (x % 2) * 256 + hf * P:(x % 2) * 256 + (hf + 1) * P],
                                          sc[:, a % 2, x, hf * P:(hf + 1) * P], ident[:, :])
                mm.then_inc(p_turned, 1)

            def values(a, i):
                k = a % 2
                halves = (0, 1) if AT_PREV[a] else (1,)
                pe.wait_ge(av_loaded[k], i * (16 * AT_PIECES[a]) + 16 * sum(AT_PIECES[k:a + 1:2]))
                for q in range(4):
                    pe.wait_ge((pt_ready, pt_ready2)[q % 2], i * 4 + (2 * a + q // 2 + 1))
                    for x in (2 * q, 2 * q + 1):
                        hd = 2 * (x % 4) + x // 4
                        for hf in halves:
                            mm = pe.matmul(ps[:, 0, x * DH:(x + 1) * DH], pt[:, x, hf, :],
                                           qkv[:, (k + 1 + hf) % 2, 2, hd * DH:(hd + 1) * DH],
                                           start=(hf == halves[0]), stop=(hf == 1))
                mm.then_inc(pv_done, 1)

            def at_step(a, i):
                if a + 1 < AU:
                    turn(a + 1, i)
                turn_p(a, i, 0)
                turn_p(a, i, 1)
                if a + 1 < AU:
                    scores(a + 1, i)
                turn_p(a, i, 2)
                turn_p(a, i, 3)
                values(a, i)

            for b in range(NB):
                pe.wait_ge(drained[b], drain(J_WO - NB + b))
            turn(0, 0)
            scores(0, 0)
            for first, n, turns in AT_RUNS:
                if turns == 1:
                    for a in range(first, first + n):
                        at_step(a, 0)
                else:
                    with pe.Fori(0, turns) as i:
                        for a in range(first, first + n):
                            at_step(a, i)
            pe.wait_ge(b_scored, NS)
            pe.wait_ge(acc_ready, AU)
            pe.transpose(ps[0:64, 3, 0:P], bS[:, 0, :, :].rearrange("p b h -> p (b h)"), ident[:, :])
            pe.transpose(ps[0:64, 3, P:P + 83], bS[0:83, 1, :, :].rearrange("p b h -> p (b h)"), ident[0:83, 0:83]).then_inc(b_turned, 1)
            pe.wait_ge(b_exp, 1)
            pe.transpose(ps[:, 4, 0:64], bP[:, 0:P], ident[0:64, 0:64])
            pe.transpose(ps[0:83, 4, 64:128], bP[:, P:P + 83], ident[0:64, 0:64]).then_inc(b_pturned, 1)
            for m in range(NP // P):
                pe.wait_ge(co_ready, m + 1)
                if m >= 2:
                    pe.wait_ge(o_lo, m - 1)
                for p in range(4):
                    mm = pe.transpose(ps[:, m % 2, p * P:(p + 1) * P], cp[:, p * P:(p + 1) * P], ident[:, :])
                mm.then_inc(co_turned, 1)
                if m == 0:
                    pe.wait_ge(b_masked, 2)
                pe.wait_ge(bv_loaded[m], 16 * 4)
                pe.matmul(ps[0:64, 2, :], bT[:, 0, m, :], bV[:, m, 0, :], start=(m == 0), stop=False)
                mm = pe.matmul(ps[0:64, 2, :], bT[0:83, 1, m, :], bV[0:83, m, 1, :], start=False, stop=(m == NS - 1))
            mm.then_inc(b_pv, 1)
            pe.wait_ge(b_diag, 1)
            for p in range(4):
                mm = pe.matmul(ps[:, 5, p * NS:(p + 1) * NS], bA[:, p * P:(p + 1) * P], bE[:, :], start=True, stop=True)
            mm.then_inc(b_out, 1)

            pe.wait_ge(b_ol, 1)
            out_projection(U_WO, J_WO, oH, oL)
            norm(1)

            def ffn_turn(i, j0, u0):
                s0, s1 = unit_ready(u0, i, 3), unit_ready(u0 + 1, i, 3)
                j = j0
                for t in range(TG):
                    pe.wait_ge(h_lo, ((2 if j0 == J_FFN0 else 4) * TG - (TG - 1 - t)) * KC)
                    for f in range(2):
                        for s in (s0, s1):
                            tokens_moving(s, f, t, bank_free(j, i, FFN_J)).then_inc(job_done, 1)
                            j += 1
                s = unit_ready(u0 + 2, i, 3)
                for t in range(TG):
                    pe.wait_ge(hid_ready, i * 6 + (6 * FG * (j0 == J_FFN1) + 2 * t + 2))
                    for d in range(KC):
                        b = bank_free(j, i, FFN_J)
                        wv = [[x_[:, s, k * D + d * P:k * D + (d + 1) * P] for x_ in (wH, wL)] for k in range(2)]
                        passes(ps[:, b, 0:TS], wv, [[x_[:, k, tok(t)] for x_ in (hidH, hidL)] for k in range(2)])\
                            .then_inc(job_done, 1)
                        j += 1

            with pe.Fori(0, FG) as i:
                ffn_turn(i, J_FFN0, U_FFN0)
            norm(2)
            with pe.Fori(0, RH) as h:
                jj = 0
                for u in range(6):
                    s = unit_ready(U_R1 + u, h, 6)
                    if u in (2, 3):
                        for m in range(MT):
                            tokens_stationary(s, m, bank_free(J_R1 + jj, h, R1_J)).then_inc(job_done, 1)
                            jj += 1
                    else:
                        for t in range(TG):
                            if u == 0:
                                pe.wait_ge(h_lo, (3 * TG - (TG - 1 - t)) * KC)
                            for f in range(2):
                                tokens_moving(s, f, t, bank_free(J_R1 + jj, h, R1_J)).then_inc(job_done, 1)
                                jj += 1

            pe.wait_ge(table_loaded, 16 * 8)
            with pe.Fori(0, RH) as h:
                for q in range(NB):
                    pe.wait_ge(drained[q], free(J_RO + q, h, RO_J))

                def keys(ch):
                    k = ch % RS
                    pe.wait_ge(r_loaded[k], h * (64 * 8 // RS) + 64 * (ch // RS + 1))
                    pe.wait_ge(kd_ready, h * 8 + (ch + 1))
                    for f in range(2):
                        mm = pe.transpose(ps[:, 0, f * P:(f + 1) * P], rkT[:, k, f, :], ident[:, :])
                    mm.then_inc(k_up, 1)
                    pe.wait_ge(sT_ready, h * 8 + (ch + 1))
                    for f in range(2):
                        mm = pe.matmul(ps[:, 1, 0:P], rkT[:, k, f, :], rqT[:, k, f, :], start=(f == 0), stop=(f == 1))
                    mm.then_inc(rs_done, 1)

                keys(0)
                for ch in range(8):
                    k = ch % 2
                    pe.wait_ge(sT_ready, h * 8 + (ch + 2))
                    pe.wait_ge(qd_ready, h * 8 + (ch + 1))
                    if ch >= 2:
                        pe.wait_ge(y_ready, h * 8 + (ch - 1))
                    if ch:
                        pe.wait_ge(st_ready, h * 16 + 2 * ch)
                    for e in range(4):
                        out = ps[:, 4 + k, e * P:(e + 1) * P]
                        mm = pe.matmul(out, rv[:, ch % RS, e * P:(e + 1) * P], sT[:, k, :], start=True, stop=(ch == 0))
                        if ch:
                            for f in range(2):
                                mm = pe.matmul(out, state[:, f, e * P:(e + 1) * P], qd[:, k, f, :], start=False, stop=(f == 1))
                    mm.then_inc(ro_done, 1)
                    if ch < 7:
                        keys(ch + 1)
                    pe.wait_ge(kd_ready, h * 8 + (ch + 2))
                    if ch:
                        pe.wait_ge(st_ready, h * 16 + 2 * ch)
                    for f in range(2):
                        mm = pe.matmul(ps[:, 2 + f, :], kd[:, k, f, :], rv[:, ch % RS, :], start=True, stop=True)
                    mm.then_inc(up_done, 1)
                    if ch == 0:
                        pe.wait_ge(zm_ready, h + 1)
                        pe.wait_ge(zo_ready, h + 1)
                    pe.wait_ge(z_new, h * (2 * NS) + (2 * ch + 2))
                    for f in range(2):
                        mm = pe.matmul(ps[0:NS, 7, :], zm[:, f, ch, :], zS[:, ch % RS, f, :],
                                       start=(ch == 0 and f == 0), stop=(ch == NS - 1 and f == 1))
                    mm.then_inc(z_read, 1)
                    pe.wait_ge(rsq_added, h * 8 + (ch + 1))
                    if ch:
                        pe.wait_ge(rroot_ready, h * 8 + ch)
                    pe.matmul(ps[:, 6, 0:P], ones[:, :], rsq[:, 0, :], start=True, stop=True).then_inc(rsum_done, 1)

                def before(n):
                    if n == 0:
                        pe.wait_ge(y_lo, h * 8 + (6 + RS))
                    if n == 2:
                        pe.wait_ge(st_ready, h * 16 + 16)
                    if n == 3:
                        pe.wait_ge(y_lo, h * 8 + (8 + RS))
                        pe.wait_ge(zo_ready, h + 2)
                        pe.sem_inc(pe_gate, 1)
                        for e in range(4):
                            mm = pe.transpose(ps[:, 6, e * NS:(e + 1) * NS], zo[:, e * P:(e + 1) * P], ident[0:NS, 0:NS])
                        mm.then_inc(zo_turned, 1)
                    if n == 6:
                        pe.wait_ge(zy_lo, h + 2)

                out_projection(U_RO, J_RO, yH, yL, h, 3, RO_J, before)
            norm(3)
            with pe.Fori(0, FG) as i:
                ffn_turn(i, J_FFN1, U_FFN1)

        @block.vector
        def _(dve):
            tt, ts, stt = dve.tensor_tensor, dve.tensor_scalar, dve.scalar_tensor_tensor

            def cut_lo(u, i=0, per_u=0):
                s = u % SLOTS
                dve.wait_ge(hi_ready[s], hi_ready_at(u, i, per_u))
                tt(wL[:, s, :], raw[:, s, :], wH[:, s, :], ALU.subtract).then_inc(lo_ready[s], 1)

            def norm(n):
                def low(a):
                    k, t = a % KC, a // KC % TG
                    dve.wait_ge(h_hi, a + 1)
                    tt(hL[:, k, tok(t)], un[:, a % 4, :], hH[:, k, tok(t)], ALU.subtract).then_inc(h_lo, 1)
                for t in range(TG):
                    dve.wait_ge(root_ready, n * TG + t + 1)
                    dve.reciprocal(rt[:, t, :], rt[:, t, :]).then_inc(recip_ready, 1)
                    dve.wait_ge(recip_ready, n * TG + t + 1)
                    for k in range(KC):
                        a = (n * TG + t) * KC + k
                        if a >= 4:
                            dve.wait_ge(h_lo, a - 3)
                        stt(out=un[:, a % 4, :], in0=xT[:, k, tok(t)], scalar=gains[:, n, k:k + 1], in1=rt[:, t, :],
                            op0=ALU.mult, op1=ALU.mult).then_inc(normed, 1)
                        if t == 0:
                            dve.wait_ge(normed, a + 1)
                            dve.tensor_copy(hH[:, k, tok(t)], un[:, a % 4, :]).then_inc(h_hi, 1)
                        if k >= 2:
                            low(a - 2)
                    low(a - 1)
                    low(a)
                    if n == 0 and t < 2:
                        cut_lo(t)

            dve.memset(ones[:, :], 1.0).then_inc(ones_set, 1)
            for b in range(NB):
                dve.sem_inc(drained[b], 1)
                dve.sem_inc(stored[b], 16)
            for b in range(4):
                dve.sem_inc(rstored[b], 16)
            for b in range(RS):
                dve.sem_inc(z_stored[b], 16)
            for s_, n_ in ((acc_stored[0], 16), (acc_stored[1], 16), (y_lo, RS), (zy_lo, 1), (z_read, RS), (kd_ready, 1), (sT_ready, 1), (rrope_done, 1), (zo_ready, 1), (state_stored, 16)):
                dve.sem_inc(s_, n_)
            dve.wait_ge(const_loaded, 96)
            norm(0)

            with dve.Fori(0, G) as g:
                for u in range(6):
                    cut_lo(u + 2, g, 6)
                    if u >= 4:
                        continue
                    for m in range(MT):
                        jj = u * MT + m
                        b, k = jj % NB, jj % 2
                        steps = g * (7 * 4 * MT) + 7 * jj
                        bank = ps[:, b, 0:HC].rearrange("p (h d) -> p h d", h=4)
                        dve.wait_ge(root_q, g * (4 * MT) + (jj + 1))
                        dve.reciprocal(ri[:, k, :], rq[:, k, :]).then_inc(rope_step, 1)
                        dve.wait_ge(rope_step, steps + 1)
                        for h, done in enumerate((rope_step, rope_step, rope_step, drained[b])):
                            stt(out=qn[:, h, :], in0=bank[:, h, :], scalar=ri[:, k, h:h + 1],
                                in1=qkg[:, bass.ds(g * 2 + u // 2, 1), :].rearrange("p a d -> p (a d)"),
                                op0=ALU.mult, op1=ALU.mult).then_inc(done, 1)
                        dve.wait_ge(rope_step, steps + 4)
                        dve.wait_ge(drained[b], drain(jj, g, QKV_J))
                        tt(qc[:, :, :], qn[:, :, :], ropeC[:, m:m + 1, :].broadcast_to([P, 4, DH]), ALU.mult).then_inc(rope_step, 1)
                        for a in range(2):
                            tt(qs[:, :, a * 32:(a + 1) * 32], qn[:, :, (1 - a) * 32:(2 - a) * 32],
                               ropeS[:, m:m + 1, a * 32:(a + 1) * 32].broadcast_to([P, 4, 32]), ALU.mult).then_inc(rope_step, 1)
                        dve.wait_ge(rope_step, steps + 7)
                        dve.wait_ge(stored[b], g * (16 * (QKV_J // NB)) + 16 * (jj // NB + 1))
                        tt(ot[:, b, :].rearrange("p (h d) -> p h d", h=4), qc[:, :, :], qs[:, :, :], ALU.add).then_inc(rope_done, 1)

            def keys(f, i):
                dve.wait_ge(k_turned, i * 2 + (f + 1))
                dve.tensor_copy(ak[:, f % 2, :, :], ps[:, 1, :].rearrange("p (c t) -> p c t", c=4)).then_inc(ak_ready, 1)
                dve.wait_ge(q_turned, i * 2 + (f + 1))
                dve.tensor_copy(aq[DH:P, 4:8, :], ps[DH:P, 0, :].rearrange("p (c t) -> p c t", c=4)).then_inc(aq_ready2, 1)

            def masked(f, i):
                w0 = 0 if AT_PREV[f] else P
                mask = maskD[:, :] if f >= 16 else maskP[:, w0:2 * P]
                for q in range(4):
                    if q % 2 == 0:
                        dve.wait_ge(s_done, i * 4 + (2 * f + q // 2 + 1))
                    tt(sc[:, f % 2, 2 * q:2 * q + 2, w0:2 * P], ps[:, 2 + q, :].rearrange("p (x w) -> p x w", x=2)[:, :, w0:2 * P],
                       mask.rearrange("p (x w) -> p x w", x=1).broadcast_to([P, 2, 2 * P - w0]), ALU.add).then_inc(s_masked, 1)

            def maxima(f, i):
                k = f % 2
                dve.wait_ge(acc_stored[k], i * (16 * AT_PIECES[f]) + (16 + 16 * sum(AT_PIECES[k:f:2])))
                dve.wait_ge(s_masked, i * 8 + (4 * f + 4))
                dve.tensor_reduce(al[:, k, :, DH:DH + 1], sc[:, k, :, (0 if AT_PREV[f] else P):2 * P], AX.X, ALU.max, negate=True)\
                    .then_inc(m_ready, 1)

            def turned_p(a, i, q):
                dve.wait_ge(p_turned, i * 8 + (4 * a + q + 1))
                src = ps[:, 6, :].rearrange("p (x h t) -> p x h t", x=2, h=2)
                if AT_PREV[a]:
                    dve.tensor_copy(pt[:, 2 * q:2 * q + 2, :, :], src).then_inc(pt_ready, 1)
                else:
                    dve.tensor_copy(pt[:, 2 * q:2 * q + 2, 1, :], src[:, :, 1, :]).then_inc(pt_ready, 1)

            def sample_scores(b, i):
                k = b % 2
                dve.wait_ge(b_loaded[k], i * (16 * 8) + 16 * 8 * (b // 2 + 1))
                for tl, n in ((0, P), (1, 83)):
                    tt(bK[0:n, k, tl, :], bK[0:n, k, tl, :], bQ[0:n, k, tl, :], ALU.mult).then_inc(b_prod, 1)
                for tl, n, done in ((0, P, b_red), (1, 83, b_scored)):
                    dve.wait_ge(b_prod, i * 4 + (2 * b + tl + 1))
                    dve.tensor_reduce(bS[0:n, tl, bass.ds(i * 2 + b, 1), :].rearrange("p a h -> p (a h)"),
                                      bK[0:n, k, tl, :].rearrange("p (h d) -> p h d", h=H), AX.X, ALU.add).then_inc(done, 1)

            def at_step(a, i):
                if a + 1 < AU:
                    keys(a + 1, i)
                turned_p(a, i, 0)
                if a < NS:
                    sample_scores(a, i)
                if a + 1 < AU:
                    masked(a + 1, i)
                turned_p(a, i, 2)
                if a + 1 < AU:
                    maxima(a + 1, i)
                dve.wait_ge(pv_done, i * 2 + (a + 1))
                dve.tensor_copy(al[:, a % 2, :, 0:DH], ps[:, 0, :].rearrange("p (x d) -> p x d", x=H)).then_inc(acc_ready, 1)

            dve.wait_ge(job_done, J_WO)
            dve.memset(aq[:, :, :], 0.0).then_inc(aq_zeroed, 1)
            dve.wait_ge(table_loaded, 32)
            dve.wait_ge(aq_zeroed, 1)
            keys(0, 0)
            masked(0, 0)
            maxima(0, 0)
            for first, n, turns in AT_RUNS:
                if turns == 1:
                    for a in range(first, first + n):
                        at_step(a, 0)
                else:
                    with dve.Fori(0, turns) as i:
                        for a in range(first, first + n):
                            at_step(a, i)

            def low_o(m):
                dve.wait_ge(o_hi, m + 1)
                cols = slice(NS + m * P, NS + (m + 1) * P)
                tt(oL[:, :, cols], ps[:, m % 2, :].rearrange("p (c t) -> p c t", c=4), oH[:, :, cols], ALU.subtract).then_inc(o_lo, 1)

            def weights(m):
                c_, k = m % CS, m % 2
                dve.wait_ge(cb_loaded[c_], 16 * (m // CS + 1))
                tt(cm[:, 0, :], cb[:, c_, 0, :, DH], cb[:, c_, 1, :, DH], ALU.min).then_inc(c_max, 1)
                dve.wait_ge(c_max, 3 * m + 1)
                tt(cm[:, 1, :], cm[:, 0, :], cb[:, c_, 2, :, DH], ALU.min).then_inc(c_max, 1)
                dve.wait_ge(c_max, 3 * m + 2)
                tt(cw[:, k, :, :], cm[:, 1:2, :].broadcast_to([P, G, H]), cb[:, c_, :, :, DH], ALU.subtract).then_inc(c_max, 1)

            def normed_weights(m):
                c_, k, n = m % CS, m % 2, 4 * m
                dve.wait_ge(cw_exp, m + 1)
                tt(cb[:, c_, :, :, DH], cw[:, k, :, :], cb[:, c_, :, :, DH + 1], ALU.mult).then_inc(c_step, 1)
                dve.wait_ge(c_step, n + 1)
                dve.tensor_reduce(cm[:, 2, :], cb[:, c_, :, :, DH].rearrange("p g h -> p h g"), AX.X, ALU.add).then_inc(c_step, 1)
                dve.wait_ge(c_step, n + 2)
                dve.reciprocal(cm[:, 3, :], cm[:, 2, :]).then_inc(c_step, 1)
                dve.wait_ge(c_step, n + 3)
                tt(cw[:, k, :, :], cw[:, k, :, :], cm[:, 3:4, :].broadcast_to([P, G, H]), ALU.mult).then_inc(c_step, 1)

            dve.wait_ge(b_red, NS)
            dve.wait_ge(b_turned, 1)
            dve.tensor_copy(bP[:, 0:211], ps[0:64, 3, 0:211]).then_inc(b_step, 1)
            dve.wait_ge(b_step, 1)
            dve.tensor_reduce(bl[:, 0:1], bP[:, 0:211], AX.X, ALU.max, negate=True).then_inc(b_step, 1)
            dve.wait_ge(b_exp, 1)
            dve.reciprocal(bl[:, 2:3], bl[:, 1:2]).then_inc(b_step, 1)
            dve.wait_ge(b_pturned, 1)
            dve.wait_ge(table_loaded, 16 * 5)
            for tl, n in ((0, P), (1, 83)):
                tt(bT[0:n, tl, :, :], ps[0:n, 4, tl * 64:(tl + 1) * 64].rearrange("p (a c) -> p a c", a=1).broadcast_to([n, NS, 64]),
                   bM[0:n, :, :], ALU.mult).then_inc(b_masked, 1)

            weights(0)
            normed_weights(0)
            for m in range(NP // P):
                c_, k = m % CS, m % 2
                if m + 1 < NP // P:
                    weights(m + 1)
                dve.wait_ge(c_step, 4 * m + 4)
                for g in range(G):
                    tt(cb[:, c_, g, :, 0:DH], cb[:, c_, g, :, 0:DH],
                       cw[:, k, g, :].rearrange("p (h a) -> p h a", a=1).broadcast_to([P, H, DH]), ALU.mult)\
                        .then_inc(cm_done, 1)
                if m + 1 < NP // P:
                    normed_weights(m + 1)
                dve.wait_ge(cm_done, 4 * m + 3)
                tt(cb[:, c_, 0, :, 0:DH], cb[:, c_, 0, :, 0:DH], cb[:, c_, 1, :, 0:DH], ALU.add).then_inc(cm_done, 1)
                dve.wait_ge(cm_done, 4 * m + 4)
                if m:
                    low_o(m - 1)
                tt(cp[:, :].rearrange("p (hp par d) -> p par hp d", hp=4, par=2),
                   cb[:, c_, 0, :, 0:DH].rearrange("p (par hp) d -> p par hp d", par=2),
                   cb[:, c_, 2, :, 0:DH].rearrange("p (par hp) d -> p par hp d", par=2), ALU.add).then_inc(co_ready, 1)
            low_o(NP // P - 1)
            dve.wait_ge(b_pv, 1)
            dve.wait_ge(b_step, 3)
            stt(out=bA[:, :], in0=ps[0:64, 2, :], scalar=bl[:, 2:3], in1=bD[:, :], op0=ALU.mult, op1=ALU.mult).then_inc(b_diag, 1)
            dve.wait_ge(b_oh, 1)
            tt(oL[:, :, 0:NS], ps[:, 5, 0:4 * NS].rearrange("p (c t) -> p c t", c=4), oH[:, :, 0:NS], ALU.subtract).then_inc(b_ol, 1)

            def out_drain(u0, j0, i=0, per_u=0, per_j=0):
                j = j0
                for a, tiles in enumerate(OUT_TILES):
                    cut_lo(u0 + a + 2, i, per_u)
                    for t in OUT_ORDER:
                        for d in tiles:
                            dve.wait_ge(job_done, i * per_j + (j + 1))
                            tt(xT[:, d, tok(t)], ps[:, j % NB, 0:TS], xT[:, d, tok(t)], ALU.add).then_inc(drained[j % NB], 1)
                            j += 1

            out_drain(U_WO, J_WO)
            norm(1)

            def ffn_turn(i, j0, u0, last=False):
                cut_lo(u0 + 2, i, 3)
                h0 = 6 * FG * (j0 == J_FFN1)
                for p in range(6):
                    jg, ju = j0 + 2 * p, j0 + 2 * p + 1
                    t, f = p // 2, p % 2
                    dve.wait_ge(drained[jg % NB], drain(jg, i, FFN_J))
                    dve.wait_ge(job_done, i * FFN_J + (ju + 1))
                    if p >= 2:
                        dve.wait_ge(hid_ready, i * 6 + (h0 + p - 1))
                    tt(us[:, p % 2, :], ps[:, ju % NB, 0:TS], gs[:, p % 3, :], ALU.mult).then_inc(drained[ju % NB], 1)
                    dve.wait_ge(drained[ju % NB], drain(ju, i, FFN_J))
                    dve.tensor_copy(hidH[:, f, tok(t)], us[:, p % 2, :]).then_inc(hid_hi, 1)
                    dve.wait_ge(hid_hi, i * 6 + (h0 + p + 1))
                    tt(hidL[:, f, tok(t)], us[:, p % 2, :], hidH[:, f, tok(t)], ALU.subtract).then_inc(hid_ready, 1)
                j = j0 + 12
                for t in range(TG):
                    for d in range(KC):
                        if t < 2 and d == 3 and not last:
                            cut_lo(u0 + 3 + t, i, 3)
                        dve.wait_ge(job_done, i * FFN_J + (j + 1))
                        tt(xT[:, d, tok(t)], ps[:, j % NB, 0:TS], xT[:, d, tok(t)], ALU.add).then_inc(drained[j % NB], 1)
                        j += 1

            with dve.Fori(0, FG) as i:
                ffn_turn(i, J_FFN0, U_FFN0)
            norm(2)

            dve.wait_ge(table_loaded, 16 * 7)
            dve.wait_ge(h_lo, 3 * TG * KC)
            with dve.Fori(0, RH) as h:
                n = 0
                for u, scale in ((0, 1.0), (1, RQ ** -0.5)):
                    cut_lo(U_R1 + u + 2, h, 6)
                    for t in range(TG):
                        j1 = J_R1 + u * 6 + 2 * t
                        b1, b2 = j1 % NB, (j1 + 1) % NB
                        x1, x2 = ps[:, b1, 0:TS], ps[:, b2, 0:TS]
                        steps = h * (6 * 3) + 3 * n
                        dve.wait_ge(job_done, h * R1_J + (j1 + 2))
                        dve.wait_ge(rrope_done, h * 6 + (n + 1))
                        stt(out=un[:, 0, :], in0=x1, scalar=scale, in1=cosR[:, tok(t)], op0=ALU.mult, op1=ALU.mult).then_inc(rrope_step, 1)
                        stt(out=un[:, 1, :], in0=x2, scalar=scale, in1=sinR[:, tok(t)], op0=ALU.mult, op1=ALU.mult).then_inc(rrope_step, 1)
                        stt(out=un[:, 2, :], in0=x2, scalar=scale, in1=cosR[:, tok(t)], op0=ALU.mult, op1=ALU.mult).then_inc(drained[b2], 1)
                        stt(out=un[:, 3, :], in0=x1, scalar=scale, in1=sinR[:, tok(t)], op0=ALU.mult, op1=ALU.mult).then_inc(drained[b1], 1)
                        dve.wait_ge(rstored[n % 4], h * (16 * 9) + 16 * (n // 4 + 1))
                        dve.wait_ge(rrope_step, steps + 2)
                        tt(rw[:, n % 4, 0:TS], un[:, 0, :], un[:, 1, :], ALU.subtract).then_inc(rrope_step, 1)
                        dve.wait_ge(drained[b2], drain(j1 + 1, h, R1_J))
                        dve.wait_ge(drained[b1], drain(j1, h, R1_J))
                        dve.wait_ge(rrope_step, steps + 3)
                        tt(rw[:, n % 4, TS:2 * TS], un[:, 2, :], un[:, 3, :], ALU.add).then_inc(rrope_done, 1)
                        n += 1
                for u in range(2, 6):
                    cut_lo(U_R1 + u + 2, h, 6)

            dve.wait_ge(table_loaded, 16 * 8)
            with dve.Fori(0, RH) as h:
                dve.wait_ge(head_loaded, h * 64 + 64)

                def y_rest(ch):
                    k = ch % 2
                    n = h * (8 * 5) + 5 * ch
                    dve.wait_ge(rroot_ready, h * 8 + (ch + 1))
                    dve.reciprocal(rr[:, k, :], rr[:, k, :]).then_inc(rstep, 1)
                    dve.wait_ge(rstep, n + 1)
                    for e in range(4):
                        stt(out=ry[:, k, e, :], in0=ps[:, 4 + k, e * P:(e + 1) * P], scalar=ron[:, e:e + 1],
                            in1=rr[:, k, :], op0=ALU.mult, op1=ALU.mult).then_inc(rstep, 1)
                    dve.wait_ge(rstep, n + 5)
                    tt(ry[:, k, :, :], ry[:, k, :, :], rg[:, ch % RS, :, :], ALU.mult).then_inc(y_ready, 1)

                def y_low(ch):
                    dve.wait_ge(y_hi, h * 8 + (ch + 1))
                    cols = slice(NS + ch * P, NS + (ch + 1) * P)
                    tt(yL[:, :, cols], ry[:, ch % 2, :, :], yH[:, :, cols], ALU.subtract).then_inc(y_lo, 1)

                dve.wait_ge(zqg_loaded, h * 48 + 48)
                for f, done in enumerate((zm_half, zm_ready)):
                    tt(zm[:, f, :, :], zq[:, 0, f, :].rearrange("p (a b) -> p b a", a=1).broadcast_to([P, NS, NS]), eye8[:, :, :],
                       ALU.mult).then_inc(done, 1)
                for ch in range(8):
                    k = ch % 2
                    dve.wait_ge(r_loaded[ch % RS], h * (64 * 8 // RS) + 64 * (ch // RS + 1))
                    tt(qd[:, k, :, :], rqT[:, ch % RS, :, :], qdec[:, :].rearrange("p (a t) -> p a t", a=1).broadcast_to([P, 2, P]), ALU.mult).then_inc(qd_ready, 1)
                    dve.wait_ge(rs_done, h * 8 + (ch + 1))
                    tt(sT[:, k, :], ps[:, 1, 0:P], dmask[:, :], ALU.mult).then_inc(sT_ready, 1)
                    if ch >= 2:
                        y_low(ch - 2)
                    dve.wait_ge(z_scaled, h * NS + (ch + 1))
                    for f in range(2):
                        stt(out=zS[:, ch % RS, f, :], in0=zV[:, ch % RS, :], scalar=zq[:, 1, f, ch:ch + 1], in1=zS[:, ch % RS, f, :],
                            op0=ALU.mult, op1=ALU.add).then_inc(z_new, 1)
                    if ch:
                        y_rest(ch - 1)
                    dve.wait_ge(up_done, h * 8 + (ch + 1))
                    if ch == 0:
                        dve.wait_ge(state_stored, h * 16 + 16)
                    for f in range(2):
                        if ch == 0:
                            dve.tensor_copy(state[:, f, :], ps[:, 2 + f, :]).then_inc(st_ready, 1)
                        else:
                            if f == 0:
                                dve.wait_ge(st_ready, h * 16 + 2 * ch)
                            stt(out=state[:, f, :], in0=state[:, f, :], scalar=gC, in1=ps[:, 2 + f, :],
                                op0=ALU.mult, op1=ALU.add).then_inc(st_ready, 1)
                y_low(6)
                y_rest(7)
                y_low(7)
                dve.wait_ge(zl_step, h * 2 + 2)
                dve.reciprocal(zl[:, 2:3], zl[:, 1:2]).then_inc(zr_ready, 1)
                dve.wait_ge(zo_turned, h + 1)
                for e in range(4):
                    ts(zy[:, 0, e, :], ps[:, 6, e * NS:(e + 1) * NS], ron[:, e:e + 1], None, ALU.mult).then_inc(zy_step, 1)
                dve.wait_ge(zy_step, h * 5 + 4)
                tt(zy[:, 1, :, :], zy[:, 0, :, :], zg[:, :, :], ALU.mult).then_inc(zy_step, 1)
                dve.wait_ge(zy_hi, h + 1)
                tt(yL[:, :, 0:NS], zy[:, 1, :, :], yH[:, :, 0:NS], ALU.subtract).then_inc(zy_lo, 1)
                out_drain(U_RO, J_RO, h, 3, RO_J)
            norm(3)
            with dve.Fori(0, FG - 1) as i:
                ffn_turn(i, J_FFN1, U_FFN1)
            ffn_turn(FG - 1, J_FFN1, U_FFN1, last=True)
    ctx.close()


def weight_units(a_w_qkv, a_w_o, r_w_in, r_w_o, f_w_gate, f_w_up, f_w_down):
    import numpy as np
    out = np.zeros((UNITS, P, UW), np.float32)
    n = 0

    def put(block):
        nonlocal n
        block = block.reshape(P, -1)
        out[n, :, :block.shape[1]] = block
        n += 1

    def columns(w, c0):
        put(w[:, c0:c0 + HC].reshape(KC, P, HC).transpose(1, 0, 2))

    def out_rows(w):
        blocks = w.reshape(4, P, KC, P).transpose(1, 2, 0, 3)
        for tiles in OUT_TILES:
            put(blocks[:, tiles[0]:tiles[-1] + 1])

    def ffn(layer):
        for i in range(FG):
            columns(f_w_gate[layer], i * HC)
            columns(f_w_up[layer], i * HC)
            put(f_w_down[layer][i * HC:(i + 1) * HC].reshape(2, P, D).transpose(1, 0, 2))

    for c0 in range(0, 3 * G * AW, HC):
        columns(a_w_qkv[0], c0)
    out_rows(a_w_o[0])
    ffn(0)
    for h in range(RH):
        for c0 in (h * RQ, D + h * RQ, 2 * D + h * RV, 2 * D + h * RV + HC, 4 * D + h * RV, 4 * D + h * RV + HC):
            columns(r_w_in[0], c0)
    for h in range(RH):
        out_rows(r_w_o[0][h * RV:(h + 1) * RV])
    ffn(1)
    assert n == UNITS
    return out


def tables():
    import numpy as np
    f = np.float32

    def angles(pos, half):
        inv = (10000.0 ** (-np.arange(half, dtype=f) / f(half)).astype(np.float64)).astype(f)
        ang = (pos.astype(f)[:, None] * inv[None, :]).astype(f).astype(np.float64)
        return np.cos(ang).astype(f), np.sin(ang).astype(f)

    pos = np.concatenate([np.full(NS, 256), np.arange(NP)])
    out = {}
    cos, sin = angles(pos, DH // 2)
    cols = np.stack([tile_columns(m) + np.arange(P) for m in range(MT)], 1)
    out["ropeC"] = np.concatenate([cos[cols], cos[cols]], -1)
    out["ropeS"] = np.concatenate([-sin[cols], sin[cols]], -1)
    cos, sin = angles(pos, RQ // 2)
    out["cosR"], out["sinR"] = cos.T, sin.T
    i = np.arange(P)
    ok_self = i[None, :] <= i[:, None]
    out["maskP"] = np.where(np.concatenate([i[None, :] >= i[:, None], ok_self], 1), 0.0, -1e38)
    out["maskD"] = np.where(ok_self & (i[None, :] // 64 == i[:, None] // 64), 0.0, -1e38)
    out["ident"] = np.eye(P)
    lg = np.log1p(-np.exp2(-5.0 - np.arange(RH))).astype(f).astype(np.float64)
    out["small"] = np.broadcast_to([EPS, 64 * EPS], (P, 2))
    decay = np.zeros((RH, P, 4))
    decay[:, :, 0] = np.exp(lg)[:, None]
    decay[:, :, 1] = np.exp(P * lg)[:, None]
    decay[:, :, 2] = np.exp((P - 1.0 - i)[None, :] * lg[:, None])
    out["decay"] = decay
    rel = (i[None, None, :] - i[None, :, None]).astype(np.float64)
    out["dmask"] = np.where(rel >= 0, np.exp(np.maximum(rel, 0) * lg[:, None, None]), 0.0)
    out["qdec"] = np.broadcast_to(np.exp((i + 1.0)[None, :] * lg[:, None])[:, None], (RH, P, P))
    out["eye8"] = np.broadcast_to(np.eye(NS)[None], (P, NS, NS))
    b, h = np.arange(NS * H) // H, np.arange(NS * H) % H
    out["blockmask"] = np.broadcast_to((b[None, :] == np.arange(NS)[:, None])[None], (P, NS, NS * H))
    out["diagmask"] = h[:, None] == np.arange(AW)[None, :] // DH
    out["select"] = b[:, None] == np.arange(NS)[None, :]
    return {k: np.ascontiguousarray(v, dtype=f) for k, v in out.items()}


def kernel(x_prompt, x_sample, cache_kv_g0, cache_kv_g1, cache_kv_g2, state_retention,
           mix_norm, ffn_norm, a_w_qkv, a_q_norm, a_k_norm, a_w_o,
           r_w_in, r_out_norm, r_w_o, f_w_gate, f_w_up, f_w_down):
    import numpy as np
    import concourse.bacc as bacc
    from concourse.bass_utils import run_bass_kernel_spmd

    nc = bacc.Bacc("TRN2", target_bir_lowering=False, num_devices=1)
    arrays = {}

    def given(name, a):
        arrays["in_" + name] = np.ascontiguousarray(a)
        return nc.dram_tensor("in_" + name, a.shape, F32, kind="ExternalInput").ap()

    def result(name, shape):
        return nc.dram_tensor(name, shape, F32, kind="ExternalOutput").ap()

    def kept(name, shape):
        return nc.dram_tensor(name, shape, F32).ap()

    def chunked(a):
        return np.asarray(a).reshape(-1, KC, P).transpose(2, 0, 1)

    x = np.concatenate([np.asarray(x_sample)[:, 0], np.asarray(x_prompt)[0]], 0)
    x_in = given("x", x.T.reshape(KC, P, T).transpose(1, 0, 2))
    w = given("w", weight_units(*(np.asarray(a) for a in (a_w_qkv, a_w_o, r_w_in, r_w_o, f_w_gate, f_w_up, f_w_down))))
    c = {name: given(name, a) for name, a in tables().items()}
    norms = np.stack([np.asarray(a)[i] for i in range(2) for a in (mix_norm, ffn_norm)])
    c["gains"] = given("gains", chunked(norms))
    qk = np.stack([np.asarray(a_q_norm)[0], np.asarray(a_k_norm)[0]], 1).reshape(2 * G, DH)
    c["qkg"] = given("qkg", np.broadcast_to(qk[None], (P, 2 * G, DH)))
    c["ron"] = given("ron", np.asarray(r_out_norm)[0].reshape(RH, 4, P).transpose(0, 2, 1))
    caches = [np.asarray(a)[0] for a in (cache_kv_g0, cache_kv_g1, cache_kv_g2)]
    kv_cache = [given(f"cache{g}", a.reshape(NS, -1, 2 * AW)) for g, a in enumerate(caches)]
    state_in = given("state_in", np.asarray(state_retention)[0])
    y = result("y", (P, KC, T))
    keep = (128, 512, 1024)
    kv_p = [result(f"kv_p{g}", (keep[g], 2, AW)) for g in range(G)]
    kv_s = [result(f"kv_s{g}", (NS, a.shape[1], 2 * AW)) for g, a in enumerate(caches)]
    ret_p = result("ret_p", (RH, RQ, RV))
    ret_s = result("ret_s", (NS, RH, RQ, RV))
    scratch = (kept("qkv_rows", (G, 3, T, AW)), kept("acc_rows", (G, NP, H * (DH + 2))), kept("q_cols", (RH, P, 2, T)),
               kept("k_cols", (RH, P, 2, T)), kept("v_rows", (RH, T, RV)), kept("g_cols", (RH, P, 4, T)))
    trunk(nc, x_in, w, c, kv_cache, state_in, y, kv_p, kv_s, ret_p, ret_s, scratch)
    r = run_bass_kernel_spmd(nc, [arrays], core_ids=[0]).results[0]
    rows = r["y"].transpose(1, 0, 2).reshape(D, T).T
    out = [rows[NS:][None], rows[:NS][:, None]]
    for g in range(G):
        out.append(r[f"kv_p{g}"].reshape(1, 1, keep[g], 2, H, DH))
        out.append(r[f"kv_s{g}"].reshape(1, NS, -1, 2, H, DH))
    out.append(r["ret_p"][None, None])
    out.append(r["ret_s"][None])
    return tuple(out)
```
